# Optimizing a Trainium2 kernel written in Bass

```python
import math
import jax, jax.numpy as jnp
from jax import lax
import numpy as np

D_MODEL = 1024
BATCH = 1
SEQ = 1024
DEPTH = 1

CHUNK = 64
N_META = 16
QBLOCK = 128
ROPE_THETA = 10000.0
EPS = 1e-6

DA_DIM = 64
DA_VDIM = 2 * DA_DIM
DA_WIDTH = D_MODEL // 2
DA_HEADS = DA_WIDTH // DA_VDIM
GDN_DK = 64
GDN_DV = 64
GDN_WIDTH = D_MODEL - DA_WIDTH
GDN_HEADS = GDN_WIDTH // GDN_DV
CONV_K = 4
MIX_WIDTH = DA_WIDTH + GDN_WIDTH

COL_QA = 2 * DA_HEADS * DA_DIM
COL_KA = 2 * DA_HEADS * DA_DIM
COL_VA = DA_WIDTH
COL_QKVB = 2 * GDN_HEADS * GDN_DK + GDN_WIDTH
COL_ZB = GDN_WIDTH
COL_AB = GDN_HEADS
COL_BB = GDN_HEADS
PROJ = COL_QA + COL_KA + COL_VA + COL_QKVB + COL_ZB + COL_AB + COL_BB
SPLITS = list(np.cumsum([COL_QA, COL_KA, COL_VA, COL_QKVB, COL_ZB, COL_AB])[:].tolist())

N_GROUPS = 4
EXPERTS_PER_GROUP = 8
N_EXPERTS = N_GROUPS * EXPERTS_PER_GROUP
TOP_K = 2
D_EXPERT = D_MODEL // 4

kernel_name = "hymba_diffattn_gdn_hmoe_block"

def rmsnorm(x, gain):
    xf = x.astype(jnp.float32)
    y = xf * lax.rsqrt(jnp.mean(xf * xf, axis=-1, keepdims=True) + EPS)
    return (y * gain.astype(jnp.float32)).astype(x.dtype)

def l2norm(x):
    xf = x.astype(jnp.float32)
    return xf * lax.rsqrt(jnp.sum(xf * xf, axis=-1, keepdims=True) + EPS)

def chunk_ids(n):
    p = jnp.arange(n, dtype=jnp.int32)
    return jnp.where(p < N_META, 0, 1 + (p - N_META) // CHUNK)

def rope(x, cos, sin):
    x1, x2 = jnp.split(x.astype(jnp.float32), 2, axis=-1)
    c, s = cos[None, :, None, :], sin[None, :, None, :]
    return jnp.concatenate([x1 * c - x2 * s, x2 * c + x1 * s], axis=-1).astype(x.dtype)

def masked_softmax(s, visible):
    return jax.nn.softmax(jnp.where(visible, s, -jnp.inf), axis=-1)

def diff_attention(q, k, v, lam):
    B, L = q.shape[0], q.shape[1]
    n_blocks = -(-L // QBLOCK)
    Lp = n_blocks * QBLOCK

    def pad(t):
        return jnp.pad(t, ((0, 0), (0, Lp - L)) + ((0, 0),) * (t.ndim - 2))

    q, k, v = pad(q), pad(k), pad(v)
    scale = DA_DIM ** -0.5
    q1 = (q[:, :, :, 0] * scale).transpose(0, 2, 1, 3)
    q2 = (q[:, :, :, 1] * scale).transpose(0, 2, 1, 3)
    k1 = k[:, :, :, 0].transpose(0, 2, 1, 3)
    k2 = k[:, :, :, 1].transpose(0, 2, 1, 3)
    vh = v.transpose(0, 2, 1, 3)
    cid = chunk_ids(Lp)

    def block(i):
        start = i * QBLOCK
        q1b = lax.dynamic_slice_in_dim(q1, start, QBLOCK, axis=2)
        q2b = lax.dynamic_slice_in_dim(q2, start, QBLOCK, axis=2)
        qc = lax.dynamic_slice_in_dim(cid, start, QBLOCK)
        visible = cid[None, :] <= qc[:, None]
        p1 = masked_softmax(jnp.einsum('bhqd,bhkd->bhqk', q1b, k1).astype(jnp.float32), visible)
        p2 = masked_softmax(jnp.einsum('bhqd,bhkd->bhqk', q2b, k2).astype(jnp.float32), visible)
        p = p1 - lam * p2
        return jnp.einsum('bhqk,bhkd->bhqd', p.astype(vh.dtype), vh)

    out = lax.map(block, jnp.arange(n_blocks))
    return out.transpose(1, 0, 3, 2, 4).reshape(B, Lp, DA_HEADS, DA_VDIM)[:, :L]

def causal_conv(x, w):
    C = x.shape[-1]
    return lax.conv_general_dilated(
        x, w[:, None, :].astype(x.dtype), window_strides=(1,), padding=[(CONV_K - 1, 0)],
        dimension_numbers=('NWC', 'WIO', 'NWC'), feature_group_count=C)

def gated_delta_rule(q, k, v, g, beta):
    B, L, H, DK = q.shape
    DV = v.shape[-1]
    n = -(-L // CHUNK)
    Lp = n * CHUNK
    f32 = jnp.float32

    def chunks(t):
        t = jnp.pad(t.astype(f32), ((0, 0), (0, Lp - L)) + ((0, 0),) * (t.ndim - 2))
        return jnp.moveaxis(t.reshape((B, n, CHUNK) + t.shape[2:]), 1, 0)

    q = chunks(q).transpose(0, 1, 3, 2, 4)
    k = chunks(k).transpose(0, 1, 3, 2, 4)
    v = chunks(v).transpose(0, 1, 3, 2, 4)
    g = chunks(g).transpose(0, 1, 3, 2)
    beta = chunks(beta).transpose(0, 1, 3, 2)

    causal = jnp.tril(jnp.ones((CHUNK, CHUNK), dtype=bool))
    strict = jnp.tril(jnp.ones((CHUNK, CHUNK), dtype=bool), -1)
    gc = jnp.cumsum(g, axis=-1)
    diff = gc[..., :, None] - gc[..., None, :]
    decay = jnp.where(causal, jnp.exp(jnp.where(causal, diff, 0.0)), 0.0)
    k_beta = k * beta[..., None]
    a_kk = jnp.where(strict, jnp.einsum('nbhcd,nbhsd->nbhcs', k_beta, k) * decay, 0.0)
    m = a_kk + jnp.eye(CHUNK, dtype=f32)
    rhs = jnp.concatenate([v * beta[..., None], k_beta * jnp.exp(gc)[..., None]], axis=-1)
    sol = lax.linalg.triangular_solve(m, rhs, left_side=True, lower=True, unit_diagonal=True)
    u, w = sol[..., :DV], sol[..., DV:]
    a_qk = jnp.where(causal, jnp.einsum('nbhcd,nbhsd->nbhcs', q, k) * decay, 0.0)
    q_g = q * jnp.exp(gc)[..., None]
    g_last = gc[..., -1]
    k_g = k * jnp.exp(g_last[..., None] - gc)[..., None]

    def step(S, xs):
        u_c, w_c, q_c, aqk_c, k_c, gl = xs
        v_new = u_c - jnp.einsum('bhck,bhkv->bhcv', w_c, S)
        o = jnp.einsum('bhck,bhkv->bhcv', q_c, S) + jnp.einsum('bhcs,bhsv->bhcv', aqk_c, v_new)
        S = S * jnp.exp(gl)[..., None, None] + jnp.einsum('bhck,bhcv->bhkv', k_c, v_new)
        return S, o

    S0 = jnp.zeros((B, H, DK, DV), f32)
    _, o = lax.scan(step, S0, (u, w, q_g, a_qk, k_g, g_last))
    return o.transpose(1, 0, 3, 2, 4).reshape(B, Lp, H, DV)[:, :L]

def hier_moe(u, w_group, b_group, w_router, b_router, w_gate, w_up, w_down):
    B, L, D = u.shape
    t = u.reshape(B * L, D)
    glog = (t @ w_group).astype(jnp.float32) + b_group.astype(jnp.float32)
    gprob = jax.nn.softmax(glog, axis=-1)
    gsel = jnp.argmax(glog, axis=-1)
    psel = jnp.take_along_axis(gprob, gsel[:, None], axis=-1)
    elog = ((t @ w_router).astype(jnp.float32) + b_router.astype(jnp.float32)).reshape(-1, N_GROUPS, EXPERTS_PER_GROUP)
    elog_g = jnp.take_along_axis(elog, gsel[:, None, None], axis=1)[:, 0]
    topv, topi = lax.top_k(jax.nn.softmax(elog_g, axis=-1), TOP_K)
    wts = topv / jnp.sum(topv, axis=-1, keepdims=True) * psel
    eidx = gsel[:, None] * EXPERTS_PER_GROUP + topi
    combine = jnp.einsum('tk,tke->te', wts, jax.nn.one_hot(eidx, N_EXPERTS, dtype=jnp.float32)).astype(t.dtype)
    y = jnp.zeros_like(t)
    for gi in range(N_GROUPS):
        sl = slice(gi * EXPERTS_PER_GROUP, (gi + 1) * EXPERTS_PER_GROUP)
        hg = jnp.einsum('td,edf->tef', t, w_gate[sl])
        hu = jnp.einsum('td,edf->tef', t, w_up[sl])
        act = jax.nn.silu(hg) * hu * combine[:, sl, None]
        y = y + jnp.einsum('tef,efd->td', act, w_down[sl])
    return y.reshape(B, L, D)

def setup_inputs(seed: int = 0) -> dict:
    key = jax.random.key(seed)
    ks = jax.random.split(key, 24)
    f32 = jnp.float32
    nrm = lambda k, shape, s: jax.random.normal(k, shape, f32) * s
    dt = jnp.exp(jax.random.uniform(ks[10], (DEPTH, GDN_HEADS), f32) * (math.log(0.1) - math.log(0.001)) + math.log(0.001))
    return {
        "x": nrm(ks[0], (BATCH, SEQ, D_MODEL), 1.0),
        "meta": nrm(ks[1], (N_META, D_MODEL), 1.0),
        "norm_mix": 1.0 + nrm(ks[2], (DEPTH, D_MODEL), 0.02),
        "w_in": nrm(ks[3], (DEPTH, D_MODEL, PROJ), D_MODEL ** -0.5),
        "lambda_q1": nrm(ks[4], (DEPTH, DA_DIM), 0.1),
        "lambda_k1": nrm(ks[5], (DEPTH, DA_DIM), 0.1),
        "lambda_q2": nrm(ks[6], (DEPTH, DA_DIM), 0.1),
        "lambda_k2": nrm(ks[7], (DEPTH, DA_DIM), 0.1),
        "diff_norm": 1.0 + nrm(ks[8], (DEPTH, DA_VDIM), 0.02),
        "conv_w": nrm(ks[9], (DEPTH, CONV_K, COL_QKVB), CONV_K ** -0.5),
        "a_log": jnp.log(jax.random.uniform(ks[11], (DEPTH, GDN_HEADS), f32, 1.0, 16.0)),
        "dt_bias": dt + jnp.log(-jnp.expm1(-dt)),
        "gdn_norm": 1.0 + nrm(ks[12], (DEPTH, GDN_DV), 0.02),
        "w_out": nrm(ks[13], (DEPTH, MIX_WIDTH, D_MODEL), MIX_WIDTH ** -0.5),
        "norm_ffn": 1.0 + nrm(ks[14], (DEPTH, D_MODEL), 0.02),
        "w_group": nrm(ks[15], (DEPTH, D_MODEL, N_GROUPS), D_MODEL ** -0.5),
        "b_group": nrm(ks[16], (DEPTH, N_GROUPS), 0.01),
        "w_router": nrm(ks[17], (DEPTH, D_MODEL, N_EXPERTS), D_MODEL ** -0.5),
        "b_router": nrm(ks[18], (DEPTH, N_EXPERTS), 0.01),
        "w_gate": nrm(ks[19], (DEPTH, N_EXPERTS, D_MODEL, D_EXPERT), D_MODEL ** -0.5),
        "w_up": nrm(ks[20], (DEPTH, N_EXPERTS, D_MODEL, D_EXPERT), D_MODEL ** -0.5),
        "w_down": nrm(ks[21], (DEPTH, N_EXPERTS, D_EXPERT, D_MODEL), D_EXPERT ** -0.5),
        "norm_final": 1.0 + nrm(ks[22], (D_MODEL,), 0.02),
    }

def reference(x, meta, norm_mix, w_in, lambda_q1, lambda_k1, lambda_q2, lambda_k2, diff_norm, conv_w,
              a_log, dt_bias, gdn_norm, w_out, norm_ffn, w_group, b_group, w_router, b_router,
              w_gate, w_up, w_down, norm_final):
    B, S, D = x.shape
    L = S + N_META
    h = jnp.concatenate([jnp.broadcast_to(meta[None].astype(x.dtype), (B, N_META, D)), x], axis=1)
    pos = jnp.arange(L, dtype=jnp.float32)
    inv_freq = ROPE_THETA ** (-jnp.arange(0, DA_DIM, 2, dtype=jnp.float32) / DA_DIM)
    ang = pos[:, None] * inv_freq[None, :]
    cos, sin = jnp.cos(ang), jnp.sin(ang)

    for l in range(DEPTH):
        lam_init = 0.8 - 0.6 * math.exp(-0.3 * l)
        u = rmsnorm(h, norm_mix[l])
        proj = u @ w_in[l]
        qa, ka, va, qkvb, zb, ab, bb = jnp.split(proj, SPLITS, axis=-1)

        qa = rope(qa.reshape(B, L, 2 * DA_HEADS, DA_DIM), cos, sin).reshape(B, L, DA_HEADS, 2, DA_DIM)
        ka = rope(ka.reshape(B, L, 2 * DA_HEADS, DA_DIM), cos, sin).reshape(B, L, DA_HEADS, 2, DA_DIM)
        lam = (jnp.exp(jnp.sum(lambda_q1[l].astype(jnp.float32) * lambda_k1[l].astype(jnp.float32)))
               - jnp.exp(jnp.sum(lambda_q2[l].astype(jnp.float32) * lambda_k2[l].astype(jnp.float32))) + lam_init)
        oa = diff_attention(qa, ka, va.reshape(B, L, DA_HEADS, DA_VDIM), lam)
        oa = rmsnorm(oa, diff_norm[l]) * (1.0 - lam_init)

        qkvb = jax.nn.silu(causal_conv(qkvb, conv_w[l]))
        qb, kb, vb = jnp.split(qkvb, [GDN_HEADS * GDN_DK, 2 * GDN_HEADS * GDN_DK], axis=-1)
        qb = l2norm(qb.reshape(B, L, GDN_HEADS, GDN_DK)) * (GDN_DK ** -0.5)
        kb = l2norm(kb.reshape(B, L, GDN_HEADS, GDN_DK))
        vb = vb.reshape(B, L, GDN_HEADS, GDN_DV)
        beta = jax.nn.sigmoid(bb.astype(jnp.float32))
        g = -jnp.exp(a_log[l].astype(jnp.float32)) * jax.nn.softplus(ab.astype(jnp.float32) + dt_bias[l].astype(jnp.float32))
        ob = gated_delta_rule(qb, kb, vb, g, beta).astype(h.dtype)
        ob = rmsnorm(ob, gdn_norm[l]) * jax.nn.silu(zb.reshape(B, L, GDN_HEADS, GDN_DV))

        mix = jnp.concatenate([oa.reshape(B, L, DA_WIDTH), ob.reshape(B, L, GDN_WIDTH)], axis=-1)
        h = h + mix @ w_out[l]

        h = h + hier_moe(rmsnorm(h, norm_ffn[l]), w_group[l], b_group[l], w_router[l], b_router[l],
                         w_gate[l], w_up[l], w_down[l])

    h = rmsnorm(h, norm_final)
    return h[:, N_META:]


_drawn_inputs = setup_inputs


def setup_inputs(seed=0):
    import zlib

    import numpy as np

    out = dict(_drawn_inputs(seed))
    spreads = {}
    factors = {'gdn_norm': 9.651,
     'b_group': 20.386,
     'b_router': 11.433,
     'norm_final': 7.985,
     'lambda_k1': 3.805,
     'lambda_q2': 3.976,
     'diff_norm': 4.677,
     'norm_ffn': 3.096}
    for name, (base, spread) in spreads.items():
        noise = np.random.default_rng([zlib.crc32(name.encode()), seed]).standard_normal(out[name].shape)
        drawn = base * np.exp(spread * noise) if base else spread * noise
        out[name] = __import__('jax').numpy.asarray(drawn.astype(out[name].dtype))
    for name, factor in factors.items():
        out[name] = (out[name] * factor).astype(out[name].dtype)
    return out
```

```python
from contextlib import ExitStack

import numpy as np

import concourse.bass as bass
from concourse import mybir

F32 = mybir.dt.float32
I32 = mybir.dt.int32
U32 = mybir.dt.uint32
ALU = mybir.AluOpType
ACT = mybir.ActivationFunctionType
AX = mybir.AxisListType

P = 128
D = 1024
KD = D // P
SEQ = 1024
META = 16
L = SEQ + META
NT = SEQ // P
EPS = 1e-6
HA = 4
HB = 8
DK = 64
VA = 128
LAM_INIT = 0.8 - 0.6
BLK = 512
COL_QA, COL_KA, COL_VA, COL_QKVB, COL_ZB, COL_AB = 0, 512, 1024, 1536, 3072, 3584
NE, NG, EPG, FE = 32, 4, 8, 256
MAXBLK = 48
BIG = 1.0e30
LEVELS = 7

C_ID, C_UP, C_SUP, C_BLK, C_LEV = 0, 128, 256, 384, 512
C_COS = C_LEV + LEVELS * 128
C_SIN = C_COS + (NT + 1) * 64
C_IOTA = C_SIN + (NT + 1) * 64
C_TOK = C_IOTA + 128
C_E128 = C_TOK + 2 * NT
C_ONE = C_E128 + 32
C_IG = C_ONE + 128
C_EPS = C_IG + 32
C_N = C_EPS + 1


def constants():
    c = np.zeros((P, C_N), np.float32)
    p = np.arange(P)
    c[:, C_ID:C_ID + 128] = np.eye(P)
    c[:, C_UP:C_UP + 128] = p[:, None] <= p[None, :]
    c[:, C_SUP:C_SUP + 128] = p[:, None] < p[None, :]
    c[:, C_BLK:C_BLK + 128] = (p[:, None] // 64) == (p[None, :] // 64)
    for lv in range(LEVELS):
        s = 1 << lv
        same = (p[:, None] // (2 * s)) == (p[None, :] // (2 * s))
        c[:, C_LEV + lv * 128:C_LEV + (lv + 1) * 128] = same & (p[:, None] // s % 2 == 0) & (p[None, :] // s % 2 == 1)
    inv = (10000.0 ** (-np.arange(0, 64, 2) / 64.0)).astype(np.float32)
    for t in range(NT + 1):
        pos = (np.arange(P) + (META + P * t if t < NT else 0)).astype(np.float32)
        ang = pos[:, None] * inv[None, :]
        co, si = np.cos(ang), np.sin(ang)
        c[:, C_COS + 64 * t:C_COS + 64 * t + 64] = np.concatenate([co, co], 1)
        c[:, C_SIN + 64 * t:C_SIN + 64 * t + 64] = np.concatenate([-si, si], 1)
    c[:, C_IOTA:C_IOTA + 128] = p[None, :]
    c[:, C_TOK:C_TOK + 2 * NT] = 2 * (p[:, None] + P * (np.arange(2 * NT) // 2)[None, :]) + np.arange(2 * NT)[None, :] % 2 + 1
    c[:, C_E128:C_E128 + 32] = 128 * np.arange(32)[None, :]
    c[:, C_ONE:C_ONE + 128] = 1.0
    c[:, C_IG:C_IG + 32] = np.arange(32)[None, :] - 1000.0
    c[:, C_EPS] = EPS
    return c


def rows(t):
    return P if t < NT else META


def col0(t):
    return META + P * t if t < NT else 0


class Seq:

    def __init__(self, eng, sem):
        self.eng, self.sem, self.n = eng, sem, 0

    def __call__(self, ins):
        self.n += 1
        ins.then_inc(self.sem, 1)
        self.eng.wait_ge(self.sem, self.n)


def clear(nc, sems):
    with nc.Block() as block:
        @block.gpsimd
        def _(pool):
            for x in sems:
                pool.sem_clear(x)


def project(nc, a, s, k):
    with ExitStack() as ctx, ExitStack() as phase:
        sb = lambda n, sh, dt=F32: ctx.enter_context(nc.sbuf_tensor(n, sh, dt))
        ps = lambda n, sh, dt=F32: ctx.enter_context(nc.psum_tensor(n, sh, dt))
        sems = []

        def sem(n):
            sems.append(ctx.enter_context(nc.semaphore(n)))
            return sems[-1]

        cst, cols = s["cst"], s["cols"]
        ident = cst[:, C_ID:C_ID + 128]
        uT = sb("uT", [P, KD, L])
        rowsb = sb("rowsb", [64, 128])
        ss = sb("ss", [P, NT + 1, 3])
        wblk = sb("wblk", [P, 2, KD, BLK])
        wab = sb("wab", [P, KD, 16])
        cv = sb("cv", [P, L])
        work = sb("work", [P, 3 + 3 * L])
        pad, sq, rn = work[:, 0:3 + L], work[:, 3 + L:3 + 2 * L], work[:, 3 + 2 * L:3 + 3 * L]
        xin = work[:, 3:3 + 2 * D].rearrange("p (b d) -> p b d", b=2)
        xsc = work[:, 3 + 2 * D:3 + 3 * D]
        rope = work[:, 3 + L:3 + L + 3 * BLK].rearrange("p (b d) -> p b d", b=3)
        zt = sb("zt", [P, 2, BLK])

        big = [ps(f"big{i}", [P, 1536]) for i in range(2)]
        small = [ps(f"small{i}", [P, 512]) for i in range(2)]

        x_in, rows_in, cst_in = [sem(f"x_in{i}") for i in range(2)], sem("rows_in"), sem("cst_in")
        w_in_sem = [sem(f"w_in{i}") for i in range(2)]
        wab_in = sem("wab_in")
        act_seq, dve_seq = sem("act_seq"), sem("dve_seq")
        ssq, xscaled, x_turned, u_copied = sem("ssq"), sem("xscaled"), sem("x_turned"), sem("u_copied")
        rows_turned, rows_copied = sem("rows_turned"), sem("rows_copied")
        pads = sem("pads")
        big_full, copied, conv0, conv_done, silu_done, sq_done, rn_done, qk_done = (
            sem(x) for x in ("big_full", "copied", "conv0", "conv_done", "silu_done", "sq_done", "rn_done", "qk_done"))
        tok_full, tok_act, roped, rope_turned, rope_copied = (
            sem(x) for x in ("tok_full", "tok_act", "roped", "rope_turned", "rope_copied"))
        w_used = sem("w_used")
        root_done = sem("root_done")
        z_out = [sem(f"z_out{i}") for i in range(2)]

        items = [("T", 0)]
        for m in range(1, 12):
            items.append(("T", m))
            if m - 1 < 8:
                items.append(("N", m - 1))
        nitem = len(items)
        tok = [("ab", t) for t in range(NT + 1)] + [("qa", t) for t in range(NT)] + [("ka", t) for t in range(NT + 1)] \
            + [("va", t) for t in range(NT + 1)] + [("zb", t) for t in range(NT)]
        wcol = [COL_QKVB, COL_QKVB + 512, COL_QKVB + 1024, COL_QA, COL_KA, COL_VA, COL_ZB]
        wbuf = {"qa": 3, "ka": 4, "va": 5, "zb": 6}
        order = [NT] + list(range(NT))
        is_rope = [kd in ("qa", "ka") for kd, _ in tok]
        tokbank = [big[0][:, 0:512], big[0][:, 512:1024], big[1][:, 0:512], big[1][:, 512:1024]]
        ropes_before = lambda n: sum(is_rope[:n])
        acts_before = lambda n: n - ropes_before(n)

        block = phase.enter_context(nc.Block())

        @block.sync
        def _(sp):
            sp.dma_start(s["cst"][:], a["consts"]).then_inc(cst_in, 16)
            sp.dma_start(rowsb[0:48, :], a["conv_w"].rearrange("o i (m c) -> (o i m) c", c=128)).then_inc(rows_in, 16)
            sp.dma_start(rowsb[48:56, :], a["norm_mix"].rearrange("o (m c) -> (o m) c", c=128)).then_inc(rows_in, 16)
            sp.dma_start(rowsb[56:64, :], a["norm_ffn"].rearrange("o (m c) -> (o m) c", c=128)).then_inc(rows_in, 16)
            wv = a["w_in"].rearrange("o (k p) c -> (o p) k c", p=P)
            for j, t in enumerate(order):
                if j >= 2:
                    sp.wait_ge(xscaled, j - 1)
                src = a["x"][0, t * P:(t + 1) * P, :] if t < NT else a["meta"]
                sp.dma_start(xin[0:rows(t), j % 2, :], src).then_inc(x_in[j % 2], 16)
                if j == 2:
                    sp.dma_start(wblk[:, 0, :, :], wv[:, :, wcol[0]:wcol[0] + BLK]).then_inc(w_in_sem[0], 16)
            sp.dma_start(wblk[:, 1, :, :], wv[:, :, wcol[1]:wcol[1] + BLK]).then_inc(w_in_sem[1], 16)
            with nc.allow_non_contiguous_dma(reason="64-byte rows of the gate columns"):
                sp.dma_start(wab[:], wv[:, :, COL_AB:COL_AB + 16]).then_inc(wab_in, 16)
            for b in range(2, 7):
                sp.wait_ge(w_used, b - 1)
                sp.dma_start(wblk[:, b % 2, :, :], wv[:, :, wcol[b]:wcol[b] + BLK]).then_inc(w_in_sem[b % 2], 16)

            for t in range(NT):
                sp.wait_ge(tok_act, acts_before(tok.index(("zb", t))) + 1)
                sp.dma_start(a["z"][t], zt[:, t % 2, :]).then_inc(z_out[t % 2], 16)
            for b in range(2):
                sp.wait_ge(z_out[b], 16 * (NT // 2))

        @block.scalar
        def _(act):
            act.wait_ge(cst_in, 16)
            for j, t in enumerate(order):
                r = rows(t)
                act.wait_ge(x_in[j % 2], 16 * (j // 2 + 1))
                if j >= 1:
                    act.wait_ge(ssq, j)
                act.activation(cv[0:r, 0:D], xin[0:r, j % 2, :], ACT.Square, accum_out=ss[0:r, j, 0:1]).then_inc(ssq, 1)
                act.wait_ge(ssq, j + 1)
                act.activation(ss[0:r, j, 1:2], ss[0:r, j, 0:1], ACT.Sqrt, bias=cst[0:r, C_EPS:C_EPS + 1], scale=1.0 / D).then_inc(root_done, 1)
            act.wait_ge(pads, 1)
            act.wait_ge(x_turned, 2 * (NT + 1))
            for m in range(12):
                i = items.index(("T", m))
                act.wait_ge(big_full, i + 1)
                if m >= 1:
                    act.wait_ge(conv_done, m)
                act.activation(pad[:, 3:3 + L], big[i % 2][:, 0:L], ACT.Copy).then_inc(copied, 1)
                act.wait_ge(copied, m + 1)
                if m >= 1:
                    act.wait_ge(silu_done, m)
                if m == 0:
                    act.wait_ge(ssq, NT + 1)
                    act.wait_ge(rows_copied, 1)
                act.activation(cv[:], pad[:, 0:L], ACT.Copy, scale=cols[:, m:m + 1]).then_inc(conv0, 1)
                act.wait_ge(conv_done, m + 1)
                dst = (s["gq"], s["gk"], s["gv"])[m // 4][:, m % 4, :]
                act.activation(dst, cv[:], ACT.Silu).then_inc(silu_done, 1)
                if 1 <= m <= 8:
                    i = items.index(("N", m - 1))
                    act.wait_ge(big_full, i + 1)
                    if m >= 2:
                        act.wait_ge(qk_done, m - 1)
                    act.activation(rn[:], big[i % 2][:, 0:L], ACT.Sqrt, bias=cst[:, C_EPS:C_EPS + 1]).then_inc(rn_done, 1)
                if m < 8:
                    act.wait_ge(silu_done, m + 1)
                    act.activation(sq[:], dst, ACT.Square).then_inc(sq_done, 1)
            for n, (kind, t) in enumerate(tok):
                r = rows(t)
                src = tokbank[n % 4]
                if is_rope[n]:
                    q = ropes_before(n)
                    dst = s["aq"] if kind == "qa" else s["ak"]
                    off = t * P if kind == "qa" else col0(t)
                    act.wait_ge(rope_turned, q + 1)
                    act.activation(dst[:, :, off:off + r], small[q % 2][:].rearrange("p (h t) -> p h t", h=4)[:, :, 0:r],
                                   ACT.Copy).then_inc(rope_copied, 1)
                    continue
                act.wait_ge(tok_full, n + 1)
                if kind == "ab":
                    act.activation(s["ab"][0:r, t, :], src[0:r, 0:16], ACT.Copy).then_inc(tok_act, 1)
                elif kind == "va":
                    act.activation(s["av"][0:r, t, :], src[0:r, :], ACT.Copy).then_inc(tok_act, 1)
                else:
                    if t >= 2:
                        act.wait_ge(z_out[t % 2], 16 * (t // 2))
                    act.activation(zt[:, t % 2, :], src[0:r, :], ACT.Silu).then_inc(tok_act, 1)

        @block.vector
        def _(dve):
            seq = Seq(dve, dve_seq)
            dve.memset(pad[:, 0:3], 0.0).then_inc(pads, 1)
            seq(dve.memset(s["ab"][:], 0.0))
            dve.wait_ge(rows_turned, 1)
            dve.tensor_copy(cols[:, 0:64], small[0][:, 0:64]).then_inc(rows_copied, 1)
            dve.wait_ge(rows_copied, 1)
            gain = cols[:, 48:56]
            for j, t in enumerate(order):
                r = rows(t)
                dve.wait_ge(root_done, j + 1)
                seq(dve.reciprocal(ss[0:r, j, 2:3], ss[0:r, j, 1:2]))
                if j >= 1:
                    dve.wait_ge(x_turned, 2 * j)
                dve.tensor_scalar(xsc[0:r, :], xin[0:r, j % 2, :], ss[0:r, j, 2:3], None, ALU.mult).then_inc(xscaled, 1)
                for half in range(2):
                    dve.wait_ge(x_turned, 2 * j + half + 1)
                    src = small[half][:].rearrange("p (k t) -> p k t", k=4)[:, :, 0:r]
                    g = gain[:, 4 * half:4 * half + 4].unsqueeze(2).to_broadcast([P, 4, r])
                    dve.tensor_tensor(uT[:, 4 * half:4 * half + 4, col0(t):col0(t) + r], src, g, ALU.mult).then_inc(u_copied, 1)

            def conv(m):
                dve.wait_ge(conv0, m + 1)
                for i in range(1, 4):
                    w = cols[:, 12 * i + m:12 * i + m + 1]
                    ins = dve.scalar_tensor_tensor(cv[:], pad[:, i:i + L], w, cv[:], ALU.mult, ALU.add)
                    if i < 3:
                        seq(ins)
                    else:
                        ins.then_inc(conv_done, 1)

            def l2(m):
                dve.wait_ge(rn_done, m + 1)
                seq(dve.reciprocal(rn[:], rn[:]))
                dst = (s["gq"], s["gk"])[m // 4][:, m % 4, :]
                dve.scalar_tensor_tensor(dst, dst, DK ** -0.5 if m < 4 else 1.0, rn[:], ALU.mult, ALU.mult).then_inc(qk_done, 1)

            for m in range(12):
                conv(m)
                if 1 <= m <= 8:
                    l2(m - 1)
            for n, (kind, t) in enumerate(tok):
                if not is_rope[n]:
                    continue
                r, q = rows(t), ropes_before(n)
                src = tokbank[n % 4][0:r, :].rearrange("p (h d) -> p h d", d=64)
                co = cst[0:r, C_COS + 64 * t:C_COS + 64 * t + 64].unsqueeze(1).to_broadcast([r, 8, 64])
                si = cst[0:r, C_SIN + 64 * t:C_SIN + 64 * t + 64]
                dve.wait_ge(tok_full, n + 1)
                v = lambda b: rope[0:r, b, :].rearrange("p (h d) -> p h d", d=64)
                if q >= 1:
                    dve.wait_ge(rope_turned, q)
                dve.tensor_tensor(v(0), src, co, ALU.mult)
                dve.tensor_tensor(v(1)[:, :, 0:32], src[:, :, 32:64], si[:, 0:32].unsqueeze(1).to_broadcast([r, 8, 32]), ALU.mult)
                seq(dve.tensor_tensor(v(1)[:, :, 32:64], src[:, :, 0:32], si[:, 32:64].unsqueeze(1).to_broadcast([r, 8, 32]), ALU.mult))
                dve.tensor_tensor(rope[0:r, 2, :], rope[0:r, 0, :], rope[0:r, 1, :], ALU.add).then_inc(roped, 1)
                dve.wait_ge(roped, q + 1)

        @block.tensor
        def _(pe):
            pe.wait_ge(cst_in, 16)
            pe.wait_ge(rows_in, 48)
            pe.transpose(small[0][:, 0:64], rowsb[:], ident[0:64, 0:64]).then_inc(rows_turned, 1)
            pe.wait_ge(rows_copied, 1)
            for j, t in enumerate(order):
                r = rows(t)
                pe.wait_ge(xscaled, j + 1)
                for half in range(2):
                    if j >= 1:
                        pe.wait_ge(u_copied, 2 * j - 1 + half)
                    for kk in range(4):
                        kx = 4 * half + kk
                        mm = pe.transpose(small[half][:, kk * 128:kk * 128 + r], xsc[0:r, kx * P:(kx + 1) * P], ident[0:r, 0:r])
                    mm.then_inc(x_turned, 1)
            pe.wait_ge(u_copied, 2 * (NT + 1))

            def freed(i):
                kind, m = items[i - 2]
                pe.wait_ge(copied if kind == "T" else rn_done, m + 1)

            for i, (kind, m) in enumerate(items):
                if i >= 2:
                    freed(i)
                if kind == "T":
                    b = m // 4
                    if m % 4 == 0:
                        pe.wait_ge(w_in_sem[b % 2], 16 * (b // 2 + 1))
                    for c in range(0, L, 512):
                        n = min(512, L - c)
                        for kx in range(KD):
                            mm = pe.matmul(big[i % 2][:, c:c + n], wblk[:, b % 2, kx, (m % 4) * 128:(m % 4 + 1) * 128],
                                           uT[:, kx, c:c + n], start=kx == 0, stop=kx == KD - 1)
                    mm.then_inc(big_full, 1)
                    if m % 4 == 3:
                        pe.wait_ge(big_full, i + 1)
                        pe.sem_inc(w_used, 1)
                else:
                    pe.wait_ge(sq_done, m + 1)
                    for c in range(0, L, 512):
                        n = min(512, L - c)
                        mm = pe.matmul(big[i % 2][:, c:c + n], cst[:, C_BLK:C_BLK + 128], sq[:, c:c + n], start=True, stop=True)
                    mm.then_inc(big_full, 1)

            def turn(n):
                kind, t = tok[n]
                r, q = rows(t), ropes_before(n)
                pe.wait_ge(roped, q + 1)
                if q >= 2:
                    pe.wait_ge(rope_copied, q - 1)
                for h in range(4):
                    mm = pe.transpose(small[q % 2][:, h * 128:h * 128 + r], rope[0:r, 2, h * 128:(h + 1) * 128], ident[0:r, 0:r])
                mm.then_inc(rope_turned, 1)

            for n, (kind, t) in enumerate(tok):
                if n < 4:
                    freed(nitem if n < 2 else nitem + 1)
                else:
                    j = n - 4
                    pe.wait_ge(roped if is_rope[j] else tok_act, (ropes_before(j) if is_rope[j] else acts_before(j)) + 1)
                c, r = col0(t), rows(t)
                if kind == "ab":
                    if n == 0:
                        pe.wait_ge(wab_in, 16)
                    w, nn = wab, 16
                else:
                    b = wbuf[kind]
                    w, nn = wblk[:, b % 2], BLK
                    if t == 0:
                        pe.wait_ge(w_in_sem[b % 2], 16 * (b // 2 + 1))
                for kx in range(KD):
                    mm = pe.matmul(tokbank[n % 4][0:r, 0:nn], uT[:, kx, c:c + r], w[:, kx, 0:nn], start=kx == 0, stop=kx == KD - 1)
                mm.then_inc(tok_full, 1)
                if kind in ("qa", "ka") and t == (NT - 1 if kind == "qa" else NT):
                    pe.wait_ge(tok_full, n + 1)
                    pe.sem_inc(w_used, 1)
                if n >= 1 and is_rope[n - 1]:
                    turn(n - 1)

        phase.close()
        clear(nc, sems)


def attention(nc, a, s):
    with ExitStack() as ctx, ExitStack() as phase:
        sb = lambda n, sh, dt=F32: ctx.enter_context(nc.sbuf_tensor(n, sh, dt))
        ps = lambda n, sh, dt=F32: ctx.enter_context(nc.psum_tensor(n, sh, dt))
        sems = []

        def sem(n):
            sems.append(ctx.enter_context(nc.semaphore(n)))
            return sems[-1]

        cst, mix = s["cst"], s["mix"]
        ident = cst[:, C_ID:C_ID + 128]
        probs = sb("probs", [P, 2, 2, L])
        probsT = sb("probsT", [P, 2, NT + 1, P])
        nmax = sb("nmax", [P, 2, 2])
        bias = sb("bias", [P, 2, 2])
        rsum = sb("rsum", [P, 2, 2])
        rinv = sb("rinv", [P, 2, 2])
        coef = sb("coef", [P, 2])
        lamv = sb("lamv", [P, 4, 64])
        lam = sb("lam", [P, 8])
        gain = sb("gain", [P, VA])
        stat = sb("stat", [P, 3, NT * HA])
        sqo = sb("sqo", [P, NT, 512])

        score = [ps(f"score{c}", [P, 1536]) for c in range(2)]
        turnb = ps("turnb", [P, 512])
        outb = ps("outb", [P, 512])

        par_in, dve_seq, act_seq = sem("par_in"), sem("dve_seq"), sem("act_seq")
        lam_sum, lam_exp, lam_done = sem("lam_sum"), sem("lam_exp"), sem("lam_done")
        s_full, maxed, exped, mixed, turned, t_copied, pv_done, o_copied = (
            sem(x) for x in ("s_full", "maxed", "exped", "mixed", "turned", "t_copied", "pv_done", "o_copied"))
        o_sq, o_root = sem("o_sq"), sem("o_root")

        items = [(i, h) for i in range(NT) for h in range(HA)]
        N = len(items)
        nkeys = lambda i: META + P * (i + 1)
        fills = lambda n: -(-(items[n][0] + 2) // 4)
        fills_before = lambda n: sum(fills(m) for m in range(n))

        block = phase.enter_context(nc.Block())

        @block.sync
        def _(sp):
            for j, n in enumerate(("lambda_q1", "lambda_k1", "lambda_q2", "lambda_k2")):
                sp.dma_start(lamv[:, j, :], a[n].to_broadcast([P, 64])).then_inc(par_in, 16)
            sp.dma_start(gain[:], a["diff_norm"].to_broadcast([P, VA])).then_inc(par_in, 16)

        @block.scalar
        def _(act):
            act.wait_ge(lam_sum, 1)
            act.activation(lam[:, 2:4], lam[:, 0:2], ACT.Exp).then_inc(lam_exp, 1)
            for n in range(N + 1):
                if n < N:
                    i, h = items[n]
                    for c in range(2):
                        act.wait_ge(maxed, 2 * n + c + 1)
                        if n >= 2 and c == 0:
                            act.wait_ge(turned, fills_before(n - 1))
                        act.activation(probs[:, n % 2, c, 0:nkeys(i)], score[c][:, 0:nkeys(i)], ACT.Exp,
                                       bias=bias[:, n % 2, c:c + 1], scale=DK ** -0.5,
                                       accum_out=rsum[:, n % 2, c:c + 1]).then_inc(exped, 1)
                if n >= 1:
                    m = n - 1
                    i = items[m][0]
                    for f in range(fills(m)):
                        act.wait_ge(turned, fills_before(m) + f + 1)
                        if f == 0 and m >= 2:
                            act.wait_ge(pv_done, m - 1)
                        nb = min(4, i + 2 - 4 * f)
                        if f == 0:
                            act.activation(probsT[0:META, m % 2, 0, :], turnb[0:META, 0:128], ACT.Copy)
                            act.activation(probsT[:, m % 2, 1:nb, :], turnb[:, 128:nb * 128], ACT.Copy).then_inc(t_copied, 1)
                        else:
                            act.activation(probsT[:, m % 2, 4 * f:4 * f + nb, :], turnb[:, 0:nb * 128], ACT.Copy).then_inc(t_copied, 1)
            act.wait_ge(o_sq, 1)
            act.activation(stat[:, 1, :], stat[:, 0, :], ACT.Sqrt, bias=cst[:, C_EPS:C_EPS + 1], scale=1.0 / VA).then_inc(o_root, 1)

        @block.vector
        def _(dve):
            seq = Seq(dve, dve_seq)
            dve.wait_ge(par_in, 80)
            seq(dve.tensor_tensor(lamv[:, 0, :], lamv[:, 0, :], lamv[:, 1, :], ALU.mult))
            seq(dve.tensor_tensor(lamv[:, 2, :], lamv[:, 2, :], lamv[:, 3, :], ALU.mult))
            dve.tensor_reduce(lam[:, 0:2], lamv[:].rearrange("p (a b) c -> p a b c", a=2)[:, :, 0, :], AX.X, ALU.add).then_inc(lam_sum, 1)
            dve.wait_ge(lam_exp, 1)
            seq(dve.tensor_tensor(lam[:, 4:5], lam[:, 3:4], lam[:, 2:3], ALU.subtract))
            seq(dve.tensor_scalar(lam[:, 5:6], lam[:, 4:5], -LAM_INIT, None, ALU.add))

            def row_max(n, c):
                i = items[n][0]
                nk = nkeys(i)
                dve.wait_ge(s_full, 2 * n + c + 1)
                seq(dve.memset(score[c][0:64, nk - 64:nk], -BIG))
                seq(dve.tensor_reduce(nmax[:, n % 2, c:c + 1], score[c][:, 0:nk], AX.X, ALU.max))
                dve.tensor_scalar(bias[:, n % 2, c:c + 1], nmax[:, n % 2, c:c + 1], -DK ** -0.5, None, ALU.mult).then_inc(maxed, 1)

            def difference(n):
                b, nk = n % 2, nkeys(items[n][0])
                dve.wait_ge(exped, 2 * n + 2)
                if n >= 2:
                    dve.wait_ge(o_copied, n - 1)
                seq(dve.reciprocal(rinv[:, b, :], rsum[:, b, :]))
                seq(dve.tensor_scalar(coef[:, b:b + 1], rinv[:, b, 1:2], rsum[:, b, 0:1], lam[:, 5:6], ALU.mult, ALU.mult))
                dve.scalar_tensor_tensor(probs[:, b, 0, 0:nk], probs[:, b, 1, 0:nk], coef[:, b:b + 1], probs[:, b, 0, 0:nk],
                                         ALU.mult, ALU.add).then_inc(mixed, 1)

            def output(n):
                i, h = items[n]
                dve.wait_ge(pv_done, n + 1)
                dve.tensor_scalar(mix[:, i, h * VA:(h + 1) * VA], outb[:, h * VA:(h + 1) * VA], rinv[:, n % 2, 0:1], None,
                                  ALU.mult).then_inc(o_copied, 1)

            for n in range(N + 1):
                if n < N:
                    row_max(n, 0)
                if n >= 2:
                    output(n - 2)
                if n >= 1:
                    difference(n - 1)
                if n < N:
                    row_max(n, 1)
            output(N - 1)
            dve.wait_ge(o_copied, N)
            om = mix[:, :, 0:512]
            seq(dve.tensor_tensor(sqo[:], om, om, ALU.mult))
            dve.tensor_reduce(stat[:, 0, :], sqo[:].rearrange("p t (h d) -> p (t h) d", d=VA), AX.X, ALU.add).then_inc(o_sq, 1)
            dve.wait_ge(o_root, 1)
            seq(dve.reciprocal(stat[:, 2, :], stat[:, 1, :]))
            seq(dve.tensor_scalar(stat[:, 2, :], stat[:, 2, :], 1.0 - LAM_INIT, None, ALU.mult))
            for i in range(NT):
                o = mix[:, i, 0:512].rearrange("p (h d) -> p h d", d=VA)
                r = stat[:, 2, HA * i:HA * i + HA].unsqueeze(2).to_broadcast([P, HA, VA])
                seq(dve.tensor_tensor(o, o, r, ALU.mult))
                seq(dve.tensor_tensor(o, o, gain[:].unsqueeze(1).to_broadcast([P, HA, VA]), ALU.mult))

        @block.tensor
        def _(pe):
            def scores(n):
                i, h = items[n]
                nk = nkeys(i)
                for c in range(2):
                    if n >= 1:
                        pe.wait_ge(exped, 2 * n + c - 1)
                    for k0 in range(0, nk, 512):
                        k1 = min(nk, k0 + 512)
                        mm = pe.matmul(score[c][:, k0:k1], s["aq"][64 * c:64 * c + 64, h, P * i:P * i + P],
                                       s["ak"][64 * c:64 * c + 64, h, k0:k1], start=True, stop=True)
                    mm.then_inc(s_full, 1)

            def weighted(n):
                i, h = items[n]
                pe.wait_ge(mixed, n + 1)
                for f in range(fills(n)):
                    g = fills_before(n) + f
                    if g >= 1:
                        pe.wait_ge(t_copied, g)
                    for b in range(4 * f, min(4 * f + 4, i + 2)):
                        k0, kn = (0, META) if b == 0 else (META + P * (b - 1), P)
                        mm = pe.transpose(turnb[0:kn, (b % 4) * 128:(b % 4 + 1) * 128], probs[:, n % 2, 0, k0:k0 + kn], ident)
                    mm.then_inc(turned, 1)
                pe.wait_ge(t_copied, fills_before(n + 1))
                if n >= 4:
                    pe.wait_ge(o_copied, n - 3)
                for b in range(i + 2):
                    kn = META if b == 0 else P
                    mm = pe.matmul(outb[:, h * VA:(h + 1) * VA], probsT[0:kn, n % 2, b, :],
                                   s["av"][0:kn, NT if b == 0 else b - 1, h * VA:(h + 1) * VA], start=b == 0, stop=b == i + 1)
                mm.then_inc(pv_done, 1)

            for n in range(N + 1):
                if n < N:
                    scores(n)
                if n >= 1:
                    weighted(n - 1)

        phase.close()
        clear(nc, sems)


def deltanet(nc, a, s):
    with ExitStack() as ctx, ExitStack() as phase:
        sb = lambda n, sh, dt=F32: ctx.enter_context(nc.sbuf_tensor(n, sh, dt))
        ps = lambda n, sh, dt=F32: ctx.enter_context(nc.psum_tensor(n, sh, dt))
        sems = []

        def sem(n):
            sems.append(ctx.enter_context(nc.semaphore(n)))
            return sems[-1]

        sem2 = lambda n: [sem(f"{n}{b}") for b in range(2)]
        cst, mix, gq, gk, gv = s["cst"], s["mix"], s["gq"], s["gk"], s["gv"]
        ident, upper = cst[:, C_ID:C_ID + 128], cst[:, C_UP:C_UP + 128]
        TILES = [NT] + list(range(NT))
        NJ = len(TILES)
        G8 = NJ * HB

        free = [0]

        def carve(*dims):
            n = int(np.prod(dims))
            v = s["region"][:, free[0]:free[0] + n]
            free[0] += n
            names = " ".join("abc"[:len(dims)])
            return v.rearrange(f"p ({names}) -> p {names}", **{k: d for k, d in zip("abc", dims)}) if len(dims) > 1 else v

        inv = carve(2, HB, P)
        aqk = carve(2, HB, P)
        tri = carve(HB, P)
        xm = carve(HB, P)
        ntm = carve(HB, P)
        bt = carve(2, HB, P)
        dec = carve(HB, P)
        dif = carve(HB, P)
        decm = carve(HB, P)
        ktok, vtok = sb("ktok", [P, 2, 512]), sb("vtok", [P, 2, 512])
        zz, vn, v2 = sb("zz", [P, 512]), sb("vn", [P, 512]), sb("v2", [P, 512])
        state = sb("state", [P, 4, DK])
        gat = sb("gat", [P, 10, G8])
        gc, eg, neg, beta = gat[:, 0, :], gat[:, 1, :], gat[:, 2, :], gat[:, 3, :]
        graw, tmp, tmp2 = gat[:, 4, :], gat[:, 5, :], gat[:, 6, :]
        par = sb("par", [P, 3, HB])
        gain = sb("gdn_gain", [P, DK])
        glc, ekl, egs = sb("glc", [P, 2, HB]), sb("ekl", [P, 2, HB]), sb("egs", [P, 2, 4])
        gl = sb("gl", [P, 2, 2, 4])
        stat = sb("gstat", [P, 3, NT * HB])
        zg = sb("zg", [P, NT, 512])
        sqg = gk[:].rearrange("p m l -> p (m l)")[:, 0:NT * 512].rearrange("p (t c) -> p t c", t=NT)

        W = [ps(f"W{i}", [P, 512]) for i in range(8)]
        par_in, z_in, dve_seq, act_seq, pool_seq = (sem(x) for x in ("gpar_in", "z_in", "gdve_seq", "gact_seq", "gpool_seq"))
        g1, g2, g3, g4, gc_full, gates, eg_done = (sem(x) for x in ("g1", "g2", "g3", "g4", "gc_full", "gates", "eg_done"))
        kk_full, kq_full, gcb_full, d_done, dec_done, decm_done = (
            sem2(x) for x in ("kk_full", "kq_full", "gcb_full", "d_done", "dec_done", "decm_done"))
        nt_done, aqk_done, r1_done, t1_turned, t1_copied, bt_done = (
            sem2(x) for x in ("nt_done", "aqk_done", "r1_done", "t1_turned", "t1_copied", "bt_done"))
        x_full, x_copied, y_full, t_new, r_turned, r_copied, r_done = (
            sem2(x) for x in ("x_full", "x_copied", "y_full", "t_new", "r_turned", "r_copied", "r_done"))
        kt_turned, kt_copied, vt_turned, vt_copied, glc_done, ekl_done, egs_done = (
            sem(x) for x in ("kt_turned", "kt_copied", "vt_turned", "vt_copied", "glc_done", "ekl_done", "egs_done"))
        ks_full, z_done, v_full, vn_done, v2_done, o2_full, s_full, s_done, o_done = (
            sem(x) for x in ("ks_full", "z_done", "v_full", "vn_done", "v2_done", "o2_full", "gs_full", "s_done", "o_done"))
        gl_done = sem("gl_done")
        o_sq, o_root = sem("go_sq"), sem("go_root")

        nlev = lambda j: 3 if j == 0 else 6
        lev0 = lambda j: 0 if j == 0 else 3 + 6 * (j - 1)
        tmat = lambda w, r: w[:].rearrange("p (h c) -> p h c", h=4)[0:r, :, 0:r]
        batch = lambda m, b, r: m.rearrange("p (hh b) c -> p b hh c", b=2)[0:r, b, :, 0:r]
        gate = lambda v, j, b, r: v.rearrange("p (t hh b) -> p t b hh", b=2, t=NJ)[0:r, TILES[j], b, :]
        one = lambda v, j, h, r: v[0:r, TILES[j] * HB + h:TILES[j] * HB + h + 1]

        block = phase.enter_context(nc.Block())

        @block.sync
        def _(sp):
            sp.dma_start(par[:, 0, :], a["a_log"].to_broadcast([P, HB])).then_inc(par_in, 16)
            sp.dma_start(par[:, 1, :], a["dt_bias"].to_broadcast([P, HB])).then_inc(par_in, 16)
            sp.dma_start(gain[:], a["gdn_norm"].to_broadcast([P, DK])).then_inc(par_in, 16)
            sp.dma_start(zg[:], a["z"].rearrange("t p c -> p t c")).then_inc(z_in, 16)

        @block.scalar
        def _(act):
            act.wait_ge(par_in, 48)
            act.activation(par[:, 2, :], par[:, 0, :], ACT.Exp).then_inc(g1, 1)
            act.wait_ge(g2, 1)
            act.activation(tmp, tmp, ACT.Exp, scale=-1.0)
            act.activation(beta, beta, ACT.Exp, scale=-1.0).then_inc(g3, 1)
            act.wait_ge(g3, 1)
            act.activation(tmp, tmp, ACT.Ln, bias=cst[:, C_ONE:C_ONE + 1]).then_inc(g4, 1)
            act.wait_ge(gates, 1)
            act.activation(eg, gc, ACT.Exp).then_inc(eg_done, 1)

            def prepare(j):
                r = rows(TILES[j])
                for b in range(2):
                    act.wait_ge(gl_done, 2 * j + b + 1)
                    if j >= 2:
                        act.wait_ge(s_done, j - 1)
                    last = gl[64 * b:64 * b + 64, j % 2, b, :]
                    act.activation(egs[64 * b:64 * b + 64, j % 2, :], last, ACT.Exp).then_inc(egs_done, 1)
                    act.wait_ge(d_done[b], j + 1)
                    if j >= 1:
                        act.wait_ge(nt_done[b], j)
                        act.wait_ge(decm_done[b], j)
                    act.activation(batch(dec, b, r), batch(dif, b, r), ACT.Exp).then_inc(dec_done[b], 1)
                act.wait_ge(glc_done, j + 1)
                act.activation(ekl[0:r, j % 2, :], glc[0:r, j % 2, :], ACT.Exp).then_inc(ekl_done, 1)
                act.wait_ge(kt_turned, j + 1)
                act.activation(ktok[0:r, j % 2, :], W[6][0:r, :], ACT.Copy).then_inc(kt_copied, 1)
                act.wait_ge(vt_turned, j + 1)
                act.activation(vtok[0:r, j % 2, :], W[6][0:r, :], ACT.Copy).then_inc(vt_copied, 1)
                for b in range(2):
                    act.wait_ge(t1_turned[b], j + 1)
                    act.activation(batch(tri, b, r), tmat(W[b], r), ACT.Copy).then_inc(t1_copied[b], 1)

            def level(j, lv):
                r, n = rows(TILES[j]), lev0(j) + lv
                for b in range(2):
                    act.wait_ge(x_full[b], n)
                    act.activation(batch(xm, b, r), tmat(W[b], r), ACT.Copy).then_inc(x_copied[b], 1)
                if lv < nlev(j):
                    for b in range(2):
                        act.wait_ge(r_turned[b], n - (j if j else 0))
                        act.activation(batch(inv[:, j % 2], b, r), tmat(W[b], r), ACT.Copy).then_inc(r_copied[b], 1)

            for j in range(NJ):
                prepare(j)
                for lv in range(1, nlev(j) + 1):
                    level(j, lv)
            act.wait_ge(o_sq, 1)
            act.activation(stat[:, 1, :], stat[:, 0, :], ACT.Sqrt, bias=cst[:, C_EPS:C_EPS + 1], scale=1.0 / DK).then_inc(o_root, 1)

        @block.gpsimd
        def _(pool):
            seq = Seq(pool, pool_seq)

            def prepare(j):
                r = rows(TILES[j])
                up = upper[0:r, 0:r].unsqueeze(1).to_broadcast([r, 4, r])
                idb = ident[0:r, 0:r].unsqueeze(1).to_broadcast([r, 4, r])
                for b in range(2):
                    pool.wait_ge(dec_done[b], j + 1)
                    if j >= 1:
                        pool.wait_ge(aqk_done[b], j)
                    pool.tensor_tensor(batch(decm, b, r), batch(dec, b, r), up, ALU.mult).then_inc(decm_done[b], 1)
                for b in range(2):
                    pool.wait_ge(nt_done[b], j + 1)
                    if j >= 2:
                        pool.wait_ge(o_done, j - 1)
                    m0 = cst[0:r, C_LEV:C_LEV + r].unsqueeze(1).to_broadcast([r, 4, r])
                    dst = batch(inv[:, j % 2], b, r)
                    seq(pool.tensor_tensor(dst, batch(ntm, b, r), m0, ALU.mult))
                    pool.tensor_tensor(dst, idb, dst, ALU.subtract).then_inc(r1_done[b], 1)

            def blocks(j, lv):
                r, n = rows(TILES[j]), lev0(j) + lv
                m = cst[0:r, C_LEV + 128 * lv:C_LEV + 128 * lv + r].unsqueeze(1).to_broadcast([r, 4, r])
                for b in range(2):
                    if n >= 3:
                        pool.wait_ge(x_full[b], n - 2)
                    pool.tensor_tensor(batch(bt[:, n % 2], b, r), batch(ntm, b, r), m, ALU.mult).then_inc(bt_done[b], 1)

            def recur(j):
                r = rows(TILES[j])
                if j == NJ - 1:
                    return
                pool.wait_ge(vn_done, j + 1)
                pool.wait_ge(ekl_done, j + 1)
                k = ekl[0:r, j % 2, :].unsqueeze(2).to_broadcast([r, HB, DK])
                v = lambda m: m[0:r, :].rearrange("p (h c) -> p h c", h=HB)
                if j >= 1:
                    pool.wait_ge(s_full, j)
                pool.tensor_tensor(v(v2), v(vn), k, ALU.mult).then_inc(v2_done, 1)

            for j in range(NJ + 1):
                if j < NJ:
                    prepare(j)
                    blocks(j, 1)
                    blocks(j, 2)
                if j >= 1:
                    recur(j - 1)
                if j < NJ:
                    for lv in range(3, nlev(j) + 1):
                        blocks(j, lv)

        @block.vector
        def _(dve):
            seq = Seq(dve, dve_seq)
            dve.wait_ge(par_in, 48)
            ab3 = s["ab"][:, :, 0:8]
            g3d = graw.rearrange("p (t h) -> p t h", h=HB)
            t3d = tmp.rearrange("p (t h) -> p t h", h=HB)
            seq(dve.tensor_tensor(g3d, ab3, par[:, 1, :].unsqueeze(1).to_broadcast([P, NJ, HB]), ALU.add))
            seq(dve.scalar_tensor_tensor(tmp, graw, -1.0, graw, ALU.mult, ALU.max))
            dve.tensor_copy(beta.rearrange("p (t h) -> p t h", h=HB), s["ab"][:, :, 8:16]).then_inc(g2, 1)
            dve.wait_ge(g4, 1)
            seq(dve.scalar_tensor_tensor(graw, graw, 0.0, tmp, ALU.max, ALU.add))
            dve.wait_ge(g1, 1)
            seq(dve.scalar_tensor_tensor(g3d, g3d, -1.0, par[:, 2, :].unsqueeze(1).to_broadcast([P, NJ, HB]), ALU.mult, ALU.mult))
            seq(dve.tensor_scalar(beta, beta, 1.0, None, ALU.add))
            seq(dve.reciprocal(beta, beta))
            dve.sem_inc(g2, 1)
            dve.wait_ge(gc_full, 1)
            dve.tensor_copy(gc, W[7][:, 0:G8]).then_inc(gates, 1)
            dve.wait_ge(eg_done, 1)
            seq(dve.tensor_scalar(neg, eg, -1.0, None, ALU.mult))

            def prepare(j):
                r = rows(TILES[j])
                for b in range(2):
                    dve.wait_ge(gcb_full[b], j + 1)
                    if j >= 1:
                        dve.wait_ge(dec_done[b], j)
                    for hh in range(4):
                        ins = dve.tensor_scalar(dif[0:r, 2 * hh + b, 0:r], W[4 + b][0:r, hh * 128:hh * 128 + r], one(gc, j, 2 * hh + b, r),
                                                0.0, ALU.subtract, ALU.min)
                    ins.then_inc(d_done[b], 1)
                    if j >= 2:
                        dve.wait_ge(egs_done, 2 * (j - 1))
                    dve.tensor_copy(gl[:, j % 2, b, :], W[4 + b][:].rearrange("p (h c) -> p h c", h=4)[:, :, r - 1]).then_inc(gl_done, 1)
                    dve.wait_ge(gl_done, 2 * j + b + 1)
                    dst = glc[0:r, j % 2, :].rearrange("p (hh b) -> p b hh", b=2)[:, b, :]
                    seq(dve.tensor_tensor(dst, gl[0:r, j % 2, b, :], gate(gc, j, b, r), ALU.subtract))
                dve.sem_inc(glc_done, 1)
                for b in range(2):
                    dve.wait_ge(kk_full[b], j + 1)
                    dve.wait_ge(dec_done[b], j + 1)
                    if j >= 1:
                        dve.wait_ge(bt_done[b], lev0(j))
                    for hh in range(4):
                        h = 2 * hh + b
                        ins = dve.scalar_tensor_tensor(ntm[0:r, h, 0:r], W[b][0:r, hh * 128:hh * 128 + r], one(beta, j, h, r), dec[0:r, h, 0:r],
                                                       ALU.mult, ALU.mult)
                    ins.then_inc(nt_done[b], 1)
                for b in range(2):
                    dve.wait_ge(kq_full[b], j + 1)
                    dve.wait_ge(decm_done[b], j + 1)
                    if j >= 2 and b == 0:
                        dve.wait_ge(o_done, j - 1)
                    dve.tensor_tensor(batch(aqk[:, j % 2], b, r), tmat(W[2 + b], r), batch(decm, b, r), ALU.mult).then_inc(aqk_done[b], 1)

            def level(j, lv):
                r, n = rows(TILES[j]), lev0(j) + lv
                for b in range(2):
                    dve.wait_ge(y_full[b], n)
                    if lv < nlev(j):
                        dve.tensor_tensor(batch(tri, b, r), batch(tri, b, r), tmat(W[b], r), ALU.subtract).then_inc(t_new[b], 1)
                    else:
                        dst = batch(inv[:, j % 2], b, r)
                        dve.tensor_tensor(dst, dst, tmat(W[b], r), ALU.subtract).then_inc(r_done[b], 1)

            v3 = lambda m, r: m[0:r, :].rearrange("p (h c) -> p h c", h=HB)

            def residual(j):
                r = rows(TILES[j])
                dve.wait_ge(vt_copied, j + 1)
                dve.wait_ge(ks_full, j)
                if j >= 2:
                    dve.wait_ge(v_full, j)
                for h in range(HB):
                    ins = dve.scalar_tensor_tensor(zz[0:r, h * DK:(h + 1) * DK], W[4 + h % 2][0:r, h // 2 * DK:h // 2 * DK + DK], one(neg, j, h, r),
                                                   vtok[0:r, j % 2, h * DK:(h + 1) * DK], ALU.mult, ALU.add)
                ins.then_inc(z_done, 1)

            def new_values(j):
                r = rows(TILES[j])
                dve.wait_ge(v_full, j + 1)
                if j >= 1:
                    dve.wait_ge(v2_done, j)
                    if j >= 2:
                        dve.wait_ge(o2_full, j - 1)
                bb = beta.rearrange("p (t h) -> p t h", h=HB)[0:r, TILES[j], :].unsqueeze(2).to_broadcast([r, HB, DK])
                dve.tensor_tensor(v3(vn, r), v3(W[6], r), bb, ALU.mult).then_inc(vn_done, 1)

            def update(j):
                r = rows(TILES[j])
                if j < NJ - 1:
                    dve.wait_ge(s_full, j + 1)
                    if j == 0:
                        dve.tensor_copy(state[:].rearrange("p h c -> p (h c)"), W[6][:, 0:256]).then_inc(s_done, 1)
                    else:
                        for hh in range(4):
                            ins = dve.scalar_tensor_tensor(state[:, hh, :], state[:, hh, :], egs[:, j % 2, hh:hh + 1], W[6][:, hh * DK:(hh + 1) * DK],
                                                           ALU.mult, ALU.add)
                        ins.then_inc(s_done, 1)
                if j == 0:
                    dve.sem_inc(o_done, 1)
                    return
                dve.wait_ge(o2_full, j)
                seq(dve.tensor_copy(zz[0:r, :], W[7][0:r, :]))
                for h in range(HB):
                    ins = dve.scalar_tensor_tensor(mix[:, TILES[j], 512 + h * DK:512 + (h + 1) * DK],
                                                   W[4 + h % 2][0:r, 256 + h // 2 * DK:256 + h // 2 * DK + DK], one(eg, j, h, r),
                                                   zz[0:r, h * DK:(h + 1) * DK], ALU.mult, ALU.add)
                ins.then_inc(o_done, 1)
                dve.wait_ge(o_done, j + 1)

            for j in range(NJ + 1):
                if j < NJ:
                    prepare(j)
                    level(j, 1)
                if j >= 2:
                    residual(j - 1)
                if j < NJ:
                    level(j, 2)
                if j >= 1:
                    new_values(j - 1)
                if j < NJ:
                    level(j, 3)
                if j >= 1:
                    update(j - 1)
                if j < NJ:
                    for lv in range(4, nlev(j) + 1):
                        level(j, lv)

            g = mix[:, :, 512:1024]
            gh = lambda t: mix[:, t, 512:1024].rearrange("p (h d) -> p h d", d=DK)
            seq(dve.tensor_tensor(sqg, g, g, ALU.mult))
            dve.tensor_reduce(stat[:, 0, :], sqg.rearrange("p t (h d) -> p (t h) d", d=DK), AX.X, ALU.add).then_inc(o_sq, 1)
            dve.wait_ge(z_in, 16)
            for t in range(NT):
                z = zg[:, t, :].rearrange("p (h d) -> p h d", d=DK)
                seq(dve.tensor_tensor(z, z, gain[:].unsqueeze(1).to_broadcast([P, HB, DK]), ALU.mult))
            dve.wait_ge(o_root, 1)
            seq(dve.reciprocal(stat[:, 2, :], stat[:, 1, :]))
            for t in range(NT):
                z = zg[:, t, :].rearrange("p (h d) -> p h d", d=DK)
                rr = stat[:, 2, HB * t:HB * t + HB].unsqueeze(2).to_broadcast([P, HB, DK])
                seq(dve.tensor_tensor(gh(t), gh(t), rr, ALU.mult))
                seq(dve.tensor_tensor(gh(t), gh(t), z, ALU.mult))

        @block.tensor
        def _(pe):
            pe.wait_ge(g2, 2)
            pe.matmul(W[7][:, 0:G8], upper, graw, start=True, stop=True).then_inc(gc_full, 1)

            def prepare(j):
                t = TILES[j]
                r, c = rows(t), col0(t)
                for b in range(2):
                    if j >= 1:
                        pe.wait_ge(r_done[b], j)
                    for hh in range(4):
                        kt = gk[64 * b:64 * b + 64, hh, c:c + r]
                        mm = pe.matmul(W[b][0:r, hh * 128:hh * 128 + r], kt, kt, start=True, stop=True)
                    mm.then_inc(kk_full[b], 1)
                for b in range(2):
                    if j >= 1:
                        pe.wait_ge(aqk_done[b], j)
                    for hh in range(4):
                        mm = pe.matmul(W[2 + b][0:r, hh * 128:hh * 128 + r], gk[64 * b:64 * b + 64, hh, c:c + r],
                                       gq[64 * b:64 * b + 64, hh, c:c + r], start=True, stop=True)
                    mm.then_inc(kq_full[b], 1)
                if j >= 2:
                    pe.wait_ge(o_done, j - 1)
                for b in range(2):
                    for hh in range(4):
                        g = graw[0:r, t * HB + 2 * hh + b:t * HB + 2 * hh + b + 1].to_broadcast([r, P])
                        mm = pe.matmul(W[4 + b][:, hh * 128:hh * 128 + r], g, upper[0:r, 0:r], start=True, stop=True)
                    mm.then_inc(gcb_full[b], 1)
                if j >= 2:
                    pe.wait_ge(s_done, j - 1)
                for hh in range(4):
                    mm = pe.transpose(W[6][0:r, hh * 128:(hh + 1) * 128], gk[:, hh, c:c + r], ident)
                mm.then_inc(kt_turned, 1)
                pe.wait_ge(kt_copied, j + 1)
                for hh in range(4):
                    mm = pe.transpose(W[6][0:r, hh * 128:(hh + 1) * 128], gv[:, hh, c:c + r], ident)
                mm.then_inc(vt_turned, 1)
                for b in range(2):
                    pe.wait_ge(r1_done[b], j + 1)
                    for hh in range(4):
                        mm = pe.transpose(W[b][0:r, hh * 128:hh * 128 + r], inv[0:r, j % 2, 2 * hh + b, 0:r], ident[0:r, 0:r])
                    mm.then_inc(t1_turned[b], 1)

            def level(j, lv):
                r, n = rows(TILES[j]), lev0(j) + lv
                last = lv == nlev(j)
                for b in range(2):
                    pe.wait_ge(bt_done[b], n)
                    if lv == 1:
                        pe.wait_ge(t1_copied[b], j + 1)
                    else:
                        pe.wait_ge(r_copied[b], n - 1 - (j if j else 0))
                    for hh in range(4):
                        h = 2 * hh + b
                        mm = pe.matmul(W[b][0:r, hh * 128:hh * 128 + r], bt[0:r, n % 2, h, 0:r], tri[0:r, h, 0:r], start=True, stop=True)
                    mm.then_inc(x_full[b], 1)
                for b in range(2):
                    pe.wait_ge(x_copied[b], n)
                    for hh in range(4):
                        h = 2 * hh + b
                        m0, m1 = (xm[0:r, h, 0:r], inv[0:r, j % 2, h, 0:r]) if last else (inv[0:r, j % 2, h, 0:r], xm[0:r, h, 0:r])
                        mm = pe.matmul(W[b][0:r, hh * 128:hh * 128 + r], m0, m1, start=True, stop=True)
                    mm.then_inc(y_full[b], 1)
                if not last:
                    for b in range(2):
                        pe.wait_ge(t_new[b], n - (j if j else 0))
                        for hh in range(4):
                            mm = pe.transpose(W[b][0:r, hh * 128:hh * 128 + r], tri[0:r, 2 * hh + b, 0:r], ident[0:r, 0:r])
                        mm.then_inc(r_turned[b], 1)

            def from_state(j):
                t = TILES[j]
                r, c = rows(t), col0(t)
                pe.wait_ge(s_done, j)
                if j + 1 < NJ:
                    pe.wait_ge(glc_done, j + 2)
                for src, o in ((gk, 0), (gq, 256)):
                    for hh in range(4):
                        for b in range(2):
                            mm = pe.matmul(W[4 + b][0:r, o + hh * DK:o + (hh + 1) * DK], src[64 * b:64 * b + 64, hh, c:c + r],
                                           state[64 * b:64 * b + 64, hh, :], start=True, stop=True)
                mm.then_inc(ks_full, 1)

            def solve(j):
                r = rows(TILES[j])
                if j >= 1:
                    pe.wait_ge(z_done, j)
                for b in range(2):
                    pe.wait_ge(r_done[b], j + 1)
                pe.wait_ge(vt_copied, min(j + 2, NJ))
                for h in range(HB):
                    z = vtok[0:r, 0, h * DK:(h + 1) * DK] if j == 0 else zz[0:r, h * DK:(h + 1) * DK]
                    mm = pe.matmul(W[6][0:r, h * DK:(h + 1) * DK], inv[0:r, j % 2, h, 0:r], z, start=True, stop=True)
                mm.then_inc(v_full, 1)

            def carry(j):
                r = rows(TILES[j])
                pe.wait_ge(vn_done, j + 1)
                if j >= 1:
                    for b in range(2):
                        pe.wait_ge(aqk_done[b], j + 1)
                    if j >= 2:
                        pe.wait_ge(o_done, j)
                    for h in range(HB):
                        mm = pe.matmul(W[7][0:r, h * DK:(h + 1) * DK], aqk[0:r, j % 2, h, 0:r], vn[0:r, h * DK:(h + 1) * DK], start=True, stop=True)
                    mm.then_inc(o2_full, 1)
                if j < NJ - 1:
                    pe.wait_ge(v2_done, j + 1)
                    for hh in range(4):
                        for b in range(2):
                            h = 2 * hh + b
                            mm = pe.matmul(W[6][64 * b:64 * b + 64, hh * DK:(hh + 1) * DK], ktok[0:r, j % 2, h * DK:(h + 1) * DK],
                                           v2[0:r, h * DK:(h + 1) * DK], start=True, stop=True)
                    mm.then_inc(s_full, 1)

            for j in range(NJ + 1):
                if j < NJ:
                    prepare(j)
                    level(j, 1)
                if j >= 2:
                    from_state(j - 1)
                if j < NJ:
                    level(j, 2)
                if j >= 1:
                    solve(j - 1)
                if j < NJ:
                    level(j, 3)
                if j >= 1:
                    carry(j - 1)
                if j < NJ:
                    for lv in range(4, nlev(j) + 1):
                        level(j, lv)

        phase.close()
        clear(nc, sems)


def output_and_route(nc, a, s):
    with ExitStack() as ctx, ExitStack() as phase:
        sb = lambda n, sh, dt=F32: ctx.enter_context(nc.sbuf_tensor(n, sh, dt))
        ps = lambda n, sh, dt=F32: ctx.enter_context(nc.psum_tensor(n, sh, dt))
        sems = []

        def sem(n):
            sems.append(ctx.enter_context(nc.semaphore(n)))
            return sems[-1]

        cst, mix, hres = s["cst"], s["mix"], s["hres"]
        ident = cst[:, C_ID:C_ID + 128]
        wout = s["gqkv"][:].rearrange("p m l -> p (m l)")[:, 0:KD * D].rearrange("p (k c) -> p k c", k=KD)
        mixT = sb("mixT", [P, 2, KD, P])
        uT = sb("u2T", [P, 2, KD, P])
        xr = sb("xr", [P, 2, D])
        u2 = sb("u2", [P, 2, D])
        scr = sb("scr", [P, D])
        gain = sb("ffn_gain", [P, D])
        wr = sb("wr", [P, KD, 36])
        rb = sb("rb", [P, 36])
        ss = sb("ss2", [P, NT, 3])
        lg = sb("lg", [P, NT, 36])
        big = lambda n: sb(n, [P, NT, NE])
        em, t1, t2, oh1, oh2, msum, mcum = (big(x) for x in ("em", "t1", "t2", "oh1", "oh2", "msum", "mcum"))
        sm = sb("sm", [P, 12, NT])
        g4, e4, goh = (sb(x, [P, NT, NG]) for x in ("g4", "e4", "goh"))
        tot = sb("tot", [P, NE])
        cmpn, ovc = sb("cmpn", [NE, 7]), sb("ovc", [NE, 1])
        base2, ovi = sb("base2", [P, NE]), sb("ovi", [P, NE])
        eob = sb("eob", [P, 16, NE])
        tabf = sb("tabf", [P, MAXBLK + 1])
        slf = sb("slf", [P, NT, 2])
        pmi, bmi = sb("pmi", [P, NT, 2], I32), sb("bmi", [P, NT, 2], I32)
        pmf, bmf = sb("pmf", [P, NT, 2]), sb("bmf", [P, NT, 2])
        ohp = mix[:, 0:2, :].rearrange("p t c -> p (t c)").rearrange("p (n s) -> p n s", s=P)
        ohb = mix[:, 2, 0:2 * NT * MAXBLK].rearrange("p (n s) -> p n s", s=MAXBLK)

        T, O, U = ([ps(f"{x}{i}", [P, 512]) for i in range(2)] for x in ("mT", "mO", "mU"))
        LGP, MISC = ps("LGP", [P, 512]), ps("MISC", [P, 512])
        w_in, x_in, gain_in, act_seq, dve_seq = sem("wo_in"), [sem(f"xr_in{i}") for i in range(2)], sem("gain_in"), sem("ract_seq"), sem("rdve_seq")
        m_turned, m_copied, o_full, h_done, sq_done, root, u_done, u_out = (
            sem(x) for x in ("m_turned", "m_copied", "o_full", "h_done", "sq2", "root2", "u_done", "u_out"))
        u_turned, uT_copied, lg_full, lg_done = (sem(x) for x in ("u_turned", "uT_copied", "lg_full", "lg_done"))
        ex_in, ex_done, p2_in, p2_done, m_done, rank_full, ovc_done, ov_full, oh_done, idx_full = (
            sem(x) for x in ("ex_in", "ex_done", "p2_in", "p2_done", "m_done", "rank_full", "ovc_done", "ov_full", "oh_done", "idx_full"))
        u_outs = [u_out, sem("u_out1")]

        block = phase.enter_context(nc.Block())

        @block.sync
        def _(sp):
            sp.dma_start(wout, a["w_out"].rearrange("o (k p) c -> (o p) k c", p=P)).then_inc(w_in, 16)
            for t in range(NT):
                if t >= 2:
                    sp.wait_ge(h_done, 2 * (t - 1))
                sp.dma_start(xr[:, t % 2, :], a["x"][0, t * P:(t + 1) * P, :]).then_inc(x_in[t % 2], 16)
                if t == 1:
                    sp.dma_start(gain[:], a["norm_ffn"].to_broadcast([P, D])).then_inc(gain_in, 16)
                    with nc.allow_non_contiguous_dma(reason="router columns, 16 and 128 bytes a row"):
                        sp.dma_start(wr[:, :, 0:4], a["w_group"].rearrange("o (k p) c -> (o p) k c", p=P)).then_inc(gain_in, 16)
                        sp.dma_start(wr[:, :, 4:36], a["w_router"].rearrange("o (k p) c -> (o p) k c", p=P)).then_inc(gain_in, 16)
                    sp.dma_start(rb[:, 0:4], a["b_group"].to_broadcast([P, 4])).then_inc(gain_in, 16)
                    sp.dma_start(rb[:, 4:36], a["b_router"].to_broadcast([P, 32])).then_inc(gain_in, 16)
                if t >= 1:
                    sp.wait_ge(u_done, t)
                    sp.dma_start(a["u2"][(t - 1) * P:t * P, :], u2[:, (t - 1) % 2, :]).then_inc(u_outs[(t - 1) % 2], 16)
            sp.wait_ge(u_done, NT)
            sp.dma_start(a["u2"][(NT - 1) * P:NT * P, :], u2[:, (NT - 1) % 2, :]).then_inc(u_outs[(NT - 1) % 2], 16)
            for b in range(2):
                sp.wait_ge(u_outs[b], 16 * NT // 2)

        @block.scalar
        def _(act):
            def turned_mix(t):
                for half in range(2):
                    act.wait_ge(m_turned, 2 * t + half + 1)
                    if t >= 2:
                        act.wait_ge(o_full, 2 * (t - 1))
                    act.activation(mixT[:, t % 2, 4 * half:4 * half + 4, :], T[half][:], ACT.Copy).then_inc(m_copied, 1)

            def statistics(t):
                act.wait_ge(h_done, 2 * t + 2)
                if t >= 1:
                    act.wait_ge(sq_done, t)
                act.activation(scr[:], hres[:, t, :], ACT.Square, accum_out=ss[:, t, 0:1]).then_inc(sq_done, 1)
                act.wait_ge(sq_done, t + 1)
                act.activation(ss[:, t, 1:2], ss[:, t, 0:1], ACT.Sqrt, bias=cst[:, C_EPS:C_EPS + 1], scale=1.0 / D).then_inc(root, 1)

            def turned_u(t):
                for half in range(2):
                    act.wait_ge(u_turned, 2 * t + half + 1)
                    if t >= 2:
                        act.wait_ge(lg_full, t - 1)
                    act.activation(uT[:, t % 2, 4 * half:4 * half + 4, :], U[half][:], ACT.Copy).then_inc(uT_copied, 1)

            act.wait_ge(gain_in, 80)
            for t in range(NT + 1):
                if t < NT:
                    turned_mix(t)
                if t >= 1:
                    turned_u(t - 1)
                if t < NT:
                    statistics(t)
            act.wait_ge(ex_in, 1)
            act.activation(e4[:], e4[:], ACT.Exp).then_inc(ex_done, 1)
            act.wait_ge(p2_in, 1)
            act.activation(sm[:, 8, :], sm[:, 8, :], ACT.Exp).then_inc(p2_done, 1)

        @block.vector
        def _(dve):
            seq = Seq(dve, dve_seq)

            def logits(t):
                dve.wait_ge(lg_full, t + 1)
                dve.tensor_tensor(lg[:, t, :], LGP[:, 0:36], rb[:], ALU.add).then_inc(lg_done, 1)

            seq(dve.memset(s["idx"][:], -1))
            dve.wait_ge(gain_in, 80)
            for t in range(NT):
                dve.wait_ge(x_in[t % 2], 16 * (t // 2 + 1))
                for half in range(2):
                    dve.wait_ge(o_full, 2 * t + half + 1)
                    c = slice(512 * half, 512 * half + 512)
                    dve.tensor_tensor(hres[:, t, c], O[half][:], xr[:, t % 2, c], ALU.add).then_inc(h_done, 1)
                dve.wait_ge(root, t + 1)
                seq(dve.reciprocal(ss[:, t, 2:3], ss[:, t, 1:2]))
                if t >= 2:
                    dve.wait_ge(u_outs[t % 2], 16 * (t // 2))
                    dve.wait_ge(u_turned, 2 * (t - 1))
                dve.scalar_tensor_tensor(u2[:, t % 2, :], hres[:, t, :], ss[:, t, 2:3], gain[:], ALU.mult, ALU.mult).then_inc(u_done, 1)
                if t >= 1:
                    logits(t - 1)
            logits(NT - 1)
            dve.wait_ge(lg_done, NT)

            bc = lambda v, n: v.unsqueeze(2).to_broadcast([P, NT, n])
            row = lambda c, n: cst[:, c:c + n].unsqueeze(1).to_broadcast([P, NT, n])
            m = lambda i: sm[:, i, :]

            def first_max(values, n, top, onehot, work):
                seq(dve.tensor_reduce(top, values, AX.X, ALU.max))
                seq(dve.tensor_tensor(work, values, bc(top, n), ALU.is_equal))
                seq(dve.tensor_tensor(work, work, row(C_IG, n), ALU.mult))
                seq(dve.tensor_reduce(m(11), work, AX.X, ALU.min))
                seq(dve.tensor_tensor(onehot, row(C_IG, n), bc(m(11), n), ALU.is_equal))

            first_max(lg[:, :, 0:NG], NG, m(0), goh[:], g4[:])
            dve.tensor_tensor(e4[:], lg[:, :, 0:NG], bc(m(0), NG), ALU.subtract).then_inc(ex_in, 1)
            seq(dve.tensor_scalar(g4[:], goh[:], BIG, -BIG, ALU.mult, ALU.add))
            groups = lambda v: v.rearrange("p t (g e) -> p (t g) e", g=NG)
            wide = lambda v: v[:].rearrange("p t g -> p (t g)").unsqueeze(2).to_broadcast([P, NT * NG, EPG])
            seq(dve.tensor_copy(em[:], lg[:, :, NG:NG + NE]))
            seq(dve.tensor_tensor(groups(em[:]), groups(em[:]), wide(goh), ALU.mult))
            seq(dve.tensor_tensor(groups(em[:]), groups(em[:]), wide(g4), ALU.add))
            first_max(em[:], NE, m(1), oh1[:], t1[:])
            seq(dve.scalar_tensor_tensor(em[:], oh1[:], -2.0 * BIG, em[:], ALU.mult, ALU.add))
            first_max(em[:], NE, m(2), oh2[:], t1[:])
            dve.tensor_tensor(m(8), m(2), m(1), ALU.subtract).then_inc(p2_in, 1)
            dve.wait_ge(ex_done, 1)
            seq(dve.tensor_reduce(m(3), e4[:], AX.X, ALU.add))
            seq(dve.reciprocal(m(4), m(3)))
            dve.wait_ge(p2_done, 1)
            seq(dve.tensor_scalar(m(5), m(8), 1.0, None, ALU.add))
            seq(dve.reciprocal(m(6), m(5)))
            seq(dve.tensor_tensor(s["wts"][:, 0, :], m(4), m(6), ALU.mult))
            seq(dve.tensor_tensor(s["wts"][:, 1, :], s["wts"][:, 0, :], m(8), ALU.mult))
            seq(dve.tensor_tensor(msum[:], oh1[:], oh2[:], ALU.add))
            seq(dve.memset(mcum[:, 0, :], 0.0))
            for t in range(1, NT):
                seq(dve.tensor_tensor(mcum[:, t, :], mcum[:, t - 1, :], msum[:, t - 1, :], ALU.add))
            dve.tensor_tensor(tot[:], mcum[:, NT - 1, :], msum[:, NT - 1, :], ALU.add).then_inc(m_done, 1)
            dve.wait_ge(rank_full, 1)
            seq(dve.tensor_tensor(cmpn[:], T[1][0:NE, 0:1].to_broadcast([NE, 7]), cst[0:NE, C_E128 + 1:C_E128 + 8], ALU.is_gt))
            dve.tensor_reduce(ovc[:], cmpn[:], AX.X, ALU.add).then_inc(ovc_done, 1)
            rank = t1[:]
            seq(dve.tensor_copy(rank, T[0][:, 0:NT * NE].rearrange("p (t e) -> p t e", t=NT)))
            dve.wait_ge(ov_full, 1)
            seq(dve.tensor_scalar(base2[:], O[0][:, 0:NE], 128.0, 31.0 * 128.0, ALU.mult, ALU.add))
            seq(dve.tensor_tensor(base2[:], base2[:], cst[:, C_E128:C_E128 + NE], ALU.subtract))
            seq(dve.tensor_copy(ovi[:], O[0][:, NE:2 * NE]))
            seq(dve.tensor_scalar(t2[:], rank, 128.0, None, ALU.is_ge))
            seq(dve.tensor_tensor(t2[:], t2[:], base2[:].unsqueeze(1).to_broadcast([P, NT, NE]), ALU.mult))
            seq(dve.tensor_tensor(t2[:], t2[:], rank, ALU.add))
            seq(dve.tensor_tensor(t2[:], t2[:], row(C_E128, NE), ALU.add))
            for c, oh in enumerate((oh1, oh2)):
                seq(dve.tensor_tensor(em[:], t2[:], oh[:], ALU.mult))
                seq(dve.tensor_reduce(slf[:, :, c], em[:], AX.X, ALU.add))
            seq(dve.tensor_copy(s["slot"][:], slf[:]))
            seq(dve.tensor_scalar(pmi[:], s["slot"][:], 127, None, ALU.bitwise_and))
            seq(dve.tensor_scalar(bmi[:], s["slot"][:], 7, None, ALU.arith_shift_right))
            seq(dve.tensor_copy(pmf[:], pmi[:]))
            seq(dve.tensor_copy(bmf[:], bmi[:]))
            for t in range(NT):
                for c in range(2):
                    seq(dve.tensor_scalar(ohp[:, 2 * t + c, :], cst[:, C_IOTA:C_IOTA + P], pmf[:, t, c:c + 1], None, ALU.is_equal))
                    seq(dve.tensor_scalar(ohb[:, 2 * t + c, :], cst[:, C_IOTA:C_IOTA + MAXBLK], bmf[:, t, c:c + 1],
                                          cst[:, C_TOK + 2 * t + c:C_TOK + 2 * t + c + 1], ALU.is_equal, ALU.mult))
            dve.sem_inc(oh_done, 1)
            io = cst[:, C_IOTA:C_IOTA + 16].unsqueeze(2).to_broadcast([P, 16, NE])
            seq(dve.tensor_tensor(eob[:], ovi[:].unsqueeze(1).to_broadcast([P, 16, NE]), io, ALU.is_le))
            seq(dve.tensor_copy(tabf[:, 0:32], cst[:, C_IOTA:C_IOTA + 32]))
            seq(dve.tensor_reduce(tabf[:, 32:48], eob[:], AX.X, ALU.add))
            seq(dve.tensor_scalar(tabf[:, 32:48], tabf[:, 32:48], 31.0, None, ALU.min))
            seq(dve.tensor_scalar(tabf[:, 48:49], ovi[:, NE - 1:NE], 33.0, None, ALU.add))
            seq(dve.tensor_copy(s["table"][:], tabf[:]))
            seq(dve.tensor_scalar(s["table"][:, 48:49], s["table"][:, 48:49], 1, None, ALU.arith_shift_right))
            dve.wait_ge(idx_full, 1)
            seq(dve.tensor_scalar(tabf[:, 0:MAXBLK], U[0][:, 0:MAXBLK], -1.0, None, ALU.add))
            seq(dve.tensor_copy(s["idx"][:, 0, 0:MAXBLK], tabf[:, 0:MAXBLK]))
            seq(dve.tensor_scalar(s["idx"][:, 1, :], s["idx"][:, 0, :], 1, None, ALU.arith_shift_right))

        @block.tensor
        def _(pe):
            def turn_mix(t):
                for half in range(2):
                    if t >= 1:
                        pe.wait_ge(m_copied, 2 * t - 1 + half)
                    for kk in range(4):
                        kx = 4 * half + kk
                        mm = pe.transpose(T[half][:, kk * P:(kk + 1) * P], mix[:, t, kx * P:(kx + 1) * P], ident)
                    mm.then_inc(m_turned, 1)

            def out_proj(t):
                pe.wait_ge(m_copied, 2 * t + 2)
                for half in range(2):
                    if t >= 1:
                        pe.wait_ge(h_done, 2 * t - 1 + half)
                    for kx in range(KD):
                        mm = pe.matmul(O[half][:], mixT[:, t % 2, kx, :], wout[:, kx, 512 * half:512 * half + 512], start=kx == 0, stop=kx == KD - 1)
                    mm.then_inc(o_full, 1)

            def turn_u(t):
                pe.wait_ge(u_done, t + 1)
                for half in range(2):
                    if t >= 1:
                        pe.wait_ge(uT_copied, 2 * t - 1 + half)
                    for kk in range(4):
                        kx = 4 * half + kk
                        mm = pe.transpose(U[half][:, kk * P:(kk + 1) * P], u2[:, t % 2, kx * P:(kx + 1) * P], ident)
                    mm.then_inc(u_turned, 1)

            def router(t):
                pe.wait_ge(uT_copied, 2 * t + 2)
                if t >= 1:
                    pe.wait_ge(lg_done, t)
                for kx in range(KD):
                    mm = pe.matmul(LGP[:, 0:36], uT[:, t % 2, kx, :], wr[:, kx, :], start=kx == 0, stop=kx == KD - 1)
                mm.then_inc(lg_full, 1)

            turn_mix(0)
            pe.wait_ge(w_in, 16)
            pe.wait_ge(gain_in, 80)
            for t in range(NT + 1):
                if t + 1 < NT:
                    turn_mix(t + 1)
                if t < NT:
                    out_proj(t)
                if t >= 1:
                    turn_u(t - 1)
                    router(t - 1)
            pe.wait_ge(m_done, 1)
            pe.wait_ge(m_copied, 2 * NT)
            ones = cst[:, C_ONE:C_ONE + P]
            pe.matmul(T[0][:, 0:NT * NE], cst[:, C_SUP:C_SUP + P], msum[:].rearrange("p t e -> p (t e)"), start=True, stop=False)
            pe.matmul(T[0][:, 0:NT * NE], ones, mcum[:].rearrange("p t e -> p (t e)"), start=False, stop=True)
            pe.matmul(T[1][0:NE, 0:1], tot[:], cst[:, C_ONE:C_ONE + 1], start=True, stop=True).then_inc(rank_full, 1)
            pe.wait_ge(ovc_done, 1)
            lhs = ovc[:].to_broadcast([NE, P])
            pe.matmul(O[0][:, 0:NE], lhs, cst[0:NE, C_SUP:C_SUP + NE], start=True, stop=True)
            pe.matmul(O[0][:, NE:2 * NE], lhs, cst[0:NE, C_UP:C_UP + NE], start=True, stop=True).then_inc(ov_full, 1)
            pe.wait_ge(oh_done, 1)
            for n in range(2 * NT):
                mm = pe.matmul(U[0][:, 0:MAXBLK], ohp[:, n, :], ohb[:, n, :], start=n == 0, stop=n == 2 * NT - 1)
            mm.then_inc(idx_full, 1)

        phase.close()
        clear(nc, sems)


def experts(nc, a, s):
    with ExitStack() as ctx, ExitStack() as phase:
        sb = lambda n, sh, dt=F32: ctx.enter_context(nc.sbuf_tensor(n, sh, dt))
        ps = lambda n, sh, dt=F32: ctx.enter_context(nc.psum_tensor(n, sh, dt))
        sems = []

        def sem(n):
            sems.append(ctx.enter_context(nc.semaphore(n)))
            return sems[-1]

        sem2 = lambda n: [sem(f"{n}{b}") for b in range(2)]
        ident = s["cst"][:, C_ID:C_ID + 128]
        gqkv, mixf = s["gqkv"][:].rearrange("p m l -> p (m l)"), s["mix"][:].rearrange("p t c -> p (t c)")
        NW = KD * 2 * FE + 2 * D
        store = [gqkv[:, 0:NW], gqkv[:, NW:2 * NW]]
        gu = [w[:, 0:KD * 2 * FE].rearrange("p (k g f) -> p k g f", k=KD, g=2) for w in store]
        down = [w[:, KD * 2 * FE:].rearrange("p (k c) -> p k c", k=2) for w in store]
        xg, xT, yb = sb("xg", [P, 2, D]), sb("xT", [P, 2, KD, P]), sb("yb", [P, 2, D])
        sg, hb, hT = sb("sg", [P, 2, FE]), sb("hb", [P, 2, FE]), sb("hT", [P, 2, 2, P])
        cur = sb("cur", [P, 2, 2], I32)
        XY = [[ps(f"XY{u}{half}", [P, 512]) for half in range(2)] for u in range(2)]
        GU = [ps(f"GU{u}", [P, 512]) for u in range(2)]
        HT = [ps(f"HT{u}", [P, 512]) for u in range(2)]
        w_in, d_in, cur_done, x_in, x_turned, xT_act, xT_dve, gu_full, silu_done, h_done, h_turned, hT_done, y_full, y_act, y_dve, y_out = (
            sem2(x) for x in ("ew_in", "ed_in", "cur_done", "ex_in_", "ex_turned", "xT_act", "xT_dve", "gu_full", "esilu", "eh_done",
                              "eh_turned", "ehT_done", "ey_full", "ey_act", "ey_dve", "ey_out"))
        wait = lambda eng, x, v: None if isinstance(v, int) and v == 0 else eng.wait_ge(x, v)
        go_pool, x_clear, cur2_done = sem("go_pool"), sem("x_clear"), sem2("cur2_done")
        gate_v = a["w_gate"].rearrange("o e (p k) f -> (o e) p k f", k=KD)
        up_v = a["w_up"].rearrange("o e (p k) f -> (o e) p k f", k=KD)
        down_v = a["w_down"].rearrange("o e (p k) c -> (o e) p k c", k=2)
        pairs = lambda eng: eng.value_load(s["table"][0:1, 48:49], min_val=16, max_val=24)

        block = phase.enter_context(nc.Block())

        @block.sync
        def _(sp):
            def turn(i):
                experts_of = range(2) if isinstance(i, int) else [
                    sp.value_load(s["table"][0:1, bass.ds(2 * i + u, 1)], min_val=0, max_val=NE - 1) for u in range(2)]
                for u, e in enumerate(experts_of):
                    wait(sp, gu_full[u], i)
                    sp.dma_start(gu[u][:, :, 0, :], gate_v[bass.ds(e, 1)].rearrange("o p k f -> (o p) k f")).then_inc(w_in[u], 16)
                    sp.dma_start(gu[u][:, :, 1, :], up_v[bass.ds(e, 1)].rearrange("o p k f -> (o p) k f")).then_inc(w_in[u], 16)
                for u, e in enumerate(experts_of):
                    wait(sp, y_full[u], 2 * i)
                    sp.dma_start(down[u], down_v[bass.ds(e, 1)].rearrange("o p k c -> (o p) k c")).then_inc(d_in[u], 16)

            turn(0)
            with sp.Fori(1, pairs(sp)) as i:
                turn(i)

        @block.gpsimd
        def _(pool):
            rows_of = lambda u, c: bass.IndirectOffsetOnAxis(ap=cur[:, u, c:c + 1].bitcast(U32), axis=0)

            def gather(i, j):
                for u in range(2):
                    wait(pool, x_in[u], 16 * i)
                    pool.tensor_copy(cur[:, u, 0:1], s["idx"][:, 1, bass.ds(2 * j + u, 1)]).then_inc(cur_done[u], 1)
                    pool.wait_ge(cur_done[u], j + 1)
                    wait(pool, x_turned[u], 2 * i)
                    pool.sem_inc(go_pool, 1)
                    pool.indirect_dma_start(out=xg[:, u, :], out_offset=None, in_=a["u2"], in_offset=rows_of(u, 0),
                                            bounds_check=SEQ - 1, oob_is_err=False).then_inc(x_in[u], 16)

            def scatter(i):
                for u in range(2):
                    wait(pool, y_out[u], 16 * i)
                    pool.tensor_copy(cur[:, u, 1:2], s["idx"][:, 0, bass.ds(2 * i + u, 1)]).then_inc(cur2_done[u], 1)
                    pool.wait_ge(cur2_done[u], i + 1)
                    pool.wait_ge(y_act[u], i + 1)
                    pool.wait_ge(y_dve[u], i + 1)
                    pool.sem_inc(go_pool, 1)
                    pool.indirect_dma_start(out=a["ys"], out_offset=rows_of(u, 1), in_=yb[:, u, :], in_offset=None,
                                            bounds_check=2 * SEQ - 1, oob_is_err=False).then_inc(y_out[u], 16)

            pool.wait_ge(x_clear, 1)
            gather(0, 0)
            gather(1, 1)
            scatter(0)
            n = pairs(pool)
            with pool.Fori(1, n) as i:
                gather(i + 1, i + 1)
                scatter(i)
            for u in range(2):
                pool.wait_ge(y_out[u], 16 * n)
                pool.wait_ge(x_in[u], 16 * n + 16)
            pool.sem_inc(go_pool, 1)

        @block.scalar
        def _(act):
            def turn(i):
                for u in range(2):
                    act.wait_ge(x_turned[u], 2 * i + 1)
                    act.activation(xT[:, u, 0:4, :], XY[u][0][:], ACT.Copy).then_inc(xT_act[u], 1)
                for u in range(2):
                    act.wait_ge(gu_full[u], i + 1)
                    act.activation(sg[:, u, :], GU[u][:, 0:FE], ACT.Silu).then_inc(silu_done[u], 1)
                for u in range(2):
                    act.wait_ge(h_turned[u], i + 1)
                    act.activation(hT[:, u], HT[u][:, 0:2 * P], ACT.Copy).then_inc(hT_done[u], 1)
                for u in range(2):
                    act.wait_ge(y_full[u], 2 * i + 1)
                    wait(act, y_out[u], 16 * i)
                    act.activation(yb[:, u, 0:512], XY[u][0][:], ACT.Copy).then_inc(y_act[u], 1)

            turn(0)
            with act.Fori(1, pairs(act)) as i:
                turn(i)

        @block.vector
        def _(dve):
            dve.memset(xg[:], 0.0).then_inc(x_clear, 1)
            def turn(i):
                for u in range(2):
                    dve.wait_ge(x_turned[u], 2 * i + 2)
                    dve.tensor_copy(xT[:, u, 4:8, :], XY[u][1][:].rearrange("p (k t) -> p k t", k=4)).then_inc(xT_dve[u], 1)
                for u in range(2):
                    dve.wait_ge(silu_done[u], i + 1)
                    dve.tensor_tensor(hb[:, u, :], GU[u][:, FE:2 * FE], sg[:, u, :], ALU.mult).then_inc(h_done[u], 1)
                for u in range(2):
                    dve.wait_ge(y_full[u], 2 * i + 2)
                    wait(dve, y_out[u], 16 * i)
                    dve.tensor_copy(yb[:, u, 512:1024], XY[u][1][:]).then_inc(y_dve[u], 1)

            turn(0)
            with dve.Fori(1, pairs(dve)) as i:
                turn(i)

        @block.tensor
        def _(pe):
            def turn(i):
                for u in range(2):
                    pe.wait_ge(x_in[u], 16 * i + 16)
                    for half in range(2):
                        wait(pe, (y_act if half == 0 else y_dve)[u], i)
                        for kk in range(4):
                            kx = 4 * half + kk
                            mm = pe.transpose(XY[u][half][:, kk * P:(kk + 1) * P], xg[:, u, kx:D:KD], ident)
                        mm.then_inc(x_turned[u], 1)
                for u in range(2):
                    pe.wait_ge(w_in[u], 32 * i + 32)
                    pe.wait_ge(xT_act[u], i + 1)
                    pe.wait_ge(xT_dve[u], i + 1)
                    wait(pe, h_done[u], i)
                    for kx in range(KD):
                        mm = pe.matmul(GU[u][:], xT[:, u, kx, :], gu[u][:, kx, :, :], start=kx == 0, stop=kx == KD - 1)
                    mm.then_inc(gu_full[u], 1)
                for u in range(2):
                    pe.wait_ge(h_done[u], i + 1)
                    wait(pe, hT_done[u], i)
                    for kx in range(2):
                        mm = pe.transpose(HT[u][:, kx * P:(kx + 1) * P], hb[:, u, kx:FE:2], ident)
                    mm.then_inc(h_turned[u], 1)
                for u in range(2):
                    pe.wait_ge(hT_done[u], i + 1)
                    pe.wait_ge(d_in[u], 16 * i + 16)
                    for half in range(2):
                        for kx in range(2):
                            mm = pe.matmul(XY[u][half][:], hT[:, u, kx, :], down[u][:, kx, 512 * half:512 * half + 512], start=kx == 0, stop=kx == 1)
                        mm.then_inc(y_full[u], 1)

            turn(0)
            with pe.Fori(1, pairs(pe)) as i:
                turn(i)

        phase.close()
        clear(nc, sems)


def combine(nc, a, s):
    with ExitStack() as ctx:
        sb = lambda n, sh, dt=F32: ctx.enter_context(nc.sbuf_tensor(n, sh, dt))
        sem = lambda n: ctx.enter_context(nc.semaphore(n))
        RB = 3
        cst, hres = s["cst"], s["hres"]
        y = sb("yc", [P, RB, 2, D])
        ob = sb("ob", [P, 2, D])
        scr, gain, ss = sb("cscr", [P, D]), sb("fgain", [P, D]), sb("ss3", [P, NT, 3])
        gain_in, seq_s, sq, root = sem("fgain_in"), sem("cseq"), sem("csq"), sem("croot")
        y_in, added, o_done, o_out = [sem(f"y_in{b}") for b in range(RB)], sem("cadded"), sem("co_done"), [sem(f"co_out{b}") for b in range(2)]

        block = ctx.enter_context(nc.Block())

        @block.sync
        def _(sp):
            sp.dma_start(gain[:], a["norm_final"].rearrange("(o d) -> o d", o=1).to_broadcast([P, D])).then_inc(gain_in, 16)
            def put(t):
                sp.wait_ge(o_done, t + 1)
                sp.dma_start(a["out"][0, t * P:(t + 1) * P, :], ob[:, t % 2, :]).then_inc(o_out[t % 2], 16)

            for t in range(NT):
                if t >= RB:
                    sp.wait_ge(added, t - RB + 1)
                sp.dma_start(y[:, t % RB, :, :], a["ys"].rearrange("(t p c) d -> t p c d", c=2, p=P)[t]).then_inc(y_in[t % RB], 16)
                if t < RB - 1:
                    continue
                put(t - RB + 1)
            for t in range(NT - RB + 1, NT):
                put(t)
            for b in range(2):
                sp.wait_ge(o_out[b], 16 * NT // 2)

        @block.scalar
        def _(act):
            for t in range(NT):
                act.wait_ge(added, t + 1)
                if t >= 1:
                    act.wait_ge(sq, t)
                act.activation(scr[:], hres[:, t, :], ACT.Square, accum_out=ss[:, t, 0:1]).then_inc(sq, 1)
                act.wait_ge(sq, t + 1)
                act.activation(ss[:, t, 1:2], ss[:, t, 0:1], ACT.Sqrt, bias=cst[:, C_EPS:C_EPS + 1], scale=1.0 / D).then_inc(root, 1)

        @block.vector
        def _(dve):
            seq = Seq(dve, seq_s)

            def finish(t):
                dve.wait_ge(root, t + 1)
                seq(dve.reciprocal(ss[:, t, 2:3], ss[:, t, 1:2]))
                if t >= 2:
                    dve.wait_ge(o_out[t % 2], 16 * (t // 2))
                dve.scalar_tensor_tensor(ob[:, t % 2, :], hres[:, t, :], ss[:, t, 2:3], gain[:], ALU.mult, ALU.mult).then_inc(o_done, 1)

            dve.wait_ge(gain_in, 16)
            for t in range(NT):
                dve.wait_ge(y_in[t % RB], 16 * (t // RB + 1))
                h = hres[:, t, :]
                seq(dve.scalar_tensor_tensor(h, y[:, t % RB, 0, :], s["wts"][:, 0, t:t + 1], h, ALU.mult, ALU.add))
                dve.scalar_tensor_tensor(h, y[:, t % RB, 1, :], s["wts"][:, 1, t:t + 1], h, ALU.mult, ALU.add).then_inc(added, 1)
                if t >= 1:
                    finish(t - 1)
            finish(NT - 1)


def build(nc, a):
    with ExitStack() as ctx:
        sb = lambda n, sh, dt=F32: ctx.enter_context(nc.sbuf_tensor(n, sh, dt))
        a["z"] = nc.dram_tensor("z_dram", (NT, P, BLK), F32, kind="Internal").ap()
        a["u2"] = nc.dram_tensor("u2_dram", (SEQ, D), F32, kind="Internal").ap()
        a["ys"] = nc.dram_tensor("ys_dram", (SEQ * 2, D), F32, kind="Internal").ap()
        s = {
            "cst": sb("cst", [P, C_N]), "cols": sb("cols", [P, 64]), "gqkv": sb("gqkv", [P, 12, L]),
            "region": sb("region", [P, HA * SEQ + HA * L + (NT + 1) * HA * VA]), "ab": sb("ab", [P, NT + 1, 16]),
            "wts": sb("wts", [P, 2, NT]), "slot": sb("slot", [P, NT, 2], I32), "idx": sb("idx", [P, 2, MAXBLK + 2], I32),
            "table": sb("table", [P, MAXBLK + 1], I32),
        }
        s["gq"], s["gk"], s["gv"] = (s["gqkv"][:, 4 * i:4 * i + 4, :] for i in range(3))
        reg, e1, e2 = s["region"], HA * SEQ, HA * (SEQ + L)
        s["aq"] = reg[:, 0:e1].rearrange("p (h t) -> p h t", h=HA)
        s["ak"] = reg[:, e1:e2].rearrange("p (h t) -> p h t", h=HA)
        s["av"] = reg[:, e2:].rearrange("p (t c) -> p t c", t=NT + 1)
        project(nc, a, s, None)
        s["mix"] = sb("mix", [P, NT, D])
        attention(nc, a, s)
        deltanet(nc, a, s)
        s["hres"] = reg[:, 0:NT * D].rearrange("p (t d) -> p t d", t=NT)
        output_and_route(nc, a, s)
        experts(nc, a, s)
        combine(nc, a, s)


_INS = ["x", "meta", "norm_mix", "w_in", "lambda_q1", "lambda_k1", "lambda_q2", "lambda_k2", "diff_norm", "conv_w",
        "a_log", "dt_bias", "gdn_norm", "w_out", "norm_ffn", "w_group", "b_group", "w_router", "b_router",
        "w_gate", "w_up", "w_down", "norm_final"]


def kernel(**inputs):
    import concourse.bacc as _bacc
    from concourse.bass_utils import run_bass_kernel_spmd as _run

    nc = _bacc.Bacc("TRN2", target_bir_lowering=False, num_devices=1)
    arrays = {"in_consts": constants()}
    arrays.update({f"in_{n}": np.ascontiguousarray(inputs[n]) for n in _INS})
    a = {n[3:]: nc.dram_tensor(n, v.shape, F32, kind="ExternalInput").ap() for n, v in arrays.items()}
    a["out"] = nc.dram_tensor("out_0", (1, SEQ, D), F32, kind="ExternalOutput").ap()
    build(nc, a)
    r = _run(nc, [arrays], core_ids=[0])
    return r.results[0]["out_0"]
```

```python
from contextlib import ExitStack

import numpy as np

import concourse.bass as bass
from concourse import mybir

F32 = mybir.dt.float32
I32 = mybir.dt.int32
U32 = mybir.dt.uint32
ALU = mybir.AluOpType
ACT = mybir.ActivationFunctionType
AX = mybir.AxisListType

P = 128
D = 1024
KD = D // P
SEQ = 1024
META = 16
L = SEQ + META
NT = SEQ // P
EPS = 1e-6
HA = 4
HB = 8
DK = 64
VA = 128
LAM_INIT = 0.8 - 0.6
BLK = 512
COL_QA, COL_KA, COL_VA, COL_QKVB, COL_ZB, COL_AB = 0, 512, 1024, 1536, 3072, 3584
NE, NG, EPG, FE = 32, 4, 8, 256
MAXBLK = 48
BIG = 1.0e30
FREE_STEPS = 12
LEVELS = 7

C_ID, C_UP, C_SUP, C_BLK, C_LEV = 0, 128, 256, 384, 512
C_IOTA = C_LEV + LEVELS * 128
C_TOK = C_IOTA + 128
C_E128 = C_TOK + 2 * NT
C_ONE = C_E128 + 32
C_IG = C_ONE + 128
C_EPS = C_IG + 32
C_N = C_EPS + 1
R_SIN = (NT + 1) * 64
R_N = 2 * R_SIN


def constants():
    c = np.zeros((P, C_N + R_N), np.float32)
    p = np.arange(P)
    c[:, C_ID:C_ID + 128] = np.eye(P)
    c[:, C_UP:C_UP + 128] = p[:, None] <= p[None, :]
    c[:, C_SUP:C_SUP + 128] = p[:, None] < p[None, :]
    c[:, C_BLK:C_BLK + 128] = (p[:, None] // 64) == (p[None, :] // 64)
    for lv in range(LEVELS):
        s = 1 << lv
        same = (p[:, None] // (2 * s)) == (p[None, :] // (2 * s))
        c[:, C_LEV + lv * 128:C_LEV + (lv + 1) * 128] = same & (p[:, None] // s % 2 == 0) & (p[None, :] // s % 2 == 1)
    inv = (10000.0 ** (-np.arange(0, 64, 2) / 64.0)).astype(np.float32)
    for t in range(NT + 1):
        pos = (np.arange(P) + (META + P * t if t < NT else 0)).astype(np.float32)
        ang = pos[:, None] * inv[None, :]
        co, si = np.cos(ang), np.sin(ang)
        c[:, C_N + 64 * t:C_N + 64 * t + 64] = np.concatenate([co, co], 1)
        c[:, C_N + R_SIN + 64 * t:C_N + R_SIN + 64 * t + 64] = np.concatenate([-si, si], 1)
    c[:, C_IOTA:C_IOTA + 128] = p[None, :]
    c[:, C_TOK:C_TOK + 2 * NT] = 2 * (p[:, None] + P * (np.arange(2 * NT) // 2)[None, :]) + np.arange(2 * NT)[None, :] % 2 + 1
    c[:, C_E128:C_E128 + 32] = 128 * np.arange(32)[None, :]
    c[:, C_ONE:C_ONE + 128] = 1.0
    c[:, C_IG:C_IG + 32] = np.arange(32)[None, :] - 1000.0
    c[:, C_EPS] = EPS
    return c


def rows(t):
    return P if t < NT else META


def col0(t):
    return META + P * t if t < NT else 0


class Seq:

    def __init__(self, eng, sem):
        self.eng, self.sem, self.n = eng, sem, 0

    def __call__(self, ins):
        self.n += 1
        ins.then_inc(self.sem, 1)
        self.eng.wait_ge(self.sem, self.n)


def clear(nc, sems):
    with nc.Block() as block:
        @block.gpsimd
        def _(pool):
            for x in sems:
                pool.sem_clear(x)


def project(nc, a, s):
    with ExitStack() as ctx, ExitStack() as phase:
        sb = lambda n, sh, dt=F32: ctx.enter_context(nc.sbuf_tensor(n, sh, dt))
        ps = lambda n, sh, dt=F32: ctx.enter_context(nc.psum_tensor(n, sh, dt))
        sems = []

        def sem(n):
            sems.append(ctx.enter_context(nc.semaphore(n)))
            return sems[-1]

        cst, cols = s["cst"], s["cols"]
        ident = cst[:, C_ID:C_ID + 128]
        uT = sb("uT", [P, KD, L])
        rowsb = sb("rowsb", [64, 128])
        ss = sb("ss", [P, NT + 1, 3])
        wblk = sb("wblk", [P, 2, KD, BLK])
        wab = sb("wab", [P, KD, 16])
        cv = sb("cv", [P, L])
        work = sb("work", [P, 3 + 3 * L])
        pad, sq, rn = work[:, 0:3 + L], work[:, 3 + L:3 + 2 * L], work[:, 3 + 2 * L:3 + 3 * L]
        xin = work[:, 3:3 + 2 * D].rearrange("p (b d) -> p b d", b=2)
        xsc = work[:, 3 + 2 * D:3 + 3 * D]
        rope = work[:, 3 + L:3 + L + 3 * BLK].rearrange("p (b d) -> p b d", b=3)
        zt = sb("zt", [P, 2, BLK])
        rot = sb("rot", [P, R_N])

        big = [ps(f"big{i}", [P, 1536]) for i in range(2)]
        small = [ps(f"small{i}", [P, 512]) for i in range(2)]

        x_in, rows_in, cst_in = [sem(f"x_in{i}") for i in range(2)], sem("rows_in"), sem("cst_in")
        w_in_sem = [sem(f"w_in{i}") for i in range(2)]
        wab_in, rot_in = sem("wab_in"), sem("rot_in")
        act_seq, dve_seq = sem("act_seq"), sem("dve_seq")
        ssq, xscaled, x_turned, u_copied = sem("ssq"), sem("xscaled"), sem("x_turned"), sem("u_copied")
        rows_turned, rows_copied = sem("rows_turned"), sem("rows_copied")
        pads = sem("pads")
        big_full, copied, conv0, conv_done, silu_done, sq_done, rn_done, qk_done = (
            sem(x) for x in ("big_full", "copied", "conv0", "conv_done", "silu_done", "sq_done", "rn_done", "qk_done"))
        tok_full, tok_act, roped, rope_turned, rope_copied = (
            sem(x) for x in ("tok_full", "tok_act", "roped", "rope_turned", "rope_copied"))
        w_used = sem("w_used")
        root_done = sem("root_done")
        z_out = [sem(f"z_out{i}") for i in range(2)]

        items = [("T", 0)]
        for m in range(1, 12):
            items.append(("T", m))
            if m - 1 < 8:
                items.append(("N", m - 1))
        nitem = len(items)
        tok = [("ab", t) for t in range(NT + 1)] + [("qa", t) for t in range(NT)] + [("ka", t) for t in range(NT + 1)] \
            + [("va", t) for t in range(NT + 1)] + [("zb", t) for t in range(NT)]
        wcol = [COL_QKVB, COL_QKVB + 512, COL_QKVB + 1024, COL_QA, COL_KA, COL_VA, COL_ZB]
        wbuf = {"qa": 3, "ka": 4, "va": 5, "zb": 6}
        order = [NT] + list(range(NT))
        is_rope = [kd in ("qa", "ka") for kd, _ in tok]
        tokbank = [big[0][:, 0:512], big[0][:, 512:1024], big[1][:, 0:512], big[1][:, 512:1024]]
        ropes_before = lambda n: sum(is_rope[:n])
        acts_before = lambda n: n - ropes_before(n)

        block = phase.enter_context(nc.Block())

        @block.sync
        def _(sp):
            sp.dma_start(s["cst"][:], a["consts"][:, 0:C_N]).then_inc(cst_in, 16)
            sp.dma_start(rowsb[0:48, :], a["conv_w"].rearrange("o i (m c) -> (o i m) c", c=128)).then_inc(rows_in, 16)
            sp.dma_start(rowsb[48:56, :], a["norm_mix"].rearrange("o (m c) -> (o m) c", c=128)).then_inc(rows_in, 16)
            sp.dma_start(rowsb[56:64, :], a["norm_ffn"].rearrange("o (m c) -> (o m) c", c=128)).then_inc(rows_in, 16)
            wv = a["w_in"].rearrange("o (k p) c -> (o p) k c", p=P)
            for j, t in enumerate(order):
                if j >= 2:
                    sp.wait_ge(xscaled, j - 1)
                src = a["x"][0, t * P:(t + 1) * P, :] if t < NT else a["meta"]
                sp.dma_start(xin[0:rows(t), j % 2, :], src).then_inc(x_in[j % 2], 16)
                if j == 2:
                    sp.dma_start(wblk[:, 0, :, :], wv[:, :, wcol[0]:wcol[0] + BLK]).then_inc(w_in_sem[0], 16)
            sp.dma_start(wblk[:, 1, :, :], wv[:, :, wcol[1]:wcol[1] + BLK]).then_inc(w_in_sem[1], 16)
            sp.dma_start(rot[:], a["consts"][:, C_N:]).then_inc(rot_in, 16)
            with nc.allow_non_contiguous_dma(reason="64-byte rows of the gate columns"):
                sp.dma_start(wab[:], wv[:, :, COL_AB:COL_AB + 16]).then_inc(wab_in, 16)
            for b in range(2, 7):
                sp.wait_ge(w_used, b - 1)
                sp.dma_start(wblk[:, b % 2, :, :], wv[:, :, wcol[b]:wcol[b] + BLK]).then_inc(w_in_sem[b % 2], 16)

            for t in range(NT):
                sp.wait_ge(tok_act, acts_before(tok.index(("zb", t))) + 1)
                sp.dma_start(a["z"][t], zt[:, t % 2, :]).then_inc(z_out[t % 2], 16)
            for b in range(2):
                sp.wait_ge(z_out[b], 16 * (NT // 2))

        @block.scalar
        def _(act):
            act.wait_ge(cst_in, 16)
            for j, t in enumerate(order):
                r = rows(t)
                act.wait_ge(x_in[j % 2], 16 * (j // 2 + 1))
                if j >= 1:
                    act.wait_ge(ssq, j)
                act.activation(cv[0:r, 0:D], xin[0:r, j % 2, :], ACT.Square, accum_out=ss[0:r, j, 0:1]).then_inc(ssq, 1)
                act.wait_ge(ssq, j + 1)
                act.activation(ss[0:r, j, 1:2], ss[0:r, j, 0:1], ACT.Sqrt, bias=cst[0:r, C_EPS:C_EPS + 1], scale=1.0 / D).then_inc(root_done, 1)
            act.wait_ge(pads, 1)
            act.wait_ge(x_turned, 2 * (NT + 1))
            for m in range(12):
                i = items.index(("T", m))
                act.wait_ge(big_full, i + 1)
                if m >= 1:
                    act.wait_ge(conv_done, m)
                act.activation(pad[:, 3:3 + L], big[i % 2][:, 0:L], ACT.Copy).then_inc(copied, 1)
                act.wait_ge(copied, m + 1)
                if m >= 1:
                    act.wait_ge(silu_done, m)
                if m == 0:
                    act.wait_ge(ssq, NT + 1)
                    act.wait_ge(rows_copied, 1)
                act.activation(cv[:], pad[:, 0:L], ACT.Copy, scale=cols[:, m:m + 1]).then_inc(conv0, 1)
                act.wait_ge(conv_done, m + 1)
                dst = (s["gq"], s["gk"], s["gv"])[m // 4][:, m % 4, :]
                act.activation(dst, cv[:], ACT.Silu).then_inc(silu_done, 1)
                if 1 <= m <= 8:
                    i = items.index(("N", m - 1))
                    act.wait_ge(big_full, i + 1)
                    if m >= 2:
                        act.wait_ge(qk_done, m - 1)
                    act.activation(rn[:], big[i % 2][:, 0:L], ACT.Sqrt, bias=cst[:, C_EPS:C_EPS + 1]).then_inc(rn_done, 1)
                if m < 8:
                    act.wait_ge(silu_done, m + 1)
                    act.activation(sq[:], dst, ACT.Square).then_inc(sq_done, 1)
            for n, (kind, t) in enumerate(tok):
                r = rows(t)
                src = tokbank[n % 4]
                if is_rope[n]:
                    q = ropes_before(n)
                    dst = s["aq"] if kind == "qa" else s["ak"]
                    off = t * P if kind == "qa" else col0(t)
                    act.wait_ge(rope_turned, q + 1)
                    act.activation(dst[:, :, off:off + r], small[q % 2][:].rearrange("p (h t) -> p h t", h=4)[:, :, 0:r],
                                   ACT.Copy).then_inc(rope_copied, 1)
                    continue
                act.wait_ge(tok_full, n + 1)
                if kind == "ab":
                    act.activation(s["ab"][0:r, t, :], src[0:r, 0:16], ACT.Copy).then_inc(tok_act, 1)
                elif kind == "va":
                    act.activation(s["av"][0:r, t, :], src[0:r, :], ACT.Copy).then_inc(tok_act, 1)
                else:
                    if t >= 2:
                        act.wait_ge(z_out[t % 2], 16 * (t // 2))
                    act.activation(zt[:, t % 2, :], src[0:r, :], ACT.Silu).then_inc(tok_act, 1)

        @block.vector
        def _(dve):
            seq = Seq(dve, dve_seq)
            dve.memset(pad[:, 0:3], 0.0).then_inc(pads, 1)
            seq(dve.memset(s["ab"][:], 0.0))
            dve.wait_ge(rows_turned, 1)
            dve.tensor_copy(cols[:, 0:64], small[0][:, 0:64]).then_inc(rows_copied, 1)
            dve.wait_ge(rows_copied, 1)
            gain = cols[:, 48:56]
            for j, t in enumerate(order):
                r = rows(t)
                dve.wait_ge(root_done, j + 1)
                seq(dve.reciprocal(ss[0:r, j, 2:3], ss[0:r, j, 1:2]))
                if j >= 1:
                    dve.wait_ge(x_turned, 2 * j)
                dve.tensor_scalar(xsc[0:r, :], xin[0:r, j % 2, :], ss[0:r, j, 2:3], None, ALU.mult).then_inc(xscaled, 1)
                for half in range(2):
                    dve.wait_ge(x_turned, 2 * j + half + 1)
                    src = small[half][:].rearrange("p (k t) -> p k t", k=4)[:, :, 0:r]
                    g = gain[:, 4 * half:4 * half + 4].unsqueeze(2).to_broadcast([P, 4, r])
                    dve.tensor_tensor(uT[:, 4 * half:4 * half + 4, col0(t):col0(t) + r], src, g, ALU.mult).then_inc(u_copied, 1)

            def conv(m):
                dve.wait_ge(conv0, m + 1)
                for i in range(1, 4):
                    w = cols[:, 12 * i + m:12 * i + m + 1]
                    ins = dve.scalar_tensor_tensor(cv[:], pad[:, i:i + L], w, cv[:], ALU.mult, ALU.add)
                    if i < 3:
                        seq(ins)
                    else:
                        ins.then_inc(conv_done, 1)

            def l2(m):
                dve.wait_ge(rn_done, m + 1)
                seq(dve.reciprocal(rn[:], rn[:]))
                dst = (s["gq"], s["gk"])[m // 4][:, m % 4, :]
                dve.scalar_tensor_tensor(dst, dst, DK ** -0.5 if m < 4 else 1.0, rn[:], ALU.mult, ALU.mult).then_inc(qk_done, 1)

            for m in range(12):
                conv(m)
                if 1 <= m <= 8:
                    l2(m - 1)
            dve.wait_ge(rot_in, 16)
            for n, (kind, t) in enumerate(tok):
                if not is_rope[n]:
                    continue
                r, q = rows(t), ropes_before(n)
                src = tokbank[n % 4][0:r, :].rearrange("p (h d) -> p h d", d=64)
                co = rot[0:r, 64 * t:64 * t + 64].unsqueeze(1).to_broadcast([r, 8, 64])
                si = rot[0:r, R_SIN + 64 * t:R_SIN + 64 * t + 64]
                dve.wait_ge(tok_full, n + 1)
                v = lambda b: rope[0:r, b, :].rearrange("p (h d) -> p h d", d=64)
                if q >= 1:
                    dve.wait_ge(rope_turned, q)
                dve.tensor_tensor(v(0), src, co, ALU.mult)
                dve.tensor_tensor(v(1)[:, :, 0:32], src[:, :, 32:64], si[:, 0:32].unsqueeze(1).to_broadcast([r, 8, 32]), ALU.mult)
                seq(dve.tensor_tensor(v(1)[:, :, 32:64], src[:, :, 0:32], si[:, 32:64].unsqueeze(1).to_broadcast([r, 8, 32]), ALU.mult))
                dve.tensor_tensor(rope[0:r, 2, :], rope[0:r, 0, :], rope[0:r, 1, :], ALU.add).then_inc(roped, 1)
                dve.wait_ge(roped, q + 1)

        @block.tensor
        def _(pe):
            pe.wait_ge(cst_in, 16)
            pe.wait_ge(rows_in, 48)
            pe.transpose(small[0][:, 0:64], rowsb[:], ident[0:64, 0:64]).then_inc(rows_turned, 1)
            pe.wait_ge(rows_copied, 1)
            for j, t in enumerate(order):
                r = rows(t)
                pe.wait_ge(xscaled, j + 1)
                for half in range(2):
                    if j >= 1:
                        pe.wait_ge(u_copied, 2 * j - 1 + half)
                    for kk in range(4):
                        kx = 4 * half + kk
                        mm = pe.transpose(small[half][:, kk * 128:kk * 128 + r], xsc[0:r, kx * P:(kx + 1) * P], ident[0:r, 0:r])
                    mm.then_inc(x_turned, 1)
            pe.wait_ge(u_copied, 2 * (NT + 1))

            def freed(i):
                kind, m = items[i - 2]
                pe.wait_ge(copied if kind == "T" else rn_done, m + 1)

            for i, (kind, m) in enumerate(items):
                if i >= 2:
                    freed(i)
                if kind == "T":
                    b = m // 4
                    if m % 4 == 0:
                        pe.wait_ge(w_in_sem[b % 2], 16 * (b // 2 + 1))
                    for c in range(0, L, 512):
                        n = min(512, L - c)
                        for kx in range(KD):
                            mm = pe.matmul(big[i % 2][:, c:c + n], wblk[:, b % 2, kx, (m % 4) * 128:(m % 4 + 1) * 128],
                                           uT[:, kx, c:c + n], start=kx == 0, stop=kx == KD - 1)
                    mm.then_inc(big_full, 1)
                    if m % 4 == 3:
                        pe.wait_ge(big_full, i + 1)
                        pe.sem_inc(w_used, 1)
                else:
                    pe.wait_ge(sq_done, m + 1)
                    for c in range(0, L, 512):
                        n = min(512, L - c)
                        mm = pe.matmul(big[i % 2][:, c:c + n], cst[:, C_BLK:C_BLK + 128], sq[:, c:c + n], start=True, stop=True)
                    mm.then_inc(big_full, 1)

            def turn(n):
                kind, t = tok[n]
                r, q = rows(t), ropes_before(n)
                pe.wait_ge(roped, q + 1)
                if q >= 2:
                    pe.wait_ge(rope_copied, q - 1)
                for h in range(4):
                    mm = pe.transpose(small[q % 2][:, h * 128:h * 128 + r], rope[0:r, 2, h * 128:(h + 1) * 128], ident[0:r, 0:r])
                mm.then_inc(rope_turned, 1)

            for n, (kind, t) in enumerate(tok):
                if n < 4:
                    freed(nitem if n < 2 else nitem + 1)
                else:
                    j = n - 4
                    pe.wait_ge(roped if is_rope[j] else tok_act, (ropes_before(j) if is_rope[j] else acts_before(j)) + 1)
                c, r = col0(t), rows(t)
                if kind == "ab":
                    if n == 0:
                        pe.wait_ge(wab_in, 16)
                    w, nn = wab, 16
                else:
                    b = wbuf[kind]
                    w, nn = wblk[:, b % 2], BLK
                    if t == 0:
                        pe.wait_ge(w_in_sem[b % 2], 16 * (b // 2 + 1))
                for kx in range(KD):
                    mm = pe.matmul(tokbank[n % 4][0:r, 0:nn], uT[:, kx, c:c + r], w[:, kx, 0:nn], start=kx == 0, stop=kx == KD - 1)
                mm.then_inc(tok_full, 1)
                if kind in ("qa", "ka") and t == (NT - 1 if kind == "qa" else NT):
                    pe.wait_ge(tok_full, n + 1)
                    pe.sem_inc(w_used, 1)
                if n >= 1 and is_rope[n - 1]:
                    turn(n - 1)

        phase.close()
        clear(nc, sems)


class Share:

    def __init__(self, piece, bounds):
        self.piece, self.bounds, self.k = piece, bounds, 0

    def __call__(self):
        for g in range(self.bounds[self.k], self.bounds[self.k + 1]):
            self.piece(g)
        self.k += 1


def mixers(nc, a, s):
    with ExitStack() as ctx, ExitStack() as phase:
        sb = lambda n, sh, dt=F32: ctx.enter_context(nc.sbuf_tensor(n, sh, dt))
        ps = lambda n, sh, dt=F32: ctx.enter_context(nc.psum_tensor(n, sh, dt))
        sems = []

        def sem(n):
            sems.append(ctx.enter_context(nc.semaphore(n)))
            return sems[-1]

        sem2 = lambda n: [sem(f"{n}{b}") for b in range(2)]
        cst, mix, gq, gk, gv = s["cst"], s["mix"], s["gq"], s["gk"], s["gv"]
        ident, upper = cst[:, C_ID:C_ID + 128], cst[:, C_UP:C_UP + 128]

        probs = sb("probs", [P, 2, 2, L])
        probsT = sb("probsT", [P, NT + 1, P])
        nmax, bias, rsum, rinv = (sb(x, [P, 2, 2]) for x in ("nmax", "bias", "rsum", "rinv"))
        coef = sb("coef", [P, 2])
        lam = sb("lam", [P, 8])
        again = sb("again", [P, VA])
        astat = sb("astat", [P, 3, NT * HA])
        sqo = sb("sqo", [P, VA])
        ring = [ps(f"ring{i}", [P, 512]) for i in range(3)]
        lam_in, ring_full, ring_read = sem("lam_in"), sem("ring_full"), sem("ring_read")
        lam_sum, lam_exp, maxed, exped, mixed = (sem(x) for x in ("lam_sum", "lam_exp", "maxed", "exped", "mixed"))
        a_sq, a_root, a_dve, a_done = sem("a_sq"), sem("a_root"), sem("a_dve"), sem("a_done")

        items = [(i, h) for i in range(NT) for h in range(HA)]
        N = len(items)
        nkeys = lambda i: META + P * (i + 1)
        pieces, weight = [], []

        def add(w, *p):
            pieces.append(p)
            weight.append(w)

        for n in range(N + 1):
            if n >= 1:
                add(0, "mix", n - 1, 0, 0)
            if n < N:
                for c in range(2):
                    nk = nkeys(items[n][0])
                    for k0 in range(0, nk, 512):
                        add(min(nk - k0, 512) + 64, "score", n, c, k0)
                    add(0, "max", n, c, 0)
            if n >= 1:
                i, h = items[n - 1]
                for f in range(0, i + 2, 4):
                    add(128 * min(4, i + 2 - f), "turn", n - 1, f, 0)
                add(128 * (i + 2), "out", n - 1, 0, 0)
            if n < N:
                add(0, "exp", n, 0, 0)
                add(0, "exp", n, 1, 0)
        add(0, "root", 0, 0, 0)
        for i in range(NT):
            add(128, "scale", i, 0, 0)
        for i in range(NT):
            add(128, "gain", i, 0, 0)
        ring_pos, after = {}, {}
        for g, p in enumerate(pieces):
            if p[0] in ("score", "turn", "out"):
                ring_pos[g] = len(ring_pos)
            after[p[0:3]] = len(ring_pos)

        TILES = [NT] + list(range(NT))
        NJ = len(TILES)
        G8 = NJ * HB
        inv, aqk = sb("inv", [P, 2, HB, P]), sb("aqk", [P, HB, P])
        tri, xm = sb("tri", [P, HB, P]), sb("xm", [P, HB, P])
        ntm, bt = sb("ntm", [P, HB, P]), sb("bt", [P, HB, P])
        dec = sb("dec", [P, HB, P])
        ktok, vtok = sb("ktok", [P, 512]), sb("vtok", [P, 512])
        zz, vn, v2 = sb("zz", [P, 512]), sb("vn", [P, 512]), sb("v2", [P, 512])
        lamv = zz[:, 0:256].rearrange("p (a c) -> p a c", a=4)
        state = sb("state", [P, 4, DK])
        gat = sb("gat", [P, 6, G8])
        gc, eg, neg, beta, graw, tmp = (gat[:, i, :] for i in range(6))
        par = sb("par", [P, 3, HB])
        gain = sb("gdn_gain", [P, DK])
        glc, ekl, egs = sb("glc", [P, 2, HB]), sb("ekl", [P, 2, HB]), sb("egs", [P, 2, 4])
        gl = sb("gl", [P, 2, 2, 4])
        stat = sb("gstat", [P, 3, NT * HB])
        zg = s["region"][:, 0:NT * 512].rearrange("p (t c) -> p t c", t=NT)

        level_bank = [ps(f"level{b}", [P, 512]) for b in range(2)]
        wide = [ps(f"wide{b}", [P, 512]) for b in range(2)]
        solo = ps("solo", [P, 512])
        par_in, z_in, dve_seq, pool_seq = (sem(x) for x in ("gpar_in", "z_in", "gdve_seq", "gpool_seq"))
        g1, g2, g3, g4, gc_full, gates, eg_done = (sem(x) for x in ("g1", "g2", "g3", "g4", "gc_full", "gates", "eg_done"))
        kk_full, kq_full, gcb_full, d_done, dec_done, aqk_raw = (
            sem2(x) for x in ("kk_full", "kq_full", "gcb_full", "d_done", "dec_done", "aqk_raw"))
        nt_done, aqk_done, r1_done, t1_turned, t1_copied, bt_done = (
            sem2(x) for x in ("nt_done", "aqk_done", "r1_done", "t1_turned", "t1_copied", "bt_done"))
        x_full, x_copied, y_full, t_new, r_turned, r_copied, r_done = (
            sem2(x) for x in ("x_full", "x_copied", "y_full", "t_new", "r_turned", "r_copied", "r_done"))
        kt_turned, kt_copied, vt_turned, vt_copied, glc_done, ekl_done, egs_done = (
            sem(x) for x in ("kt_turned", "kt_copied", "vt_turned", "vt_copied", "glc_done", "ekl_done", "egs_done"))
        ks_full, z_done, v_full, vn_done, v2_done, o2_full, s_full, s_done, o_done = (
            sem(x) for x in ("ks_full", "z_done", "v_full", "vn_done", "v2_done", "o2_full", "gs_full", "s_done", "o_done"))
        gl_done = sem("gl_done")
        o_sq, o_root, zg_done, normed, wout_in = (sem(x) for x in ("go_sq", "go_root", "zg_done", "normed", "wout_in"))

        nlev = lambda j: 3 if j == 0 else 6
        lev0 = lambda j: 0 if j == 0 else 3 + 6 * (j - 1)
        turns_before = lambda j, lv: lev0(j) + lv - j
        tmat = lambda w, r: w[:].rearrange("p (h c) -> p h c", h=4)[0:r, :, 0:r]
        batch = lambda m, b, r: m.rearrange("p (hh b) c -> p b hh c", b=2)[0:r, b, :, 0:r]
        gate = lambda v, j, b, r: v.rearrange("p (t hh b) -> p t b hh", b=2, t=NJ)[0:r, TILES[j], b, :]
        one = lambda v, j, h, r: v[0:r, TILES[j] * HB + h:TILES[j] * HB + h + 1]

        STEPS = sum(3 + 3 * nlev(j) for j in range(NJ)) + 2 * (NJ - 1) + 4 * NJ
        room = STEPS - FREE_STEPS
        total, run, bounds = sum(weight), 0, [0]
        for k in range(STEPS):
            g = bounds[-1]
            while g < len(pieces) and (run + weight[g] / 2) * room <= (k + 1) * total:
                run += weight[g]
                g += 1
            bounds.append(g)
        assert bounds[-1] == len(pieces)

        block = phase.enter_context(nc.Block())

        @block.sync
        def _(sp):
            for j, n in enumerate(("lambda_q1", "lambda_k1", "lambda_q2", "lambda_k2")):
                sp.dma_start(lamv[:, j, :], a[n].to_broadcast([P, 64])).then_inc(lam_in, 16)
            sp.dma_start(again[:], a["diff_norm"].to_broadcast([P, VA])).then_inc(lam_in, 16)
            sp.dma_start(par[:, 0, :], a["a_log"].to_broadcast([P, HB])).then_inc(par_in, 16)
            sp.dma_start(par[:, 1, :], a["dt_bias"].to_broadcast([P, HB])).then_inc(par_in, 16)
            sp.dma_start(gain[:], a["gdn_norm"].to_broadcast([P, DK])).then_inc(par_in, 16)
            sp.wait_ge(ring_full, len(ring_pos))
            sp.dma_start(zg[:], a["z"].rearrange("t p c -> p t c")).then_inc(z_in, 16)
            sp.dma_start(s["wout"], a["w_out"].rearrange("o (k p) c -> (o p) k c", p=P)).then_inc(wout_in, 16)
            sp.wait_ge(wout_in, 16)

        @block.scalar
        def _(act):
            def piece(g):
                what, n, c, k0 = pieces[g]
                if g in ring_pos:
                    bank = ring[ring_pos[g] % 3]
                    act.wait_ge(ring_full, ring_pos[g] + 1)
                if what == "score":
                    k1 = min(nkeys(items[n][0]), k0 + 512)
                    act.activation(probs[:, n % 2, c, k0:k1], bank[:, 0:k1 - k0], ACT.Copy).then_inc(ring_read, 1)
                elif what == "turn":
                    nb = min(4, items[n][0] + 2 - c)
                    if c == 0:
                        act.activation(probsT[0:META, 0, :], bank[0:META, 0:128], ACT.Copy)
                        act.activation(probsT[:, 1:nb, :], bank[:, 128:nb * 128], ACT.Copy).then_inc(ring_read, 1)
                    else:
                        act.activation(probsT[:, c:c + nb, :], bank[:, 0:nb * 128], ACT.Copy).then_inc(ring_read, 1)
                elif what == "out":
                    i, h = items[n]
                    if n >= 1:
                        act.wait_ge(a_sq, n)
                    act.activation(sqo[:], bank[:, 0:VA], ACT.Square, scale=rinv[:, n % 2, 0:1], accum_out=astat[:, 0, n:n + 1]).then_inc(a_sq, 1)
                    act.activation(mix[:, i, h * VA:(h + 1) * VA], bank[:, 0:VA], ACT.Copy,
                                   scale=rinv[:, n % 2, 0:1]).then_inc(ring_read, 1)
                elif what == "exp":
                    row = probs[:, n % 2, c, 0:nkeys(items[n][0])]
                    act.wait_ge(maxed, 2 * n + c + 1)
                    act.activation(row, row, ACT.Exp, bias=bias[:, n % 2, c:c + 1], scale=DK ** -0.5,
                                   accum_out=rsum[:, n % 2, c:c + 1]).then_inc(exped, 1)
                elif what == "root":
                    act.wait_ge(a_sq, N)
                    act.activation(astat[:, 1, :], astat[:, 0, :], ACT.Sqrt, bias=cst[:, C_EPS:C_EPS + 1], scale=1.0 / VA).then_inc(a_root, 1)

            attend = Share(piece, bounds)
            act.wait_ge(lam_sum, 1)
            act.activation(lam[:, 2:4], lam[:, 0:2], ACT.Exp).then_inc(lam_exp, 1)
            act.wait_ge(par_in, 48)
            act.activation(par[:, 2, :], par[:, 0, :], ACT.Exp).then_inc(g1, 1)
            act.wait_ge(g2, 1)
            act.activation(tmp, tmp, ACT.Exp, scale=-1.0)
            act.activation(beta, beta, ACT.Exp, scale=-1.0).then_inc(g3, 1)
            act.wait_ge(g3, 1)
            act.activation(tmp, tmp, ACT.Ln, bias=cst[:, C_ONE:C_ONE + 1]).then_inc(g4, 1)
            act.wait_ge(gates, 1)
            act.activation(eg, gc, ACT.Exp).then_inc(eg_done, 1)

            def prepare(j):
                r = rows(TILES[j])
                for b in range(2):
                    act.wait_ge(gl_done, 2 * j + b + 1)
                    if j >= 2:
                        act.wait_ge(s_done, j - 1)
                    last = gl[64 * b:64 * b + 64, j % 2, b, :]
                    act.activation(egs[64 * b:64 * b + 64, j % 2, :], last, ACT.Exp).then_inc(egs_done, 1)
                    act.wait_ge(d_done[b], j + 1)
                    act.activation(batch(dec, b, r), batch(dec, b, r), ACT.Exp).then_inc(dec_done[b], 1)
                act.wait_ge(glc_done, j + 1)
                act.activation(ekl[0:r, j % 2, :], glc[0:r, j % 2, :], ACT.Exp).then_inc(ekl_done, 1)
                attend()
                attend()
                for b in range(2):
                    act.wait_ge(t1_turned[b], j + 1)
                    act.activation(batch(tri, b, r), tmat(level_bank[b], r), ACT.Copy).then_inc(t1_copied[b], 1)
                attend()

            def level(j, lv):
                r, n = rows(TILES[j]), lev0(j) + lv
                for b in range(2):
                    act.wait_ge(x_full[b], n)
                    act.activation(batch(xm, b, r), tmat(level_bank[b], r), ACT.Copy).then_inc(x_copied[b], 1)
                attend()
                attend()
                if lv < nlev(j):
                    for b in range(2):
                        act.wait_ge(r_turned[b], turns_before(j, lv))
                        act.activation(batch(inv[:, j % 2], b, r), tmat(level_bank[b], r), ACT.Copy).then_inc(r_copied[b], 1)
                attend()

            def roots(t0, t1):
                c = slice(HB * t0, HB * t1)
                act.wait_ge(o_sq, t1)
                act.activation(stat[:, 1, c], stat[:, 0, c], ACT.Sqrt, bias=cst[:, C_EPS:C_EPS + 1], scale=1.0 / DK).then_inc(o_root, 1)

            def tokens(j):
                r = rows(TILES[j])
                act.wait_ge(kt_turned, j + 1)
                act.activation(ktok[0:r, :], solo[0:r, :], ACT.Copy).then_inc(kt_copied, 1)
                attend()
                act.wait_ge(vt_turned, j + 1)
                act.activation(vtok[0:r, :], solo[0:r, :], ACT.Copy).then_inc(vt_copied, 1)
                attend()

            for j in range(NJ + 1):
                if j >= 1:
                    tokens(j - 1)
                if j < NJ:
                    prepare(j)
                    level(j, 1)
                if j >= 2:
                    attend()
                if j < NJ:
                    level(j, 2)
                if j >= 1:
                    attend()
                if j < NJ:
                    level(j, 3)
                if j >= 1:
                    attend()
                if 1 <= j < NJ:
                    level(j, 4)
                    attend()
                    if j == NJ - 1:
                        roots(0, NT - 1)
                    level(j, 5)
                    level(j, 6)
            roots(NT - 1, NT)

        @block.gpsimd
        def _(pool):
            seq = Seq(pool, pool_seq)

            def prepare(j):
                r = rows(TILES[j])
                idb = ident[0:r, 0:r].unsqueeze(1).to_broadcast([r, 4, r])
                for b in range(2):
                    pool.wait_ge(nt_done[b], j + 1)
                    if j >= 2:
                        pool.wait_ge(o_done, j - 1)
                    m0 = cst[0:r, C_LEV:C_LEV + r].unsqueeze(1).to_broadcast([r, 4, r])
                    dst = batch(inv[:, j % 2], b, r)
                    seq(pool.tensor_tensor(dst, batch(ntm, b, r), m0, ALU.mult))
                    pool.tensor_tensor(dst, idb, dst, ALU.subtract).then_inc(r1_done[b], 1)
                blocks(j, 1)

            def blocks(j, lv):
                r, n = rows(TILES[j]), lev0(j) + lv
                m = cst[0:r, C_LEV + 128 * lv:C_LEV + 128 * lv + r].unsqueeze(1).to_broadcast([r, 4, r])
                for b in range(2):
                    if n >= 2:
                        pool.wait_ge(x_full[b], n - 1)
                    pool.tensor_tensor(batch(bt[:], b, r), batch(ntm, b, r), m, ALU.mult).then_inc(bt_done[b], 1)

            def mask(j):
                up = upper.unsqueeze(1).to_broadcast([P, 4, P])
                for b in range(2):
                    pool.wait_ge(aqk_raw[b], j)
                    dst = batch(aqk[:], b, P)
                    pool.tensor_tensor(dst, dst, up, ALU.mult).then_inc(aqk_done[b], 1)

            def recur(j):
                r = rows(TILES[j])
                if j == NJ - 1:
                    return
                pool.wait_ge(vn_done, j + 1)
                pool.wait_ge(ekl_done, j + 1)
                k = ekl[0:r, j % 2, :].unsqueeze(2).to_broadcast([r, HB, DK])
                v = lambda m: m[0:r, :].rearrange("p (h c) -> p h c", h=HB)
                if j >= 1:
                    pool.wait_ge(s_full, j)
                pool.tensor_tensor(v(v2), v(vn), k, ALU.mult).then_inc(v2_done, 1)

            for j in range(NJ + 1):
                if j < NJ:
                    prepare(j)
                    blocks(j, 2)
                    blocks(j, 3)
                if j >= 1:
                    recur(j - 1)
                if 1 <= j < NJ:
                    blocks(j, 4)
                    mask(j)
                    blocks(j, 5)
                    blocks(j, 6)

        @block.vector
        def _(dve):
            seq, aseq = Seq(dve, dve_seq), Seq(dve, a_dve)
            dve.wait_ge(lam_in, 80)
            seq(dve.tensor_tensor(lamv[:, 0, :], lamv[:, 0, :], lamv[:, 1, :], ALU.mult))
            seq(dve.tensor_tensor(lamv[:, 2, :], lamv[:, 2, :], lamv[:, 3, :], ALU.mult))
            dve.tensor_reduce(lam[:, 0:2], lamv[:].rearrange("p (a b) c -> p a b c", a=2)[:, :, 0, :], AX.X, ALU.add).then_inc(lam_sum, 1)
            dve.wait_ge(lam_exp, 1)
            seq(dve.tensor_tensor(lam[:, 4:5], lam[:, 3:4], lam[:, 2:3], ALU.subtract))
            seq(dve.tensor_scalar(lam[:, 5:6], lam[:, 4:5], -LAM_INIT, None, ALU.add))
            dve.wait_ge(par_in, 48)
            ab3 = s["ab"][:, :, 0:8]
            g3d = graw.rearrange("p (t h) -> p t h", h=HB)
            seq(dve.tensor_tensor(g3d, ab3, par[:, 1, :].unsqueeze(1).to_broadcast([P, NJ, HB]), ALU.add))
            seq(dve.scalar_tensor_tensor(tmp, graw, -1.0, graw, ALU.mult, ALU.max))
            dve.tensor_copy(beta.rearrange("p (t h) -> p t h", h=HB), s["ab"][:, :, 8:16]).then_inc(g2, 1)
            dve.wait_ge(g4, 1)
            seq(dve.scalar_tensor_tensor(graw, graw, 0.0, tmp, ALU.max, ALU.add))
            dve.wait_ge(g1, 1)
            seq(dve.scalar_tensor_tensor(g3d, g3d, -1.0, par[:, 2, :].unsqueeze(1).to_broadcast([P, NJ, HB]), ALU.mult, ALU.mult))
            seq(dve.tensor_scalar(beta, beta, 1.0, None, ALU.add))
            seq(dve.reciprocal(beta, beta))
            dve.sem_inc(g2, 1)
            dve.wait_ge(gc_full, 1)
            dve.tensor_copy(gc, solo[:, 0:G8]).then_inc(gates, 1)
            dve.wait_ge(eg_done, 1)
            seq(dve.tensor_scalar(neg, eg, -1.0, None, ALU.mult))

            def piece(g):
                what, n, c, _ = pieces[g]
                if what == "max":
                    b, nk = n % 2, nkeys(items[n][0])
                    dve.wait_ge(ring_read, after["score", n, c])
                    aseq(dve.memset(probs[0:64, b, c, nk - 64:nk], -BIG))
                    aseq(dve.tensor_reduce(nmax[:, b, c:c + 1], probs[:, b, c, 0:nk], AX.X, ALU.max))
                    dve.tensor_scalar(bias[:, b, c:c + 1], nmax[:, b, c:c + 1], -DK ** -0.5, None, ALU.mult).then_inc(maxed, 1)
                elif what == "mix":
                    b, nk = n % 2, nkeys(items[n][0])
                    dve.wait_ge(exped, 2 * n + 2)
                    if n >= 2:
                        dve.wait_ge(ring_read, after["out", n - 2, 0])
                    aseq(dve.reciprocal(rinv[:, b, :], rsum[:, b, :]))
                    aseq(dve.tensor_scalar(coef[:, b:b + 1], rinv[:, b, 1:2], rsum[:, b, 0:1], lam[:, 5:6], ALU.mult, ALU.mult))
                    dve.scalar_tensor_tensor(probs[:, b, 0, 0:nk], probs[:, b, 1, 0:nk], coef[:, b:b + 1], probs[:, b, 0, 0:nk],
                                             ALU.mult, ALU.add).then_inc(mixed, 1)
                elif what == "scale":
                    if n == 0:
                        dve.wait_ge(a_root, 1)
                        aseq(dve.reciprocal(astat[:, 2, :], astat[:, 1, :]))
                        aseq(dve.tensor_scalar(astat[:, 2, :], astat[:, 2, :], 1.0 - LAM_INIT, None, ALU.mult))
                    o = mix[:, n, 0:512].rearrange("p (h d) -> p h d", d=VA)
                    r = astat[:, 2, HA * n:HA * n + HA].unsqueeze(2).to_broadcast([P, HA, VA])
                    aseq(dve.tensor_tensor(o, o, r, ALU.mult))
                    dve.tensor_tensor(o, o, again[:].unsqueeze(1).to_broadcast([P, HA, VA]), ALU.mult).then_inc(a_done, 1)
                elif what == "gain":
                    if n == 0:
                        dve.wait_ge(z_in, 16)
                    z = zg[:, n, :].rearrange("p (h d) -> p h d", d=DK)
                    dve.tensor_tensor(z, z, gain[:].unsqueeze(1).to_broadcast([P, HB, DK]), ALU.mult).then_inc(zg_done, 1)

            attend = Share(piece, bounds)

            def prepare(j):
                r = rows(TILES[j])
                for b in range(2):
                    dve.wait_ge(gcb_full[b], j + 1)
                    if j >= 1:
                        dve.wait_ge(nt_done[b], j)
                    if j >= 2:
                        dve.wait_ge(aqk_raw[b], j - 1)
                    for hh in range(4):
                        ins = dve.tensor_scalar(dec[0:r, 2 * hh + b, 0:r], wide[b][0:r, hh * 128:hh * 128 + r], one(gc, j, 2 * hh + b, r),
                                                0.0, ALU.subtract, ALU.min)
                    ins.then_inc(d_done[b], 1)
                    if j >= 2:
                        dve.wait_ge(egs_done, 2 * (j - 1))
                    dve.tensor_copy(gl[:, j % 2, b, :], wide[b][:].rearrange("p (h c) -> p h c", h=4)[:, :, r - 1]).then_inc(gl_done, 1)
                    dve.wait_ge(gl_done, 2 * j + b + 1)
                    dst = glc[0:r, j % 2, :].rearrange("p (hh b) -> p b hh", b=2)[:, b, :]
                    seq(dve.tensor_tensor(dst, gl[0:r, j % 2, b, :], gate(gc, j, b, r), ALU.subtract))
                dve.sem_inc(glc_done, 1)
                attend()
                for b in range(2):
                    dve.wait_ge(kk_full[b], j + 1)
                    dve.wait_ge(dec_done[b], j + 1)
                    if j >= 1:
                        dve.wait_ge(bt_done[b], lev0(j))
                    for hh in range(4):
                        h = 2 * hh + b
                        ins = dve.scalar_tensor_tensor(ntm[0:r, h, 0:r], level_bank[b][0:r, hh * 128:hh * 128 + r], one(beta, j, h, r), dec[0:r, h, 0:r],
                                                       ALU.mult, ALU.mult)
                    ins.then_inc(nt_done[b], 1)
                attend()
                attend()

            def decayed(j):
                for b in range(2):
                    dve.wait_ge(kq_full[b], j)
                    if j >= 2:
                        dve.wait_ge(o2_full, j - 1)
                    dve.tensor_tensor(batch(aqk[:], b, P), tmat(wide[b], P), batch(dec, b, P), ALU.mult).then_inc(aqk_raw[b], 1)

            def level(j, lv):
                r, n = rows(TILES[j]), lev0(j) + lv
                attend()
                for b in range(2):
                    dve.wait_ge(y_full[b], n)
                    if lv < nlev(j):
                        dve.tensor_tensor(batch(tri, b, r), batch(tri, b, r), tmat(level_bank[b], r), ALU.subtract).then_inc(t_new[b], 1)
                    else:
                        dst = batch(inv[:, j % 2], b, r)
                        dve.tensor_tensor(dst, dst, tmat(level_bank[b], r), ALU.subtract).then_inc(r_done[b], 1)
                attend()
                attend()

            def normalise(*tiles):
                part = slice(0, NT - 1) if tiles[0] < NT - 1 else slice(NT - 1, NT)
                if tiles[0] in (0, NT - 1):
                    dve.wait_ge(o_root, 1 if tiles[0] == 0 else 2)
                    seq(dve.reciprocal(stat[:, 2, HB * part.start:HB * part.stop], stat[:, 1, HB * part.start:HB * part.stop]))
                    dve.wait_ge(zg_done, NT)
                for t in tiles:
                    g = mix[:, t, 512:1024].rearrange("p (h d) -> p h d", d=DK)
                    z = zg[:, t, :].rearrange("p (h d) -> p h d", d=DK)
                    seq(dve.tensor_tensor(g, g, stat[:, 2, HB * t:HB * t + HB].unsqueeze(2).to_broadcast([P, HB, DK]), ALU.mult))
                    dve.tensor_tensor(g, g, z, ALU.mult).then_inc(normed, 1)

            v3 = lambda m, r: m[0:r, :].rearrange("p (h c) -> p h c", h=HB)

            def residual(j):
                r = rows(TILES[j])
                dve.wait_ge(vt_copied, j + 1)
                dve.wait_ge(ks_full, j)
                if j >= 2:
                    dve.wait_ge(v_full, j)
                for h in range(HB):
                    ins = dve.scalar_tensor_tensor(zz[0:r, h * DK:(h + 1) * DK], wide[h % 2][0:r, h // 2 * DK:h // 2 * DK + DK], one(neg, j, h, r),
                                                   vtok[0:r, h * DK:(h + 1) * DK], ALU.mult, ALU.add)
                ins.then_inc(z_done, 1)

            def new_values(j):
                r = rows(TILES[j])
                dve.wait_ge(v_full, j + 1)
                if j >= 1:
                    dve.wait_ge(v2_done, j)
                    if j >= 2:
                        dve.wait_ge(o2_full, j - 1)
                bb = beta.rearrange("p (t h) -> p t h", h=HB)[0:r, TILES[j], :].unsqueeze(2).to_broadcast([r, HB, DK])
                dve.tensor_tensor(v3(vn, r), v3(solo, r), bb, ALU.mult).then_inc(vn_done, 1)

            def update(j):
                r, t = rows(TILES[j]), TILES[j]
                if j < NJ - 1:
                    dve.wait_ge(s_full, j + 1)
                    if j == 0:
                        dve.tensor_copy(state[:].rearrange("p h c -> p (h c)"), solo[:, 0:256]).then_inc(s_done, 1)
                    else:
                        for hh in range(4):
                            ins = dve.scalar_tensor_tensor(state[:, hh, :], state[:, hh, :], egs[:, j % 2, hh:hh + 1], solo[:, hh * DK:(hh + 1) * DK],
                                                           ALU.mult, ALU.add)
                        ins.then_inc(s_done, 1)
                if j == 0:
                    dve.sem_inc(o_done, 1)
                    return
                dve.wait_ge(o2_full, j)
                for b in range(2):
                    ins = dve.tensor_copy(zz[0:r, :].rearrange("p (hh b c) -> p b hh c", b=2, c=DK)[:, b, :, :],
                                          wide[b][0:r, 0:256].rearrange("p (h c) -> p h c", c=DK))
                seq(ins)
                for h in range(HB):
                    ins = dve.scalar_tensor_tensor(mix[:, t, 512 + h * DK:512 + (h + 1) * DK],
                                                   wide[h % 2][0:r, 256 + h // 2 * DK:256 + h // 2 * DK + DK], one(eg, j, h, r),
                                                   zz[0:r, h * DK:(h + 1) * DK], ALU.mult, ALU.add)
                ins.then_inc(o_done, 1)
                dve.wait_ge(o_done, j + 1)
                seq(dve.tensor_tensor(zz[:], mix[:, t, 512:1024], mix[:, t, 512:1024], ALU.mult))
                dve.tensor_reduce(stat[:, 0, HB * t:HB * t + HB], zz[:].rearrange("p (h d) -> p h d", d=DK), AX.X, ALU.add).then_inc(o_sq, 1)
                dve.wait_ge(o_sq, j)

            for j in range(NJ + 1):
                if j >= 1:
                    attend()
                    attend()
                if j < NJ:
                    prepare(j)
                    level(j, 1)
                if j >= 2:
                    residual(j - 1)
                    attend()
                if j == NJ:
                    normalise(4)
                if j < NJ:
                    level(j, 2)
                if j >= 1:
                    new_values(j - 1)
                    attend()
                if j == NJ:
                    normalise(5, 6)
                if j < NJ:
                    level(j, 3)
                if j >= 1:
                    update(j - 1)
                    attend()
                if 1 <= j < NJ:
                    level(j, 4)
                    decayed(j)
                    attend()
                    level(j, 5)
                    if j == NJ - 1:
                        normalise(0, 1)
                    level(j, 6)
                    if j == NJ - 1:
                        normalise(2, 3)

            normalise(NT - 1)

        @block.tensor
        def _(pe):
            def piece(g):
                what, n, c, k0 = pieces[g]
                if g not in ring_pos:
                    return
                i, h = items[n]
                u = ring_pos[g]
                bank = ring[u % 3]
                if u >= 3:
                    pe.wait_ge(ring_read, u - 2)
                if what == "score":
                    k1 = min(nkeys(i), k0 + 512)
                    mm = pe.matmul(bank[:, 0:k1 - k0], s["aq"][64 * c:64 * c + 64, h, P * i:P * i + P],
                                   s["ak"][64 * c:64 * c + 64, h, k0:k1], start=True, stop=True)
                elif what == "turn":
                    if c == 0:
                        pe.wait_ge(mixed, n + 1)
                    for b in range(c, min(c + 4, i + 2)):
                        key, kn = (0, META) if b == 0 else (META + P * (b - 1), P)
                        mm = pe.transpose(bank[0:kn, (b - c) * 128:(b - c + 1) * 128], probs[:, n % 2, 0, key:key + kn], ident)
                else:
                    pe.wait_ge(ring_read, u)
                    for b in range(i + 2):
                        kn = META if b == 0 else P
                        mm = pe.matmul(bank[:, 0:VA], probsT[0:kn, b, :], s["av"][0:kn, NT if b == 0 else b - 1, h * VA:(h + 1) * VA],
                                       start=b == 0, stop=b == i + 1)
                mm.then_inc(ring_full, 1)

            attend = Share(piece, bounds)
            pe.wait_ge(g2, 2)
            pe.matmul(solo[:, 0:G8], upper, graw, start=True, stop=True).then_inc(gc_full, 1)

            def prepare(j):
                t = TILES[j]
                r, c = rows(t), col0(t)
                for b in range(2):
                    if j >= 2:
                        pe.wait_ge(aqk_raw[b], j - 1)
                    for hh in range(4):
                        g = graw[0:r, t * HB + 2 * hh + b:t * HB + 2 * hh + b + 1].to_broadcast([r, P])
                        mm = pe.matmul(wide[b][:, hh * 128:hh * 128 + r], g, upper[0:r, 0:r], start=True, stop=True)
                    mm.then_inc(gcb_full[b], 1)
                attend()
                for b in range(2):
                    if j >= 1:
                        pe.wait_ge(r_done[b], j)
                    for hh in range(4):
                        kt = gk[64 * b:64 * b + 64, hh, c:c + r]
                        mm = pe.matmul(level_bank[b][0:r, hh * 128:hh * 128 + r], kt, kt, start=True, stop=True)
                    mm.then_inc(kk_full[b], 1)
                attend()
                for b in range(2):
                    pe.wait_ge(r1_done[b], j + 1)
                    for hh in range(4):
                        mm = pe.transpose(level_bank[b][0:r, hh * 128:hh * 128 + r], inv[0:r, j % 2, 2 * hh + b, 0:r], ident[0:r, 0:r])
                    mm.then_inc(t1_turned[b], 1)
                attend()

            def tokens(j):
                t = TILES[j]
                r, c = rows(t), col0(t)
                if j == 0:
                    pe.wait_ge(gates, 1)
                else:
                    pe.wait_ge(s_done, j)
                for hh in range(4):
                    mm = pe.transpose(solo[0:r, hh * 128:(hh + 1) * 128], gk[:, hh, c:c + r], ident)
                mm.then_inc(kt_turned, 1)
                attend()
                pe.wait_ge(kt_copied, j + 1)
                for hh in range(4):
                    mm = pe.transpose(solo[0:r, hh * 128:(hh + 1) * 128], gv[:, hh, c:c + r], ident)
                mm.then_inc(vt_turned, 1)
                attend()

            def query_key(j):
                c = col0(TILES[j])
                if j >= 2:
                    pe.wait_ge(o_done, j)
                for b in range(2):
                    for hh in range(4):
                        mm = pe.matmul(wide[b][:, hh * 128:(hh + 1) * 128], gk[64 * b:64 * b + 64, hh, c:c + P],
                                       gq[64 * b:64 * b + 64, hh, c:c + P], start=True, stop=True)
                    mm.then_inc(kq_full[b], 1)

            def level(j, lv):
                r, n = rows(TILES[j]), lev0(j) + lv
                last = lv == nlev(j)
                for b in range(2):
                    pe.wait_ge(bt_done[b], n)
                    if lv == 1:
                        pe.wait_ge(t1_copied[b], j + 1)
                    else:
                        pe.wait_ge(r_copied[b], turns_before(j, lv - 1))
                    for hh in range(4):
                        h = 2 * hh + b
                        mm = pe.matmul(level_bank[b][0:r, hh * 128:hh * 128 + r], bt[0:r, h, 0:r], tri[0:r, h, 0:r], start=True, stop=True)
                    mm.then_inc(x_full[b], 1)
                attend()
                for b in range(2):
                    pe.wait_ge(x_copied[b], n)
                    for hh in range(4):
                        h = 2 * hh + b
                        m0, m1 = (xm[0:r, h, 0:r], inv[0:r, j % 2, h, 0:r]) if last else (inv[0:r, j % 2, h, 0:r], xm[0:r, h, 0:r])
                        mm = pe.matmul(level_bank[b][0:r, hh * 128:hh * 128 + r], m0, m1, start=True, stop=True)
                    mm.then_inc(y_full[b], 1)
                attend()
                if not last:
                    for b in range(2):
                        pe.wait_ge(t_new[b], turns_before(j, lv))
                        for hh in range(4):
                            mm = pe.transpose(level_bank[b][0:r, hh * 128:hh * 128 + r], tri[0:r, 2 * hh + b, 0:r], ident[0:r, 0:r])
                        mm.then_inc(r_turned[b], 1)
                attend()

            def from_state(j):
                t = TILES[j]
                r, c = rows(t), col0(t)
                pe.wait_ge(s_done, j)
                if j + 1 < NJ:
                    pe.wait_ge(glc_done, j + 2)
                for src, o in ((gk, 0), (gq, 256)):
                    for hh in range(4):
                        for b in range(2):
                            mm = pe.matmul(wide[b][0:r, o + hh * DK:o + (hh + 1) * DK], src[64 * b:64 * b + 64, hh, c:c + r],
                                           state[64 * b:64 * b + 64, hh, :], start=True, stop=True)
                mm.then_inc(ks_full, 1)

            def solve(j):
                r = rows(TILES[j])
                if j >= 1:
                    pe.wait_ge(z_done, j)
                for b in range(2):
                    pe.wait_ge(r_done[b], j + 1)
                pe.wait_ge(vt_copied, j + 1)
                for h in range(HB):
                    z = vtok[0:r, h * DK:(h + 1) * DK] if j == 0 else zz[0:r, h * DK:(h + 1) * DK]
                    mm = pe.matmul(solo[0:r, h * DK:(h + 1) * DK], inv[0:r, j % 2, h, 0:r], z, start=True, stop=True)
                mm.then_inc(v_full, 1)

            def carry(j):
                r = rows(TILES[j])
                pe.wait_ge(vn_done, j + 1)
                if j >= 1:
                    for b in range(2):
                        pe.wait_ge(aqk_done[b], j)
                    for h in range(HB):
                        mm = pe.matmul(wide[h % 2][0:r, h // 2 * DK:h // 2 * DK + DK], aqk[0:r, h, 0:r], vn[0:r, h * DK:(h + 1) * DK],
                                       start=True, stop=True)
                    mm.then_inc(o2_full, 1)
                if j < NJ - 1:
                    pe.wait_ge(v2_done, j + 1)
                    for hh in range(4):
                        for b in range(2):
                            h = 2 * hh + b
                            mm = pe.matmul(solo[64 * b:64 * b + 64, hh * DK:(hh + 1) * DK], ktok[0:r, h * DK:(h + 1) * DK],
                                           v2[0:r, h * DK:(h + 1) * DK], start=True, stop=True)
                    mm.then_inc(s_full, 1)

            for j in range(NJ + 1):
                if j >= 1:
                    tokens(j - 1)
                if j < NJ:
                    prepare(j)
                    level(j, 1)
                if j >= 2:
                    from_state(j - 1)
                    attend()
                if j < NJ:
                    level(j, 2)
                if j >= 1:
                    solve(j - 1)
                    attend()
                if j < NJ:
                    level(j, 3)
                if j >= 1:
                    carry(j - 1)
                    attend()
                if 1 <= j < NJ:
                    level(j, 4)
                    query_key(j)
                    attend()
                    level(j, 5)
                    level(j, 6)

        phase.close()
        clear(nc, sems)


def output_and_route(nc, a, s):
    with ExitStack() as ctx, ExitStack() as phase:
        sb = lambda n, sh, dt=F32: ctx.enter_context(nc.sbuf_tensor(n, sh, dt))
        ps = lambda n, sh, dt=F32: ctx.enter_context(nc.psum_tensor(n, sh, dt))
        sems = []

        def sem(n):
            sems.append(ctx.enter_context(nc.semaphore(n)))
            return sems[-1]

        cst, mix, hres = s["cst"], s["mix"], s["hres"]
        ident = cst[:, C_ID:C_ID + 128]
        wout = s["wout"]
        mixT = sb("mixT", [P, 2, KD, P])
        uT = sb("u2T", [P, 2, KD, P])
        xr = sb("xr", [P, 2, D])
        u2 = sb("u2", [P, 2, D])
        scr = sb("scr", [P, D])
        gain = sb("ffn_gain", [P, D])
        wr = sb("wr", [P, KD, 36])
        rb = sb("rb", [P, 36])
        ss = sb("ss2", [P, NT, 3])
        lg = sb("lg", [P, NT, 36])
        big = lambda n: sb(n, [P, NT, NE])
        em, t1, t2, oh1, oh2, msum, mcum = (big(x) for x in ("em", "t1", "t2", "oh1", "oh2", "msum", "mcum"))
        sm = sb("sm", [P, 12, NT])
        g4, e4, goh = (sb(x, [P, NT, NG]) for x in ("g4", "e4", "goh"))
        tot = sb("tot", [P, NE])
        cmpn, ovc = sb("cmpn", [NE, 7]), sb("ovc", [NE, 1])
        base2, ovi = sb("base2", [P, NE]), sb("ovi", [P, NE])
        eob = sb("eob", [P, 16, NE])
        tabf = sb("tabf", [P, MAXBLK + 1])
        slf = sb("slf", [P, NT, 2])
        pmi, bmi = sb("pmi", [P, NT, 2], I32), sb("bmi", [P, NT, 2], I32)
        pmf, bmf = sb("pmf", [P, NT, 2]), sb("bmf", [P, NT, 2])
        ohp = s["region"][:, 0:2 * NT * P].rearrange("p (n s) -> p n s", s=P)
        ohb = s["region"][:, 2 * NT * P:2 * NT * (P + MAXBLK)].rearrange("p (n s) -> p n s", s=MAXBLK)
        gu, down = expert_slots(s)

        T, O, U = ([ps(f"{x}{i}", [P, 512]) for i in range(2)] for x in ("mT", "mO", "mU"))
        LGP, MISC = ps("LGP", [P, 512]), ps("MISC", [P, 512])
        w_first, x_in, gain_in, dve_seq = sem("w_first"), [sem(f"xr_in{i}") for i in range(2)], sem("gain_in"), sem("rdve_seq")
        m_turned, m_copied, o_full, h_done, sq_done, root, u_done, u_out = (
            sem(x) for x in ("m_turned", "m_copied", "o_full", "h_done", "sq2", "root2", "u_done", "u_out"))
        u_turned, uT_copied, lg_full, lg_done = (sem(x) for x in ("u_turned", "uT_copied", "lg_full", "lg_done"))
        ex_in, ex_done, p2_in, p2_done, m_done, rank_full, ovc_done, ov_full, oh_done, idx_full = (
            sem(x) for x in ("ex_in", "ex_done", "p2_in", "p2_done", "m_done", "rank_full", "ovc_done", "ov_full", "oh_done", "idx_full"))
        u_outs = [u_out, sem("u_out1")]

        block = phase.enter_context(nc.Block())

        @block.sync
        def _(sp):
            for t in range(NT):
                if t >= 2:
                    sp.wait_ge(h_done, 2 * (t - 1))
                sp.dma_start(xr[:, t % 2, :], a["x"][0, t * P:(t + 1) * P, :]).then_inc(x_in[t % 2], 16)
                if t == 1:
                    sp.dma_start(gain[:], a["norm_ffn"].to_broadcast([P, D])).then_inc(gain_in, 16)
                    with nc.allow_non_contiguous_dma(reason="router columns, 16 and 128 bytes a row"):
                        sp.dma_start(wr[:, :, 0:4], a["w_group"].rearrange("o (k p) c -> (o p) k c", p=P)).then_inc(gain_in, 16)
                        sp.dma_start(wr[:, :, 4:36], a["w_router"].rearrange("o (k p) c -> (o p) k c", p=P)).then_inc(gain_in, 16)
                    sp.dma_start(rb[:, 0:4], a["b_group"].to_broadcast([P, 4])).then_inc(gain_in, 16)
                    sp.dma_start(rb[:, 4:36], a["b_router"].to_broadcast([P, 32])).then_inc(gain_in, 16)
                if t >= 1:
                    sp.wait_ge(u_done, t)
                    sp.dma_start(a["u2"][(t - 1) * P:t * P, :], u2[:, (t - 1) % 2, :]).then_inc(u_outs[(t - 1) % 2], 16)
                if t in (2, 3):
                    load_gate_up(sp, a, gu[t - 2], t - 2, w_first)
                elif t in (4, 5):
                    load_down(sp, a, down[t - 4], t - 4, w_first)
            sp.wait_ge(u_done, NT)
            sp.dma_start(a["u2"][(NT - 1) * P:NT * P, :], u2[:, (NT - 1) % 2, :]).then_inc(u_outs[(NT - 1) % 2], 16)
            for b in range(2):
                sp.wait_ge(u_outs[b], 16 * NT // 2)
            sp.wait_ge(w_first, 96)

        @block.scalar
        def _(act):
            def turned_mix(t):
                for half in range(2):
                    act.wait_ge(m_turned, 2 * t + half + 1)
                    if t >= 2:
                        act.wait_ge(o_full, 2 * (t - 1))
                    act.activation(mixT[:, t % 2, 4 * half:4 * half + 4, :], T[half][:], ACT.Copy).then_inc(m_copied, 1)

            def statistics(t):
                act.wait_ge(h_done, 2 * t + 2)
                if t >= 1:
                    act.wait_ge(sq_done, t)
                act.activation(scr[:], hres[:, t, :], ACT.Square, accum_out=ss[:, t, 0:1]).then_inc(sq_done, 1)
                act.wait_ge(sq_done, t + 1)
                act.activation(ss[:, t, 1:2], ss[:, t, 0:1], ACT.Sqrt, bias=cst[:, C_EPS:C_EPS + 1], scale=1.0 / D).then_inc(root, 1)

            def turned_u(t):
                for half in range(2):
                    act.wait_ge(u_turned, 2 * t + half + 1)
                    if t >= 2:
                        act.wait_ge(lg_full, t - 1)
                    act.activation(uT[:, t % 2, 4 * half:4 * half + 4, :], U[half][:], ACT.Copy).then_inc(uT_copied, 1)

            act.wait_ge(gain_in, 80)
            for t in range(NT + 1):
                if t < NT:
                    turned_mix(t)
                if t >= 1:
                    turned_u(t - 1)
                if t < NT:
                    statistics(t)
            act.wait_ge(ex_in, 1)
            act.activation(e4[:], e4[:], ACT.Exp).then_inc(ex_done, 1)
            act.wait_ge(p2_in, 1)
            act.activation(sm[:, 8, :], sm[:, 8, :], ACT.Exp).then_inc(p2_done, 1)

        @block.vector
        def _(dve):
            seq = Seq(dve, dve_seq)

            def logits(t):
                dve.wait_ge(lg_full, t + 1)
                dve.tensor_tensor(lg[:, t, :], LGP[:, 0:36], rb[:], ALU.add).then_inc(lg_done, 1)

            seq(dve.memset(s["idx"][:], -1))
            dve.wait_ge(gain_in, 80)
            for t in range(NT):
                dve.wait_ge(x_in[t % 2], 16 * (t // 2 + 1))
                for half in range(2):
                    dve.wait_ge(o_full, 2 * t + half + 1)
                    c = slice(512 * half, 512 * half + 512)
                    dve.tensor_tensor(hres[:, t, c], O[half][:], xr[:, t % 2, c], ALU.add).then_inc(h_done, 1)
                dve.wait_ge(root, t + 1)
                seq(dve.reciprocal(ss[:, t, 2:3], ss[:, t, 1:2]))
                if t >= 2:
                    dve.wait_ge(u_outs[t % 2], 16 * (t // 2))
                    dve.wait_ge(u_turned, 2 * (t - 1))
                dve.scalar_tensor_tensor(u2[:, t % 2, :], hres[:, t, :], ss[:, t, 2:3], gain[:], ALU.mult, ALU.mult).then_inc(u_done, 1)
                if t >= 1:
                    logits(t - 1)
            logits(NT - 1)
            dve.wait_ge(lg_done, NT)

            bc = lambda v, n: v.unsqueeze(2).to_broadcast([P, NT, n])
            row = lambda c, n: cst[:, c:c + n].unsqueeze(1).to_broadcast([P, NT, n])
            m = lambda i: sm[:, i, :]

            def first_max(values, n, top, onehot, work):
                seq(dve.tensor_reduce(top, values, AX.X, ALU.max))
                seq(dve.tensor_tensor(work, values, bc(top, n), ALU.is_equal))
                seq(dve.tensor_tensor(work, work, row(C_IG, n), ALU.mult))
                seq(dve.tensor_reduce(m(11), work, AX.X, ALU.min))
                seq(dve.tensor_tensor(onehot, row(C_IG, n), bc(m(11), n), ALU.is_equal))

            first_max(lg[:, :, 0:NG], NG, m(0), goh[:], g4[:])
            dve.tensor_tensor(e4[:], lg[:, :, 0:NG], bc(m(0), NG), ALU.subtract).then_inc(ex_in, 1)
            seq(dve.tensor_scalar(g4[:], goh[:], BIG, -BIG, ALU.mult, ALU.add))
            groups = lambda v: v.rearrange("p t (g e) -> p (t g) e", g=NG)
            wide = lambda v: v[:].rearrange("p t g -> p (t g)").unsqueeze(2).to_broadcast([P, NT * NG, EPG])
            seq(dve.tensor_copy(em[:], lg[:, :, NG:NG + NE]))
            seq(dve.tensor_tensor(groups(em[:]), groups(em[:]), wide(goh), ALU.mult))
            seq(dve.tensor_tensor(groups(em[:]), groups(em[:]), wide(g4), ALU.add))
            first_max(em[:], NE, m(1), oh1[:], t1[:])
            seq(dve.scalar_tensor_tensor(em[:], oh1[:], -2.0 * BIG, em[:], ALU.mult, ALU.add))
            first_max(em[:], NE, m(2), oh2[:], t1[:])
            dve.tensor_tensor(m(8), m(2), m(1), ALU.subtract).then_inc(p2_in, 1)
            dve.wait_ge(ex_done, 1)
            seq(dve.tensor_reduce(m(3), e4[:], AX.X, ALU.add))
            seq(dve.reciprocal(m(4), m(3)))
            dve.wait_ge(p2_done, 1)
            seq(dve.tensor_scalar(m(5), m(8), 1.0, None, ALU.add))
            seq(dve.reciprocal(m(6), m(5)))
            seq(dve.tensor_tensor(s["wts"][:, 0, :], m(4), m(6), ALU.mult))
            seq(dve.tensor_tensor(s["wts"][:, 1, :], s["wts"][:, 0, :], m(8), ALU.mult))
            seq(dve.tensor_tensor(msum[:], oh1[:], oh2[:], ALU.add))
            seq(dve.memset(mcum[:, 0, :], 0.0))
            for t in range(1, NT):
                seq(dve.tensor_tensor(mcum[:, t, :], mcum[:, t - 1, :], msum[:, t - 1, :], ALU.add))
            dve.tensor_tensor(tot[:], mcum[:, NT - 1, :], msum[:, NT - 1, :], ALU.add).then_inc(m_done, 1)
            dve.wait_ge(rank_full, 1)
            seq(dve.tensor_tensor(cmpn[:], T[1][0:NE, 0:1].to_broadcast([NE, 7]), cst[0:NE, C_E128 + 1:C_E128 + 8], ALU.is_gt))
            dve.tensor_reduce(ovc[:], cmpn[:], AX.X, ALU.add).then_inc(ovc_done, 1)
            rank = t1[:]
            seq(dve.tensor_copy(rank, T[0][:, 0:NT * NE].rearrange("p (t e) -> p t e", t=NT)))
            dve.wait_ge(ov_full, 1)
            seq(dve.tensor_scalar(base2[:], O[0][:, 0:NE], 128.0, 31.0 * 128.0, ALU.mult, ALU.add))
            seq(dve.tensor_tensor(base2[:], base2[:], cst[:, C_E128:C_E128 + NE], ALU.subtract))
            seq(dve.tensor_copy(ovi[:], O[0][:, NE:2 * NE]))
            seq(dve.tensor_scalar(t2[:], rank, 128.0, None, ALU.is_ge))
            seq(dve.tensor_tensor(t2[:], t2[:], base2[:].unsqueeze(1).to_broadcast([P, NT, NE]), ALU.mult))
            seq(dve.tensor_tensor(t2[:], t2[:], rank, ALU.add))
            seq(dve.tensor_tensor(t2[:], t2[:], row(C_E128, NE), ALU.add))
            for c, oh in enumerate((oh1, oh2)):
                seq(dve.tensor_tensor(em[:], t2[:], oh[:], ALU.mult))
                seq(dve.tensor_reduce(slf[:, :, c], em[:], AX.X, ALU.add))
            seq(dve.tensor_copy(s["slot"][:], slf[:]))
            seq(dve.tensor_scalar(pmi[:], s["slot"][:], 127, None, ALU.bitwise_and))
            seq(dve.tensor_scalar(bmi[:], s["slot"][:], 7, None, ALU.arith_shift_right))
            seq(dve.tensor_copy(pmf[:], pmi[:]))
            seq(dve.tensor_copy(bmf[:], bmi[:]))
            grid = lambda v, n: v.rearrange("p t c -> p (t c)").unsqueeze(2).to_broadcast([P, 2 * NT, n])
            step = lambda c, n: cst[:, c:c + n].unsqueeze(1).to_broadcast([P, 2 * NT, n])
            seq(dve.tensor_tensor(ohb, step(C_IOTA, MAXBLK), grid(bmf[:], MAXBLK), ALU.is_equal))
            seq(dve.tensor_tensor(ohb, ohb, cst[:, C_TOK:C_TOK + 2 * NT].unsqueeze(2).to_broadcast([P, 2 * NT, MAXBLK]), ALU.mult))
            seq(dve.tensor_tensor(ohp, step(C_IOTA, P), grid(pmf[:], P), ALU.is_equal))
            dve.sem_inc(oh_done, 1)
            io = cst[:, C_IOTA:C_IOTA + 16].unsqueeze(2).to_broadcast([P, 16, NE])
            seq(dve.tensor_tensor(eob[:], ovi[:].unsqueeze(1).to_broadcast([P, 16, NE]), io, ALU.is_le))
            seq(dve.tensor_copy(tabf[:, 0:32], cst[:, C_IOTA:C_IOTA + 32]))
            seq(dve.tensor_reduce(tabf[:, 32:48], eob[:], AX.X, ALU.add))
            seq(dve.tensor_scalar(tabf[:, 32:48], tabf[:, 32:48], 31.0, None, ALU.min))
            seq(dve.tensor_scalar(tabf[:, 48:49], ovi[:, NE - 1:NE], 33.0, None, ALU.add))
            seq(dve.tensor_copy(s["table"][:], tabf[:]))
            seq(dve.tensor_scalar(s["table"][:, 48:49], s["table"][:, 48:49], 1, None, ALU.arith_shift_right))
            dve.wait_ge(idx_full, 1)
            seq(dve.tensor_scalar(tabf[:, 0:MAXBLK], U[0][:, 0:MAXBLK], -1.0, None, ALU.add))
            seq(dve.tensor_copy(s["idx"][:, 0, 0:MAXBLK], tabf[:, 0:MAXBLK]))
            seq(dve.tensor_scalar(s["idx"][:, 1, :], s["idx"][:, 0, :], 1, None, ALU.arith_shift_right))

        @block.tensor
        def _(pe):
            def turn_mix(t):
                for half in range(2):
                    if t >= 1:
                        pe.wait_ge(m_copied, 2 * t - 1 + half)
                    for kk in range(4):
                        kx = 4 * half + kk
                        mm = pe.transpose(T[half][:, kk * P:(kk + 1) * P], mix[:, t, kx * P:(kx + 1) * P], ident)
                    mm.then_inc(m_turned, 1)

            def out_proj(t):
                pe.wait_ge(m_copied, 2 * t + 2)
                for half in range(2):
                    if t >= 1:
                        pe.wait_ge(h_done, 2 * t - 1 + half)
                    for kx in range(KD):
                        mm = pe.matmul(O[half][:], mixT[:, t % 2, kx, :], wout[:, kx, 512 * half:512 * half + 512], start=kx == 0, stop=kx == KD - 1)
                    mm.then_inc(o_full, 1)

            def turn_u(t):
                pe.wait_ge(u_done, t + 1)
                for half in range(2):
                    if t >= 1:
                        pe.wait_ge(uT_copied, 2 * t - 1 + half)
                    for kk in range(4):
                        kx = 4 * half + kk
                        mm = pe.transpose(U[half][:, kk * P:(kk + 1) * P], u2[:, t % 2, kx * P:(kx + 1) * P], ident)
                    mm.then_inc(u_turned, 1)

            def router(t):
                pe.wait_ge(uT_copied, 2 * t + 2)
                if t >= 1:
                    pe.wait_ge(lg_done, t)
                for kx in range(KD):
                    mm = pe.matmul(LGP[:, 0:36], uT[:, t % 2, kx, :], wr[:, kx, :], start=kx == 0, stop=kx == KD - 1)
                mm.then_inc(lg_full, 1)

            turn_mix(0)
            pe.wait_ge(gain_in, 80)
            for t in range(NT + 1):
                if t + 1 < NT:
                    turn_mix(t + 1)
                if t < NT:
                    out_proj(t)
                if t >= 1:
                    turn_u(t - 1)
                    router(t - 1)
            pe.wait_ge(m_done, 1)
            pe.wait_ge(m_copied, 2 * NT)
            ones = cst[:, C_ONE:C_ONE + P]
            pe.matmul(T[0][:, 0:NT * NE], cst[:, C_SUP:C_SUP + P], msum[:].rearrange("p t e -> p (t e)"), start=True, stop=False)
            pe.matmul(T[0][:, 0:NT * NE], ones, mcum[:].rearrange("p t e -> p (t e)"), start=False, stop=True)
            pe.matmul(T[1][0:NE, 0:1], tot[:], cst[:, C_ONE:C_ONE + 1], start=True, stop=True).then_inc(rank_full, 1)
            pe.wait_ge(ovc_done, 1)
            lhs = ovc[:].to_broadcast([NE, P])
            pe.matmul(O[0][:, 0:NE], lhs, cst[0:NE, C_SUP:C_SUP + NE], start=True, stop=True)
            pe.matmul(O[0][:, NE:2 * NE], lhs, cst[0:NE, C_UP:C_UP + NE], start=True, stop=True).then_inc(ov_full, 1)
            pe.wait_ge(oh_done, 1)
            for n in range(2 * NT):
                mm = pe.matmul(U[0][:, 0:MAXBLK], ohp[:, n, :], ohb[:, n, :], start=n == 0, stop=n == 2 * NT - 1)
            mm.then_inc(idx_full, 1)

        phase.close()
        clear(nc, sems)


def expert_slots(s):
    flat, n = s["gqkv"][:].rearrange("p m l -> p (m l)"), KD * 2 * FE + 2 * D
    store = [flat[:, n * u:n * u + n] for u in range(2)]
    return ([w[:, 0:KD * 2 * FE].rearrange("p (k g f) -> p k g f", k=KD, g=2) for w in store],
            [w[:, KD * 2 * FE:].rearrange("p (k c) -> p k c", k=2) for w in store])


def load_gate_up(sp, a, dst, e, signal):
    for g, w in enumerate(("w_gate", "w_up")):
        v = a[w].rearrange("o e (p k) f -> (o e) p k f", k=KD)
        sp.dma_start(dst[:, :, g, :], v[bass.ds(e, 1)].rearrange("o p k f -> (o p) k f")).then_inc(signal, 16)


def load_down(sp, a, dst, e, signal):
    v = a["w_down"].rearrange("o e (p k) c -> (o e) p k c", k=2)
    sp.dma_start(dst, v[bass.ds(e, 1)].rearrange("o p k c -> (o p) k c")).then_inc(signal, 16)


def experts(nc, a, s):
    with ExitStack() as ctx, ExitStack() as phase:
        sb = lambda n, sh, dt=F32: ctx.enter_context(nc.sbuf_tensor(n, sh, dt))
        ps = lambda n, sh, dt=F32: ctx.enter_context(nc.psum_tensor(n, sh, dt))
        sems = []

        def sem(n):
            sems.append(ctx.enter_context(nc.semaphore(n)))
            return sems[-1]

        sem2 = lambda n: [sem(f"{n}{b}") for b in range(2)]
        ident = s["cst"][:, C_ID:C_ID + 128]
        gu, down = expert_slots(s)
        xg, xT, yb = sb("xg", [P, 2, D]), sb("xT", [P, 2, KD, P]), sb("yb", [P, 2, D])
        sg, hb, hT = sb("sg", [P, 2, FE]), sb("hb", [P, 2, FE]), sb("hT", [P, 2, 2, P])
        cur = sb("cur", [P, 2, 2], I32)
        XY = [[ps(f"XY{u}{half}", [P, 512]) for half in range(2)] for u in range(2)]
        GU = [ps(f"GU{u}", [P, 512]) for u in range(2)]
        HT = [ps(f"HT{u}", [P, 512]) for u in range(2)]
        w_in, d_in, cur_done, x_in, x_turned, xT_act, xT_dve, gu_full, silu_done, h_done, h_turned, hT_done, y_full, y_act, y_dve, y_out = (
            sem2(x) for x in ("ew_in", "ed_in", "cur_done", "ex_in_", "ex_turned", "xT_act", "xT_dve", "gu_full", "esilu", "eh_done",
                              "eh_turned", "ehT_done", "ey_full", "ey_act", "ey_dve", "ey_out"))
        wait = lambda eng, x, v: None if isinstance(v, int) and v == 0 else eng.wait_ge(x, v)
        go_pool, x_clear, cur2_done = sem("go_pool"), sem("x_clear"), sem2("cur2_done")
        pairs = lambda eng: eng.value_load(s["table"][0:1, 48:49], min_val=16, max_val=24)

        block = phase.enter_context(nc.Block())

        @block.sync
        def _(sp):
            with sp.Fori(1, pairs(sp)) as i:
                experts_of = [sp.value_load(s["table"][0:1, bass.ds(2 * i + u, 1)], min_val=0, max_val=NE - 1) for u in range(2)]
                for u, e in enumerate(experts_of):
                    sp.wait_ge(gu_full[u], i)
                    load_gate_up(sp, a, gu[u], e, w_in[u])
                for u, e in enumerate(experts_of):
                    sp.wait_ge(y_full[u], 2 * i)
                    load_down(sp, a, down[u], e, d_in[u])

        @block.gpsimd
        def _(pool):
            rows_of = lambda u, c: bass.IndirectOffsetOnAxis(ap=cur[:, u, c:c + 1].bitcast(U32), axis=0)

            def gather(i, j):
                for u in range(2):
                    wait(pool, x_in[u], 16 * i)
                    pool.tensor_copy(cur[:, u, 0:1], s["idx"][:, 1, bass.ds(2 * j + u, 1)]).then_inc(cur_done[u], 1)
                    pool.wait_ge(cur_done[u], j + 1)
                    wait(pool, x_turned[u], 2 * i)
                    pool.sem_inc(go_pool, 1)
                    pool.indirect_dma_start(out=xg[:, u, :], out_offset=None, in_=a["u2"], in_offset=rows_of(u, 0),
                                            bounds_check=SEQ - 1, oob_is_err=False).then_inc(x_in[u], 16)

            def scatter(i):
                for u in range(2):
                    wait(pool, y_out[u], 16 * i)
                    pool.tensor_copy(cur[:, u, 1:2], s["idx"][:, 0, bass.ds(2 * i + u, 1)]).then_inc(cur2_done[u], 1)
                    pool.wait_ge(cur2_done[u], i + 1)
                    pool.wait_ge(y_act[u], i + 1)
                    pool.wait_ge(y_dve[u], i + 1)
                    pool.sem_inc(go_pool, 1)
                    pool.indirect_dma_start(out=a["ys"], out_offset=rows_of(u, 1), in_=yb[:, u, :], in_offset=None,
                                            bounds_check=2 * SEQ - 1, oob_is_err=False).then_inc(y_out[u], 16)

            pool.wait_ge(x_clear, 1)
            gather(0, 0)
            gather(1, 1)
            scatter(0)
            n = pairs(pool)
            with pool.Fori(1, n) as i:
                gather(i + 1, i + 1)
                scatter(i)
            for u in range(2):
                pool.wait_ge(y_out[u], 16 * n)
                pool.wait_ge(x_in[u], 16 * n + 16)
            pool.sem_inc(go_pool, 1)

        @block.scalar
        def _(act):
            def turn(i):
                for u in range(2):
                    act.wait_ge(x_turned[u], 2 * i + 1)
                    act.activation(xT[:, u, 0:4, :], XY[u][0][:], ACT.Copy).then_inc(xT_act[u], 1)
                for u in range(2):
                    act.wait_ge(gu_full[u], i + 1)
                    act.activation(sg[:, u, :], GU[u][:, 0:FE], ACT.Silu).then_inc(silu_done[u], 1)
                for u in range(2):
                    act.wait_ge(h_turned[u], i + 1)
                    act.activation(hT[:, u], HT[u][:, 0:2 * P], ACT.Copy).then_inc(hT_done[u], 1)
                for u in range(2):
                    act.wait_ge(y_full[u], 2 * i + 1)
                    wait(act, y_out[u], 16 * i)
                    act.activation(yb[:, u, 0:512], XY[u][0][:], ACT.Copy).then_inc(y_act[u], 1)

            turn(0)
            with act.Fori(1, pairs(act)) as i:
                turn(i)

        @block.vector
        def _(dve):
            dve.memset(xg[:], 0.0).then_inc(x_clear, 1)
            def turn(i):
                for u in range(2):
                    dve.wait_ge(x_turned[u], 2 * i + 2)
                    dve.tensor_copy(xT[:, u, 4:8, :], XY[u][1][:].rearrange("p (k t) -> p k t", k=4)).then_inc(xT_dve[u], 1)
                for u in range(2):
                    dve.wait_ge(silu_done[u], i + 1)
                    dve.tensor_tensor(hb[:, u, :], GU[u][:, FE:2 * FE], sg[:, u, :], ALU.mult).then_inc(h_done[u], 1)
                for u in range(2):
                    dve.wait_ge(y_full[u], 2 * i + 2)
                    wait(dve, y_out[u], 16 * i)
                    dve.tensor_copy(yb[:, u, 512:1024], XY[u][1][:]).then_inc(y_dve[u], 1)

            turn(0)
            with dve.Fori(1, pairs(dve)) as i:
                turn(i)

        @block.tensor
        def _(pe):
            def turn(i):
                for u in range(2):
                    pe.wait_ge(x_in[u], 16 * i + 16)
                    for half in range(2):
                        wait(pe, (y_act if half == 0 else y_dve)[u], i)
                        for kk in range(4):
                            kx = 4 * half + kk
                            mm = pe.transpose(XY[u][half][:, kk * P:(kk + 1) * P], xg[:, u, kx:D:KD], ident)
                        mm.then_inc(x_turned[u], 1)
                for u in range(2):
                    wait(pe, w_in[u], 32 * i)
                    pe.wait_ge(xT_act[u], i + 1)
                    pe.wait_ge(xT_dve[u], i + 1)
                    wait(pe, h_done[u], i)
                    for kx in range(KD):
                        mm = pe.matmul(GU[u][:], xT[:, u, kx, :], gu[u][:, kx, :, :], start=kx == 0, stop=kx == KD - 1)
                    mm.then_inc(gu_full[u], 1)
                for u in range(2):
                    pe.wait_ge(h_done[u], i + 1)
                    wait(pe, hT_done[u], i)
                    for kx in range(2):
                        mm = pe.transpose(HT[u][:, kx * P:(kx + 1) * P], hb[:, u, kx:FE:2], ident)
                    mm.then_inc(h_turned[u], 1)
                for u in range(2):
                    pe.wait_ge(hT_done[u], i + 1)
                    wait(pe, d_in[u], 16 * i)
                    for half in range(2):
                        for kx in range(2):
                            mm = pe.matmul(XY[u][half][:], hT[:, u, kx, :], down[u][:, kx, 512 * half:512 * half + 512], start=kx == 0, stop=kx == 1)
                        mm.then_inc(y_full[u], 1)

            turn(0)
            with pe.Fori(1, pairs(pe)) as i:
                turn(i)

        phase.close()
        clear(nc, sems)


def combine(nc, a, s):
    with ExitStack() as ctx:
        sb = lambda n, sh, dt=F32: ctx.enter_context(nc.sbuf_tensor(n, sh, dt))
        sem = lambda n: ctx.enter_context(nc.semaphore(n))
        RB = 3
        cst, hres = s["cst"], s["hres"]
        y = sb("yc", [P, RB, 2, D])
        ob = sb("ob", [P, 2, D])
        scr, gain, ss = sb("cscr", [P, D]), sb("fgain", [P, D]), sb("ss3", [P, NT, 3])
        gain_in, seq_s, sq, root = sem("fgain_in"), sem("cseq"), sem("csq"), sem("croot")
        y_in, added, o_done, o_out = [sem(f"y_in{b}") for b in range(RB)], sem("cadded"), sem("co_done"), [sem(f"co_out{b}") for b in range(2)]

        block = ctx.enter_context(nc.Block())

        @block.sync
        def _(sp):
            sp.dma_start(gain[:], a["norm_final"].rearrange("(o d) -> o d", o=1).to_broadcast([P, D])).then_inc(gain_in, 16)
            def put(t):
                sp.wait_ge(o_done, t + 1)
                sp.dma_start(a["out"][0, t * P:(t + 1) * P, :], ob[:, t % 2, :]).then_inc(o_out[t % 2], 16)

            for t in range(NT):
                if t >= RB:
                    sp.wait_ge(added, t - RB + 1)
                sp.dma_start(y[:, t % RB, :, :], a["ys"].rearrange("(t p c) d -> t p c d", c=2, p=P)[t]).then_inc(y_in[t % RB], 16)
                if t < RB - 1:
                    continue
                put(t - RB + 1)
            for t in range(NT - RB + 1, NT):
                put(t)
            for b in range(2):
                sp.wait_ge(o_out[b], 16 * NT // 2)

        @block.scalar
        def _(act):
            for t in range(NT):
                act.wait_ge(added, t + 1)
                if t >= 1:
                    act.wait_ge(sq, t)
                act.activation(scr[:], hres[:, t, :], ACT.Square, accum_out=ss[:, t, 0:1]).then_inc(sq, 1)
                act.wait_ge(sq, t + 1)
                act.activation(ss[:, t, 1:2], ss[:, t, 0:1], ACT.Sqrt, bias=cst[:, C_EPS:C_EPS + 1], scale=1.0 / D).then_inc(root, 1)

        @block.vector
        def _(dve):
            seq = Seq(dve, seq_s)

            def finish(t):
                dve.wait_ge(root, t + 1)
                seq(dve.reciprocal(ss[:, t, 2:3], ss[:, t, 1:2]))
                if t >= 2:
                    dve.wait_ge(o_out[t % 2], 16 * (t // 2))
                dve.scalar_tensor_tensor(ob[:, t % 2, :], hres[:, t, :], ss[:, t, 2:3], gain[:], ALU.mult, ALU.mult).then_inc(o_done, 1)

            dve.wait_ge(gain_in, 16)
            for t in range(NT):
                dve.wait_ge(y_in[t % RB], 16 * (t // RB + 1))
                h = hres[:, t, :]
                seq(dve.scalar_tensor_tensor(h, y[:, t % RB, 0, :], s["wts"][:, 0, t:t + 1], h, ALU.mult, ALU.add))
                dve.scalar_tensor_tensor(h, y[:, t % RB, 1, :], s["wts"][:, 1, t:t + 1], h, ALU.mult, ALU.add).then_inc(added, 1)
                if t >= 1:
                    finish(t - 1)
            finish(NT - 1)


def build(nc, a):
    with ExitStack() as ctx:
        sb = lambda n, sh, dt=F32: ctx.enter_context(nc.sbuf_tensor(n, sh, dt))
        a["z"] = nc.dram_tensor("z_dram", (NT, P, BLK), F32, kind="Internal").ap()
        a["u2"] = nc.dram_tensor("u2_dram", (SEQ, D), F32, kind="Internal").ap()
        a["ys"] = nc.dram_tensor("ys_dram", (SEQ * 2, D), F32, kind="Internal").ap()
        s = {
            "cst": sb("cst", [P, C_N]), "cols": sb("cols", [P, 64]), "gqkv": sb("gqkv", [P, 12, L]),
            "region": sb("region", [P, HA * SEQ + HA * L + (NT + 1) * HA * VA]), "ab": sb("ab", [P, NT + 1, 16]),
            "wts": sb("wts", [P, 2, NT]), "slot": sb("slot", [P, NT, 2], I32), "idx": sb("idx", [P, 2, MAXBLK + 2], I32),
            "table": sb("table", [P, MAXBLK + 1], I32),
        }
        s["gq"], s["gk"], s["gv"] = (s["gqkv"][:, 4 * i:4 * i + 4, :] for i in range(3))
        reg, e1, e2 = s["region"], HA * SEQ, HA * (SEQ + L)
        s["aq"] = reg[:, 0:e1].rearrange("p (h t) -> p h t", h=HA)
        s["ak"] = reg[:, e1:e2].rearrange("p (h t) -> p h t", h=HA)
        s["av"] = reg[:, e2:].rearrange("p (t c) -> p t c", t=NT + 1)
        project(nc, a, s)
        s["mix"] = sb("mix", [P, NT, D])
        s["wout"] = reg[:, NT * 512:NT * 512 + KD * D].rearrange("p (k c) -> p k c", k=KD)
        mixers(nc, a, s)
        s["hres"] = s["mix"][:]
        output_and_route(nc, a, s)
        experts(nc, a, s)
        combine(nc, a, s)


_INS = ["x", "meta", "norm_mix", "w_in", "lambda_q1", "lambda_k1", "lambda_q2", "lambda_k2", "diff_norm", "conv_w",
        "a_log", "dt_bias", "gdn_norm", "w_out", "norm_ffn", "w_group", "b_group", "w_router", "b_router",
        "w_gate", "w_up", "w_down", "norm_final"]


def kernel(**inputs):
    import concourse.bacc as _bacc
    from concourse.bass_utils import run_bass_kernel_spmd as _run

    nc = _bacc.Bacc("TRN2", target_bir_lowering=False, num_devices=1)
    arrays = {"in_consts": constants()}
    arrays.update({f"in_{n}": np.ascontiguousarray(inputs[n]) for n in _INS})
    a = {n[3:]: nc.dram_tensor(n, v.shape, F32, kind="ExternalInput").ap() for n, v in arrays.items()}
    a["out"] = nc.dram_tensor("out_0", (1, SEQ, D), F32, kind="ExternalOutput").ap()
    build(nc, a)
    r = _run(nc, [arrays], core_ids=[0])
    return r.results[0]["out_0"]
```

```python
from contextlib import ExitStack

import numpy as np

import concourse.bass as bass
from concourse import mybir

F32 = mybir.dt.float32
F32R = mybir.dt.float32r
I32 = mybir.dt.int32
U32 = mybir.dt.uint32
ALU = mybir.AluOpType
ACT = mybir.ActivationFunctionType
AX = mybir.AxisListType

P = 128
D = 1024
KD = D // P
SEQ = 1024
META = 16
L = SEQ + META
NT = SEQ // P
EPS = 1e-6
HA = 4
HB = 8
DK = 64
VA = 128
LAM_INIT = 0.8 - 0.6
BLK = 256
PASSES = [(0, 0), (0, 1), (1, 0)]
COL_QA, COL_KA, COL_VA, COL_QKVB, COL_ZB, COL_AB = 0, 512, 1024, 1536, 3072, 3584
NE, NG, EPG, FE = 32, 4, 8, 256
MAXBLK = 48
BIG = 1.0e30
PREPARE_SHARE = [2, 3, 2]
LEVEL_SHARE = [1, 1, 1]
FIRST_SHARE = [1, 1, 1]
TOKENS_SHARE = [1, 1]
SCALE_WEIGHT = 200
FREE_STEPS = 8
LEVELS = 7

C_ID, C_UP, C_SUP, C_BLK, C_LEV = 0, 128, 256, 384, 512
C_IOTA = C_LEV + LEVELS * 128
C_TOK = C_IOTA + 128
C_E128 = C_TOK + 2 * NT
C_ONE = C_E128 + 32
C_IG = C_ONE + 128
C_EPS = C_IG + 32
C_N = C_EPS + 1
R_SIN = (NT + 1) * 64
R_N = 2 * R_SIN


def constants():
    c = np.zeros((P, C_N + R_N), np.float32)
    p = np.arange(P)
    c[:, C_ID:C_ID + 128] = np.eye(P)
    c[:, C_UP:C_UP + 128] = p[:, None] <= p[None, :]
    c[:, C_SUP:C_SUP + 128] = p[:, None] < p[None, :]
    c[:, C_BLK:C_BLK + 128] = (p[:, None] // 64) == (p[None, :] // 64)
    for lv in range(LEVELS):
        s = 1 << lv
        same = (p[:, None] // (2 * s)) == (p[None, :] // (2 * s))
        c[:, C_LEV + lv * 128:C_LEV + (lv + 1) * 128] = same & (p[:, None] // s % 2 == 0) & (p[None, :] // s % 2 == 1)
    inv = (10000.0 ** (-np.arange(0, 64, 2) / 64.0)).astype(np.float32)
    for t in range(NT + 1):
        pos = (np.arange(P) + (META + P * t if t < NT else 0)).astype(np.float32)
        ang = pos[:, None] * inv[None, :]
        co, si = np.cos(ang), np.sin(ang)
        c[:, C_N + 64 * t:C_N + 64 * t + 64] = np.concatenate([co, co], 1)
        c[:, C_N + R_SIN + 64 * t:C_N + R_SIN + 64 * t + 64] = np.concatenate([-si, si], 1)
    c[:, C_IOTA:C_IOTA + 128] = p[None, :]
    c[:, C_TOK:C_TOK + 2 * NT] = 2 * (p[:, None] + P * (np.arange(2 * NT) // 2)[None, :]) + np.arange(2 * NT)[None, :] % 2 + 1
    c[:, C_E128:C_E128 + 32] = 128 * np.arange(32)[None, :]
    c[:, C_ONE:C_ONE + 128] = 1.0
    c[:, C_IG:C_IG + 32] = np.arange(32)[None, :] - 1000.0
    c[:, C_EPS] = EPS
    return c


def rows(t):
    return P if t < NT else META


def col0(t):
    return META + P * t if t < NT else 0


class Seq:

    def __init__(self, eng, sem):
        self.eng, self.sem, self.n = eng, sem, 0

    def __call__(self, ins):
        self.n += 1
        ins.then_inc(self.sem, 1)
        self.eng.wait_ge(self.sem, self.n)


def clear(nc, sems):
    with nc.Block() as block:
        @block.gpsimd
        def _(pool):
            for x in sems:
                pool.sem_clear(x)


def split_place(nc, stack, name):
    return [stack.enter_context(nc.sbuf_tensor(f"split_{name}_{x}", [P, KD, BLK], F32R)) for x in ("hi", "lo")]


def project(nc, a, s):
    with ExitStack() as ctx, ExitStack() as phase:
        sb = lambda n, sh, dt=F32: ctx.enter_context(nc.sbuf_tensor(n, sh, dt))
        ps = lambda n, sh, dt=F32: ctx.enter_context(nc.psum_tensor(n, sh, dt))
        sems = []

        def sem(n):
            sems.append(ctx.enter_context(nc.semaphore(n)))
            return sems[-1]

        cst, cols = s["cst"], s["cols"]
        ident = cst[:, C_ID:C_ID + 128]
        region = s["region"]
        uT = [sb(f"uT_{x}", [P, KD, L], F32R) for x in ("hi", "lo")]
        rowsb = sb("rowsb", [64, 128])
        ss = sb("ss", [P, NT + 1, 3])
        raw = sb("raw", [P, KD, BLK])
        wab, wab_r = sb("wab", [P, KD, 16]), [sb(f"wab_{x}", [P, KD, 16], F32R) for x in ("hi", "lo")]
        with ExitStack() as shared:
            split_in_conv = split_place(nc, shared, "conv")
        conv_space = sb("conv_space", [P, 4 * L + 3])
        cv, work = conv_space[:, 0:L], conv_space[:, L:]
        pad, sq, rn = work[:, 0:3 + L], work[:, 3 + L:3 + 2 * L], work[:, 3 + 2 * L:3 + 3 * L]
        xin = work[:, 3:3 + 2 * D].rearrange("p (b d) -> p b d", b=2)
        xsc = region[:, HA * (SEQ + L):HA * (SEQ + L) + 2 * D].rearrange("p (b d) -> p b d", b=2)
        rope = sb("rope", [P, 3, BLK])
        zt = rope[:, 0:2, :]
        rot = sb("rot", [P, R_N])
        split = s["split_in_region"] + [split_in_conv]

        big = [ps(f"big{i}", [P, 1536]) for i in range(2)]
        small = [ps(f"small{i}", [P, 512]) for i in range(2)]

        x_in, rows_in, cst_in = [sem(f"x_in{i}") for i in range(2)], sem("rows_in"), sem("cst_in")
        raw_in, raw_used, w_ready, wab_ready, gained, pool_seq = (
            sem(x) for x in ("raw_in", "raw_used", "w_ready", "wab_ready", "gained", "ppool_seq"))
        u_hi, ab_out, ab_turned, ab_copied, last_hi, ab_clear = (
            sem(x) for x in ("u_hi", "ab_out", "ab_turned", "ab_copied", "last_hi", "ab_clear"))
        wab_in, rot_in = sem("wab_in"), sem("rot_in")
        dve_seq = sem("dve_seq")
        ssq, xscaled, x_turned, u_copied = sem("ssq"), sem("xscaled"), sem("x_turned"), sem("u_copied")
        rows_turned, rows_copied = sem("rows_turned"), sem("rows_copied")
        pads = sem("pads")
        big_full, copied, conv0, conv_done, silu_done, sq_done, rn_done, qk_done = (
            sem(x) for x in ("big_full", "copied", "conv0", "conv_done", "silu_done", "sq_done", "rn_done", "qk_done"))
        tok_full, tok_act, roped, rope_turned, rope_copied = (
            sem(x) for x in ("tok_full", "tok_act", "roped", "rope_turned", "rope_copied"))
        w_used = sem("w_used")
        root_done = sem("root_done")
        z_out = [sem(f"z_out{i}") for i in range(2)]

        items = [("T", 0)]
        for m in range(1, 12):
            items.append(("T", m))
            if m - 1 < 8:
                items.append(("N", m - 1))
        items.append(("A", 0))
        nitem = len(items)
        PART = 348
        parts = [(c, min(PART, L - c), 512 * i) for i, c in enumerate(range(0, L, PART))]
        bank_parts = lambda x, n: x[:].rearrange("p (b c) -> p b c", c=512)[:, 0:n, 0:PART]
        blocks = [("qkvb", b, COL_QKVB + b * BLK, b % 2) for b in range(6)] \
            + [(kind, hf, c + hf * BLK, pl[hf]) for kind, c, pl in
               (("zb", COL_ZB, (0, 1)), ("va", COL_VA, (0, 1)), ("qa", COL_QA, (2, 1)), ("ka", COL_KA, (2, 2))) for hf in range(2)]
        NB = len(blocks)
        before = [max([x for x in range(b) if blocks[x][3] == blocks[b][3]], default=None) for b in range(NB)]
        tok = [(blocks[b][0], t, b) for b in range(6, NB) for t in range(NT + (blocks[b][0] in ("ka", "va")))]
        order = [NT] + list(range(NT))
        is_rope = [kd in ("qa", "ka") for kd, _, _ in tok]
        tokbank = [big[0][:, 0:512], big[0][:, 512:1024], big[1][:, 0:512], big[1][:, 512:1024]]
        ropes_before = lambda n: sum(is_rope[:n])
        acts_before = lambda n: n - ropes_before(n)

        block = phase.enter_context(nc.Block())

        @block.sync
        def _(sp):
            sp.dma_start(s["cst"][:], a["consts"][:, 0:C_N]).then_inc(cst_in, 16)
            sp.dma_start(rowsb[0:48, :], a["conv_w"].rearrange("o i (m c) -> (o i m) c", c=128)).then_inc(rows_in, 16)
            sp.dma_start(rowsb[48:56, :], a["norm_mix"].rearrange("o (m c) -> (o m) c", c=128)).then_inc(rows_in, 16)
            sp.dma_start(rowsb[56:64, :], a["norm_ffn"].rearrange("o (m c) -> (o m) c", c=128)).then_inc(rows_in, 16)
            wv = a["w_in"].rearrange("o (k p) c -> (o p) k c", p=P)
            for j, t in enumerate(order):
                if j >= 2:
                    sp.wait_ge(xscaled, j - 1)
                src = a["x"][0, t * P:(t + 1) * P, :] if t < NT else a["meta"]
                sp.dma_start(xin[0:rows(t), j % 2, :], src).then_inc(x_in[j % 2], 16)
                if j == 1:
                    sp.dma_start(raw[:], wv[:, :, blocks[0][2]:blocks[0][2] + BLK]).then_inc(raw_in, 16)
            sp.dma_start(rot[:], a["consts"][:, C_N:]).then_inc(rot_in, 16)
            with nc.allow_non_contiguous_dma(reason="64-byte rows of the gate columns"):
                sp.dma_start(wab[:], wv[:, :, COL_AB:COL_AB + 16]).then_inc(wab_in, 16)
            for b in range(1, NB):
                sp.wait_ge(raw_used, b)
                sp.dma_start(raw[:], wv[:, :, blocks[b][2]:blocks[b][2] + BLK]).then_inc(raw_in, 16)
                if blocks[b][0] == "va":
                    for n in range(len(tok)):
                        if tok[n][0] == "zb" and tok[n][2] == b - 2:
                            t = tok[n][1]
                            sp.wait_ge(tok_act, acts_before(n) + 1)
                            sp.dma_start(a["z"][t][:, BLK * (b - 8):BLK * (b - 7)], zt[:, t % 2, :]).then_inc(z_out[t % 2], 16)
            for b in range(2):
                sp.wait_ge(z_out[b], 16 * NT)

        @block.gpsimd
        def _(pool):
            seq = Seq(pool, pool_seq)

            def gain_in_place(src, n):
                seq(pool.tensor_tensor(src, src, cols[:, 48:56].unsqueeze(2).to_broadcast([P, KD, n]), ALU.mult))

            def divide(src, hi, lo, n, signal):
                seq(pool.tensor_tensor(hi, src, cols[:, 48:56].unsqueeze(2).to_broadcast([P, KD, n]), ALU.mult))
                gain_in_place(src, n)
                pool.tensor_tensor(lo, src, hi, ALU.subtract).then_inc(signal, 1)

            pool.wait_ge(rows_copied, 1)
            for b in range(NB - 1):
                hi, lo = split[blocks[b][3]]
                if blocks[b][0] == "qa" and blocks[b][1] == 0:
                    pool.wait_ge(silu_done, 12)
                    pool.wait_ge(qk_done, 8)
                    pool.wait_ge(ab_turned, 1)
                pool.wait_ge(raw_in, 16 * (b + 1))
                if before[b] is not None:
                    pool.wait_ge(w_used, before[b] + 1)
                divide(raw[:], hi[:], lo[:], BLK, w_ready)
                pool.wait_ge(w_ready, b + 1)
                pool.sem_inc(raw_used, 1)
                if b == 0:
                    pool.wait_ge(wab_in, 16)
                    divide(wab[:], wab_r[0][:], wab_r[1][:], 16, wab_ready)
            pool.wait_ge(raw_in, 16 * NB)
            gain_in_place(raw[:], BLK)
            pool.sem_inc(gained, 1)

        @block.scalar
        def _(act):
            def rounded(j):
                r, c = rows(order[j]), col0(order[j])
                for half in range(2):
                    act.wait_ge(x_turned, 2 * j + half + 1)
                    act.activation(uT[0][:, 4 * half:4 * half + 4, c:c + r], small[half][:].rearrange("p (k t) -> p k t", k=4)[:, :, 0:r],
                                   ACT.Copy).then_inc(u_hi, 1)

            def spread(dst, src, function, signal, **more):
                n = 2 * PART
                act.activation(dst[:, 0:n].rearrange("p (b c) -> p b c", c=PART), bank_parts(src, 2), function, **more)
                act.activation(dst[:, n:L], src[:, 1024:1024 + L - n], function, **more).then_inc(signal, 1)

            act.wait_ge(cst_in, 16)
            for j, t in enumerate(order):
                r = rows(t)
                act.wait_ge(x_in[j % 2], 16 * (j // 2 + 1))
                if j >= 1:
                    act.wait_ge(ssq, j)
                act.activation(cv[0:r, 0:D], xin[0:r, j % 2, :], ACT.Square, accum_out=ss[0:r, j, 0:1]).then_inc(ssq, 1)
                act.wait_ge(ssq, j + 1)
                act.activation(ss[0:r, j, 1:2], ss[0:r, j, 0:1], ACT.Sqrt, bias=cst[0:r, C_EPS:C_EPS + 1], scale=1.0 / D).then_inc(root_done, 1)
                if j >= 1:
                    rounded(j - 1)
            rounded(NT)
            act.wait_ge(pads, 1)
            act.wait_ge(x_turned, 2 * (NT + 1))
            for m in range(12):
                i = items.index(("T", m))
                act.wait_ge(big_full, i + 1)
                if m >= 1:
                    act.wait_ge(conv_done, m)
                spread(pad[:, 3:3 + L], big[i % 2], ACT.Copy, copied)
                act.wait_ge(copied, m + 1)
                if m >= 1:
                    act.wait_ge(silu_done, m)
                if m == 0:
                    act.wait_ge(ssq, NT + 1)
                    act.wait_ge(rows_copied, 1)
                act.activation(cv[:], pad[:, 0:L], ACT.Copy, scale=cols[:, m:m + 1]).then_inc(conv0, 1)
                if 1 <= m <= 8:
                    i = items.index(("N", m - 1))
                    act.wait_ge(big_full, i + 1)
                    if m >= 2:
                        act.wait_ge(qk_done, m - 1)
                    spread(rn, big[i % 2], ACT.Sqrt, rn_done, bias=cst[:, C_EPS:C_EPS + 1])
                act.wait_ge(conv_done, m + 1)
                dst = (s["gq"], s["gk"], s["gv"])[m // 4][:, m % 4, :]
                act.activation(dst, cv[:], ACT.Silu).then_inc(silu_done, 1)
                if m < 8:
                    act.wait_ge(silu_done, m + 1)
                    act.activation(sq[:], dst, ACT.Square).then_inc(sq_done, 1)
            act.wait_ge(big_full, nitem)
            act.wait_ge(qk_done, 8)
            for c, n, o in parts:
                ins = act.activation(rn[0:16, c:c + n], big[(nitem - 1) % 2][0:16, o:o + n], ACT.Copy)
            ins.then_inc(ab_out, 1)
            act.wait_ge(ab_turned, 1)
            act.wait_ge(ab_clear, 1)
            act.activation(s["ab"][:, 0:NT, :], small[0][:, 0:16 * NT].rearrange("p (t c) -> p t c", c=16), ACT.Copy)
            act.activation(s["ab"][0:META, NT, :], small[0][0:META, 16 * NT:16 * NT + 16], ACT.Copy).then_inc(ab_copied, 1)
            for n, (kind, t, b) in enumerate(tok):
                r = rows(t)
                src = tokbank[n % 4]
                hf = blocks[b][1]
                if b == NB - 1 and t == 0:
                    act.wait_ge(gained, 1)
                    act.wait_ge(w_used, NB - 1)
                    act.activation(split[blocks[b][3]][0][:], raw[:], ACT.Copy).then_inc(last_hi, 1)
                if is_rope[n]:
                    q = ropes_before(n)
                    dst = s["aq"] if kind == "qa" else s["ak"]
                    off = t * P if kind == "qa" else col0(t)
                    act.wait_ge(rope_turned, q + 1)
                    act.activation(dst[:, 2 * hf:2 * hf + 2, off:off + r], small[q % 2][:, 0:256].rearrange("p (h t) -> p h t", h=2)[:, :, 0:r],
                                   ACT.Copy).then_inc(rope_copied, 1)
                    continue
                act.wait_ge(tok_full, n + 1)
                if kind == "va":
                    act.activation(s["av"][0:r, t, BLK * hf:BLK * (hf + 1)], src[0:r, 0:BLK], ACT.Copy).then_inc(tok_act, 1)
                else:
                    if hf or t >= 2:
                        act.wait_ge(z_out[t % 2], 16 * ((NT * hf + t) // 2))
                    act.activation(zt[:, t % 2, :], src[0:r, 0:BLK], ACT.Silu).then_inc(tok_act, 1)

        @block.vector
        def _(dve):
            seq = Seq(dve, dve_seq)
            dve.memset(pad[:, 0:3], 0.0).then_inc(pads, 1)
            dve.memset(s["ab"][:], 0.0).then_inc(ab_clear, 1)
            dve.wait_ge(rows_turned, 1)
            dve.tensor_copy(cols[:, 0:64], small[0][:, 0:64]).then_inc(rows_copied, 1)
            dve.wait_ge(rows_copied, 1)

            def rest(j):
                r, c = rows(order[j]), col0(order[j])
                for half in range(2):
                    dve.wait_ge(u_hi, 2 * j + half + 1)
                    src = small[half][:].rearrange("p (k t) -> p k t", k=4)[:, :, 0:r]
                    k = slice(4 * half, 4 * half + 4)
                    dve.tensor_tensor(uT[1][:, k, c:c + r], src, uT[0][:, k, c:c + r], ALU.subtract).then_inc(u_copied, 1)

            for j, t in enumerate(order):
                r = rows(t)
                dve.wait_ge(root_done, j + 1)
                seq(dve.reciprocal(ss[0:r, j, 2:3], ss[0:r, j, 1:2]))
                if j >= 2:
                    dve.wait_ge(x_turned, 2 * (j - 1))
                dve.tensor_scalar(xsc[0:r, j % 2, :], xin[0:r, j % 2, :], ss[0:r, j, 2:3], None, ALU.mult).then_inc(xscaled, 1)
                if j >= 1:
                    rest(j - 1)
            rest(NT)

            def conv(m):
                dve.wait_ge(conv0, m + 1)
                for i in range(1, 4):
                    w = cols[:, 12 * i + m:12 * i + m + 1]
                    ins = dve.scalar_tensor_tensor(cv[:], pad[:, i:i + L], w, cv[:], ALU.mult, ALU.add)
                    if i < 3:
                        seq(ins)
                    else:
                        ins.then_inc(conv_done, 1)

            def l2(m):
                dve.wait_ge(rn_done, m + 1)
                seq(dve.reciprocal(rn[:], rn[:]))
                dst = (s["gq"], s["gk"])[m // 4][:, m % 4, :]
                dve.scalar_tensor_tensor(dst, dst, DK ** -0.5 if m < 4 else 1.0, rn[:], ALU.mult, ALU.mult).then_inc(qk_done, 1)

            for m in range(12):
                conv(m)
                if 1 <= m <= 8:
                    l2(m - 1)
            dve.wait_ge(rot_in, 16)
            for b in range(2):
                dve.wait_ge(z_out[b], 16 * NT)
            nh = BLK // 64
            for n, (kind, t, b) in enumerate(tok):
                if not is_rope[n]:
                    continue
                if b == NB - 1 and t == 0:
                    dve.wait_ge(last_hi, 1)
                    hi, lo = split[blocks[b][3]]
                    dve.tensor_tensor(lo[:], raw[:], hi[:], ALU.subtract).then_inc(w_ready, 1)
                r, q = rows(t), ropes_before(n)
                src = tokbank[n % 4][0:r, 0:BLK].rearrange("p (h d) -> p h d", d=64)
                co = rot[0:r, 64 * t:64 * t + 64].unsqueeze(1).to_broadcast([r, nh, 64])
                si = rot[0:r, R_SIN + 64 * t:R_SIN + 64 * t + 64]
                dve.wait_ge(tok_full, n + 1)
                v = lambda b: rope[0:r, b, :].rearrange("p (h d) -> p h d", d=64)
                if q >= 1:
                    dve.wait_ge(rope_turned, q)
                dve.tensor_tensor(v(0), src, co, ALU.mult)
                dve.tensor_tensor(v(1)[:, :, 0:32], src[:, :, 32:64], si[:, 0:32].unsqueeze(1).to_broadcast([r, nh, 32]), ALU.mult)
                seq(dve.tensor_tensor(v(1)[:, :, 32:64], src[:, :, 0:32], si[:, 32:64].unsqueeze(1).to_broadcast([r, nh, 32]), ALU.mult))
                dve.tensor_tensor(rope[0:r, 2, :], rope[0:r, 0, :], rope[0:r, 1, :], ALU.add).then_inc(roped, 1)
                dve.wait_ge(roped, q + 1)

        @block.tensor
        def _(pe):
            pe.wait_ge(cst_in, 16)
            pe.wait_ge(rows_in, 48)
            pe.transpose(small[0][:, 0:64], rowsb[:], ident[0:64, 0:64]).then_inc(rows_turned, 1)
            pe.wait_ge(rows_copied, 1)
            for j, t in enumerate(order):
                r = rows(t)
                pe.wait_ge(xscaled, j + 1)
                for half in range(2):
                    if j >= 1:
                        pe.wait_ge(u_copied, 2 * j - 1 + half)
                    for kk in range(4):
                        kx = 4 * half + kk
                        mm = pe.transpose(small[half][:, kk * 128:kk * 128 + r], xsc[0:r, j % 2, kx * P:(kx + 1) * P], ident[0:r, 0:r])
                    mm.then_inc(x_turned, 1)
            pe.wait_ge(u_copied, 2 * (NT + 1))

            def freed(i):
                kind, m = items[i - 2]
                pe.wait_ge({"T": copied, "N": rn_done, "A": ab_out}[kind], m + 1)

            for i, (kind, m) in enumerate(items):
                if i >= 2:
                    freed(i)
                if kind == "T":
                    b = m // 2
                    w = split[blocks[b][3]]
                    if m % 2 == 0:
                        pe.wait_ge(w_ready, b + 1)
                    for c, n, o in parts:
                        for kx in range(KD):
                            for x, y in PASSES:
                                mm = pe.matmul(big[i % 2][:, o:o + n], w[x][:, kx, (m % 2) * 128:(m % 2 + 1) * 128], uT[y][:, kx, c:c + n],
                                               start=kx == 0 and (x, y) == PASSES[0], stop=kx == KD - 1 and (x, y) == PASSES[-1])
                    mm.then_inc(big_full, 1)
                    if m % 2 == 1:
                        pe.wait_ge(big_full, i + 1)
                        pe.sem_inc(w_used, 1)
                elif kind == "A":
                    pe.wait_ge(wab_ready, 1)
                    for c, n, o in parts:
                        for kx in range(KD):
                            for x, y in PASSES:
                                mm = pe.matmul(big[i % 2][0:16, o:o + n], wab_r[x][:, kx, :], uT[y][:, kx, c:c + n],
                                               start=kx == 0 and (x, y) == PASSES[0], stop=kx == KD - 1 and (x, y) == PASSES[-1])
                    mm.then_inc(big_full, 1)
                else:
                    pe.wait_ge(sq_done, m + 1)
                    for c, n, o in parts:
                        mm = pe.matmul(big[i % 2][:, o:o + n], cst[:, C_BLK:C_BLK + 128], sq[:, c:c + n], start=True, stop=True)
                    mm.then_inc(big_full, 1)

            def turn(n):
                kind, t, _ = tok[n]
                r, q = rows(t), ropes_before(n)
                pe.wait_ge(roped, q + 1)
                if q == 0:
                    pe.wait_ge(ab_copied, 1)
                if q >= 2:
                    pe.wait_ge(rope_copied, q - 1)
                for h in range(2):
                    mm = pe.transpose(small[q % 2][:, h * 128:h * 128 + r], rope[0:r, 2, h * 128:(h + 1) * 128], ident[0:r, 0:r])
                mm.then_inc(rope_turned, 1)

            for n, (kind, t, b) in enumerate(tok):
                if n < 4:
                    freed(max(i for i in range(nitem) if i % 2 == n // 2) + 2)
                else:
                    j = n - 4
                    pe.wait_ge(roped if is_rope[j] else tok_act, (ropes_before(j) if is_rope[j] else acts_before(j)) + 1)
                c, r = col0(t), rows(t)
                w = split[blocks[b][3]]
                early = b == NB - 1 and t == 0
                if early:
                    turn(n - 1)
                if t == 0:
                    pe.wait_ge(w_ready, b + 1)
                for kx in range(KD):
                    for x, y in PASSES:
                        mm = pe.matmul(tokbank[n % 4][0:r, 0:BLK], uT[y][:, kx, c:c + r], w[x][:, kx, :],
                                       start=kx == 0 and (x, y) == PASSES[0], stop=kx == KD - 1 and (x, y) == PASSES[-1])
                mm.then_inc(tok_full, 1)
                if n + 1 == len(tok) or tok[n + 1][2] != b:
                    pe.wait_ge(tok_full, n + 1)
                    pe.sem_inc(w_used, 1)
                if n == 3:
                    pe.wait_ge(ab_out, 1)
                    for t in range(NT + 1):
                        mm = pe.transpose(small[0][0:rows(t), 16 * t:16 * t + 16], rn[0:16, col0(t):col0(t) + rows(t)], ident[0:16, 0:16])
                    mm.then_inc(ab_turned, 1)
                if n >= 1 and is_rope[n - 1] and not early:
                    turn(n - 1)
            turn(len(tok) - 1)

        phase.close()
        clear(nc, sems)


class Share:

    def __init__(self, piece, bounds):
        self.piece, self.bounds, self.k = piece, bounds, 0

    def __call__(self):
        for g in range(self.bounds[self.k], self.bounds[self.k + 1]):
            self.piece(g)
        self.k += 1


def mixers(nc, a, s):
    with ExitStack() as ctx, ExitStack() as phase:
        sb = lambda n, sh, dt=F32: ctx.enter_context(nc.sbuf_tensor(n, sh, dt))
        ps = lambda n, sh, dt=F32: ctx.enter_context(nc.psum_tensor(n, sh, dt))
        sems = []

        def sem(n):
            sems.append(ctx.enter_context(nc.semaphore(n)))
            return sems[-1]

        sem2 = lambda n: [sem(f"{n}{b}") for b in range(2)]
        cst, mix, gq, gk, gv = s["cst"], s["mix"], s["gq"], s["gk"], s["gv"]
        ident, upper = cst[:, C_ID:C_ID + 128], cst[:, C_UP:C_UP + 128]

        probs = sb("probs", [P, 2, 2, L])
        probsT = sb("probsT", [P, NT + 1, P])
        nmax, bias, rsum, rinv = (sb(x, [P, 2, 2]) for x in ("nmax", "bias", "rsum", "rinv"))
        coef = sb("coef", [P, 2])
        lam = sb("lam", [P, 8])
        again = sb("again", [P, VA])
        astat = sb("astat", [P, 3, NT * HA])
        sqo = sb("sqo", [P, VA])
        ring = [ps(f"ring{i}", [P, 512]) for i in range(3)]
        lam_in, ring_full, ring_read = sem("lam_in"), sem("ring_full"), sem("ring_read")
        lam_sum, lam_exp, maxed, exped, mixed = (sem(x) for x in ("lam_sum", "lam_exp", "maxed", "exped", "mixed"))
        a_sq, a_root, a_dve, a_done = sem("a_sq"), sem("a_root"), sem("a_dve"), sem("a_done")

        items = [(i, h) for i in range(NT) for h in range(HA)]
        N = len(items)
        nkeys = lambda i: META + P * (i + 1)
        pieces, weight = [], []

        def add(w, *p):
            pieces.append(p)
            weight.append(w)

        def add_scores(n, c):
            nk = nkeys(items[n][0])
            for k0 in range(0, nk, 512):
                add(min(nk - k0, 512) + 64, "score", n, c, k0)

        for n in range(N + 1):
            if n < N:
                add_scores(n, 0)
            if n >= 1:
                add(0, "mix", n - 1, 0, 0)
            if n < N:
                add_scores(n, 1)
                add(0, "max", n, 0, 0)
            if n >= 1:
                i = items[n - 1][0]
                for f in range(0, i + 2, 4):
                    add(128 * min(4, i + 2 - f), "turn", n - 1, f, 0)
            if n < N:
                add(0, "max", n, 1, 0)
                add(0, "exp", n, 0, 0)
            if n >= 1:
                add(128 * (i + 2), "out", n - 1, 0, 0)
            if n < N:
                add(0, "exp", n, 1, 0)
        add(0, "root", 0, 0, 0)
        for i in range(NT):
            add(SCALE_WEIGHT, "scale", i, 0, 0)
        ring_pos, after = {}, {}
        for g, p in enumerate(pieces):
            if p[0] in ("score", "turn", "out"):
                ring_pos[g] = len(ring_pos)
            after[p[0:3]] = len(ring_pos)

        TILES = [NT] + list(range(NT))
        NJ = len(TILES)
        G8 = NJ * HB
        inv, aqk = sb("inv", [P, 2, HB, P]), sb("aqk", [P, HB, P])
        tri, xm = sb("tri", [P, HB, P]), sb("xm", [P, HB, P])
        ntm, bt = sb("ntm", [P, HB, P]), sb("bt", [P, HB, P])
        dec = sb("dec", [P, HB, P])
        ktok, vtok = sb("ktok", [P, 512]), sb("vtok", [P, 512])
        zz, vn, v2 = sb("zz", [P, 512]), sb("vn", [P, 512]), sb("v2", [P, 512])
        lamv = zz[:, 0:256].rearrange("p (a c) -> p a c", a=4)
        state = sb("state", [P, 4, DK])
        gat = sb("gat", [P, 6, G8])
        gc, eg, neg, beta, graw, tmp = (gat[:, i, :] for i in range(6))
        par = sb("par", [P, 3, HB])
        gain = sb("gdn_gain", [P, DK])
        glc, ekl, egs = sb("glc", [P, 2, HB]), sb("ekl", [P, 2, HB]), sb("egs", [P, 2, 4])
        gl = sb("gl", [P, 2, 2, 4])
        stat = sb("gstat", [P, 3, NT * HB])
        zg = s["region"][:, 0:NT * 512].rearrange("p (t c) -> p t c", t=NT)

        level_bank = [ps(f"level{b}", [P, 512]) for b in range(2)]
        wide = [ps(f"wide{b}", [P, 512]) for b in range(2)]
        solo = ps("solo", [P, 512])
        par_in, z_in, dve_seq = (sem(x) for x in ("gpar_in", "z_in", "gdve_seq"))
        g1, g2, g3, g4, gc_full, gates, eg_done = (sem(x) for x in ("g1", "g2", "g3", "g4", "gc_full", "gates", "eg_done"))
        kk_full, kq_full, gcb_full, d_done, dec_done, aqk_raw = (
            sem2(x) for x in ("kk_full", "kq_full", "gcb_full", "d_done", "dec_done", "aqk_raw"))
        nt_done, aqk_done, r1_done, t1_turned, t1_copied, bt_done = (
            sem2(x) for x in ("nt_done", "aqk_done", "r1_done", "t1_turned", "t1_copied", "bt_done"))
        x_full, x_copied, y_full, t_new, r_turned, r_copied, r_done = (
            sem2(x) for x in ("x_full", "x_copied", "y_full", "t_new", "r_turned", "r_copied", "r_done"))
        kt_turned, kt_copied, vt_turned, vt_copied, glc_done, ekl_done, egs_done = (
            sem(x) for x in ("kt_turned", "kt_copied", "vt_turned", "vt_copied", "glc_done", "ekl_done", "egs_done"))
        ks_full, z_done, v_full, vn_done, v2_done, o2_full, s_full, s_done, o_done = (
            sem(x) for x in ("ks_full", "z_done", "v_full", "vn_done", "v2_done", "o2_full", "gs_full", "s_done", "o_done"))
        gl_done, gain_in = sem("gl_done"), sem("ggain_in")
        o_sq, o_root, zg_done, normed, wout_in = (sem(x) for x in ("go_sq", "go_root", "zg_done", "normed", "wout_in"))

        nlev = lambda j: 3 if j == 0 else 6
        lev0 = lambda j: 0 if j == 0 else 3 + 6 * (j - 1)
        turns_before = lambda j, lv: lev0(j) + lv - j
        tmat = lambda w, r: w[:].rearrange("p (h c) -> p h c", h=4)[0:r, :, 0:r]
        batch = lambda m, b, r: m.rearrange("p (hh b) c -> p b hh c", b=2)[0:r, b, :, 0:r]
        gate = lambda v, j, b, r: v.rearrange("p (t hh b) -> p t b hh", b=2, t=NJ)[0:r, TILES[j], b, :]
        one = lambda v, j, h, r: v[0:r, TILES[j] * HB + h:TILES[j] * HB + h + 1]

        share = []
        for j in range(NJ + 1):
            level_share = LEVEL_SHARE if j else FIRST_SHARE
            if j >= 1:
                share += TOKENS_SHARE
            if j < NJ:
                share += PREPARE_SHARE + level_share
            if j >= 2:
                share += [1]
            if j < NJ:
                share += level_share
            if j >= 1:
                share += [1]
            if j < NJ:
                share += level_share
            if j >= 1:
                share += [1]
            if 1 <= j < NJ:
                share += level_share + [1] + 2 * level_share
        share[-FREE_STEPS:] = [0] * FREE_STEPS
        whole, run, place, bounds = sum(share), 0, 0, [0]
        for k in range(len(share)):
            g = bounds[-1]
            place += share[k]
            while g < len(pieces) and (run + weight[g] / 2) * whole <= place * sum(weight):
                run += weight[g]
                g += 1
            bounds.append(g)
        assert bounds[-1] == len(pieces)

        block = phase.enter_context(nc.Block())

        @block.sync
        def _(sp):
            sp.dma_start(par[:, 0, :], a["a_log"].to_broadcast([P, HB])).then_inc(par_in, 16)
            sp.dma_start(par[:, 1, :], a["dt_bias"].to_broadcast([P, HB])).then_inc(par_in, 16)
            for j, n in enumerate(("lambda_q1", "lambda_k1", "lambda_q2", "lambda_k2")):
                sp.dma_start(lamv[:, j, :], a[n].to_broadcast([P, 64])).then_inc(lam_in, 16)
            sp.dma_start(again[:], a["diff_norm"].to_broadcast([P, VA])).then_inc(lam_in, 16)
            sp.dma_start(gain[:], a["gdn_norm"].to_broadcast([P, DK])).then_inc(gain_in, 16)
            sp.wait_ge(ring_full, len(ring_pos))
            sp.dma_start(zg[:], a["z"].rearrange("t p c -> p t c")).then_inc(z_in, 16)
            sp.dma_start(s["wout"], a["w_out"].rearrange("o (k p) c -> (o p) k c", p=P)).then_inc(wout_in, 16)
            sp.wait_ge(wout_in, 16)

        @block.scalar
        def _(act):
            def piece(g):
                what, n, c, k0 = pieces[g]
                if g in ring_pos:
                    bank = ring[ring_pos[g] % 3]
                    act.wait_ge(ring_full, ring_pos[g] + 1)
                if what == "score":
                    k1 = min(nkeys(items[n][0]), k0 + 512)
                    act.activation(probs[:, n % 2, c, k0:k1], bank[:, 0:k1 - k0], ACT.Copy).then_inc(ring_read, 1)
                elif what == "turn":
                    nb = min(4, items[n][0] + 2 - c)
                    if c == 0:
                        act.activation(probsT[0:META, 0, :], bank[0:META, 0:128], ACT.Copy)
                        act.activation(probsT[:, 1:nb, :], bank[:, 128:nb * 128], ACT.Copy).then_inc(ring_read, 1)
                    else:
                        act.activation(probsT[:, c:c + nb, :], bank[:, 0:nb * 128], ACT.Copy).then_inc(ring_read, 1)
                elif what == "out":
                    i, h = items[n]
                    if n >= 1:
                        act.wait_ge(a_sq, n)
                    act.activation(sqo[:], bank[:, 0:VA], ACT.Square, scale=rinv[:, n % 2, 0:1], accum_out=astat[:, 0, n:n + 1]).then_inc(a_sq, 1)
                    act.activation(mix[:, i, h * VA:(h + 1) * VA], bank[:, 0:VA], ACT.Copy,
                                   scale=rinv[:, n % 2, 0:1]).then_inc(ring_read, 1)
                elif what == "exp":
                    row = probs[:, n % 2, c, 0:nkeys(items[n][0])]
                    act.wait_ge(maxed, 2 * n + c + 1)
                    act.activation(row, row, ACT.Exp, bias=bias[:, n % 2, c:c + 1], scale=DK ** -0.5,
                                   accum_out=rsum[:, n % 2, c:c + 1]).then_inc(exped, 1)
                elif what == "root":
                    act.wait_ge(a_sq, N)
                    act.activation(astat[:, 1, :], astat[:, 0, :], ACT.Sqrt, bias=cst[:, C_EPS:C_EPS + 1], scale=1.0 / VA).then_inc(a_root, 1)

            attend = Share(piece, bounds)
            act.wait_ge(par_in, 32)
            act.activation(par[:, 2, :], par[:, 0, :], ACT.Exp).then_inc(g1, 1)
            act.wait_ge(g2, 1)
            act.activation(tmp, tmp, ACT.Exp, scale=-1.0)
            act.activation(beta, beta, ACT.Exp, scale=-1.0).then_inc(g3, 1)
            act.wait_ge(lam_sum, 1)
            act.activation(lam[:, 2:4], lam[:, 0:2], ACT.Exp).then_inc(lam_exp, 1)
            act.wait_ge(g3, 1)
            act.activation(tmp, tmp, ACT.Ln, bias=cst[:, C_ONE:C_ONE + 1]).then_inc(g4, 1)
            act.wait_ge(gates, 1)
            act.activation(eg, gc, ACT.Exp).then_inc(eg_done, 1)

            def prepare(j):
                r = rows(TILES[j])
                for b in range(2):
                    act.wait_ge(gl_done, 2 * j + b + 1)
                    if j >= 2:
                        act.wait_ge(s_done, j - 1)
                    last = gl[64 * b:64 * b + 64, j % 2, b, :]
                    act.activation(egs[64 * b:64 * b + 64, j % 2, :], last, ACT.Exp).then_inc(egs_done, 1)
                    act.wait_ge(d_done[b], j + 1)
                    act.activation(batch(dec, b, r), batch(dec, b, r), ACT.Exp).then_inc(dec_done[b], 1)
                act.wait_ge(glc_done, j + 1)
                act.activation(ekl[0:r, j % 2, :], glc[0:r, j % 2, :], ACT.Exp).then_inc(ekl_done, 1)
                attend()
                attend()
                for b in range(2):
                    act.wait_ge(t1_turned[b], j + 1)
                    act.activation(batch(tri, b, r), tmat(level_bank[b], r), ACT.Copy).then_inc(t1_copied[b], 1)
                attend()

            def level(j, lv):
                r, n = rows(TILES[j]), lev0(j) + lv
                for b in range(2):
                    act.wait_ge(x_full[b], n)
                    act.activation(batch(xm, b, r), tmat(level_bank[b], r), ACT.Copy).then_inc(x_copied[b], 1)
                attend()
                attend()
                if lv < nlev(j):
                    for b in range(2):
                        act.wait_ge(r_turned[b], turns_before(j, lv))
                        act.activation(batch(inv[:, j % 2], b, r), tmat(level_bank[b], r), ACT.Copy).then_inc(r_copied[b], 1)
                attend()

            def roots(t0, t1):
                c = slice(HB * t0, HB * t1)
                act.wait_ge(o_sq, t1)
                act.activation(stat[:, 1, c], stat[:, 0, c], ACT.Sqrt, bias=cst[:, C_EPS:C_EPS + 1], scale=1.0 / DK).then_inc(o_root, 1)

            def tokens(j):
                r = rows(TILES[j])
                act.wait_ge(kt_turned, j + 1)
                act.activation(ktok[0:r, :], solo[0:r, :], ACT.Copy).then_inc(kt_copied, 1)
                attend()
                act.wait_ge(vt_turned, j + 1)
                act.activation(vtok[0:r, :], solo[0:r, :], ACT.Copy).then_inc(vt_copied, 1)
                attend()

            for j in range(NJ + 1):
                if j >= 1:
                    tokens(j - 1)
                if j < NJ:
                    prepare(j)
                    level(j, 1)
                if j >= 2:
                    attend()
                if j < NJ:
                    level(j, 2)
                if j >= 1:
                    attend()
                if j < NJ:
                    level(j, 3)
                if j >= 1:
                    attend()
                if 1 <= j < NJ:
                    level(j, 4)
                    attend()
                    if j == NJ - 1:
                        roots(0, NT - 1)
                    level(j, 5)
                    level(j, 6)
            roots(NT - 1, NT)

        @block.gpsimd
        def _(pool):
            def blocks(j, lv):
                r, n = rows(TILES[j]), lev0(j) + lv
                m = cst[0:r, C_LEV + 128 * lv:C_LEV + 128 * lv + r].unsqueeze(1).to_broadcast([r, 4, r])
                for b in range(2):
                    pool.wait_ge(nt_done[b], j + 1)
                    if n >= 2:
                        pool.wait_ge(x_full[b], n - 1)
                    pool.tensor_tensor(batch(bt[:], b, r), batch(ntm, b, r), m, ALU.mult).then_inc(bt_done[b], 1)

            def mask(j):
                up = upper.unsqueeze(1).to_broadcast([P, 4, P])
                for b in range(2):
                    pool.wait_ge(aqk_raw[b], j)
                    dst = batch(aqk[:], b, P)
                    pool.tensor_tensor(dst, dst, up, ALU.mult).then_inc(aqk_done[b], 1)

            def gains(t0, t1):
                pool.wait_ge(z_in, 16)
                pool.wait_ge(gain_in, 16)
                for t in range(t0, t1):
                    z = zg[:, t, :].rearrange("p (h d) -> p h d", d=DK)
                    pool.tensor_tensor(z, z, gain[:].unsqueeze(1).to_broadcast([P, HB, DK]), ALU.mult).then_inc(zg_done, 1)

            def recur(j):
                r = rows(TILES[j])
                if j == NJ - 1:
                    return
                pool.wait_ge(vn_done, j + 1)
                pool.wait_ge(ekl_done, j + 1)
                k = ekl[0:r, j % 2, :].unsqueeze(2).to_broadcast([r, HB, DK])
                v = lambda m: m[0:r, :].rearrange("p (h c) -> p h c", h=HB)
                if j >= 1:
                    pool.wait_ge(s_full, j)
                pool.tensor_tensor(v(v2), v(vn), k, ALU.mult).then_inc(v2_done, 1)

            for j in range(NJ + 1):
                if j < NJ:
                    blocks(j, 1)
                    blocks(j, 2)
                    blocks(j, 3)
                if j >= 1:
                    recur(j - 1)
                if 1 <= j < NJ:
                    blocks(j, 4)
                    blocks(j, 5)
                    if j == NJ - 1:
                        gains(0, NT // 2)
                    blocks(j, 6)
                    if j == NJ - 1:
                        gains(NT // 2, NT)
                    mask(j)

        @block.vector
        def _(dve):
            seq, aseq = Seq(dve, dve_seq), Seq(dve, a_dve)
            dve.wait_ge(par_in, 32)
            ab3 = s["ab"][:, :, 0:8]
            g3d = graw.rearrange("p (t h) -> p t h", h=HB)
            seq(dve.tensor_tensor(g3d, ab3, par[:, 1, :].unsqueeze(1).to_broadcast([P, NJ, HB]), ALU.add))
            seq(dve.scalar_tensor_tensor(tmp, graw, -1.0, graw, ALU.mult, ALU.max))
            dve.tensor_copy(beta.rearrange("p (t h) -> p t h", h=HB), s["ab"][:, :, 8:16]).then_inc(g2, 1)
            dve.wait_ge(lam_in, 80)
            seq(dve.tensor_tensor(lamv[:, 0, :], lamv[:, 0, :], lamv[:, 1, :], ALU.mult))
            seq(dve.tensor_tensor(lamv[:, 2, :], lamv[:, 2, :], lamv[:, 3, :], ALU.mult))
            dve.tensor_reduce(lam[:, 0:2], lamv[:].rearrange("p (a b) c -> p a b c", a=2)[:, :, 0, :], AX.X, ALU.add).then_inc(lam_sum, 1)
            dve.wait_ge(g4, 1)
            seq(dve.scalar_tensor_tensor(graw, graw, 0.0, tmp, ALU.max, ALU.add))
            dve.wait_ge(g1, 1)
            seq(dve.scalar_tensor_tensor(g3d, g3d, -1.0, par[:, 2, :].unsqueeze(1).to_broadcast([P, NJ, HB]), ALU.mult, ALU.mult))
            seq(dve.tensor_scalar(beta, beta, 1.0, None, ALU.add))
            seq(dve.reciprocal(beta, beta))
            dve.sem_inc(g2, 1)
            dve.wait_ge(lam_exp, 1)
            seq(dve.tensor_tensor(lam[:, 4:5], lam[:, 3:4], lam[:, 2:3], ALU.subtract))
            seq(dve.tensor_scalar(lam[:, 5:6], lam[:, 4:5], -LAM_INIT, None, ALU.add))
            dve.wait_ge(gc_full, 1)
            dve.tensor_copy(gc, solo[:, 0:G8]).then_inc(gates, 1)
            dve.wait_ge(eg_done, 1)
            seq(dve.tensor_scalar(neg, eg, -1.0, None, ALU.mult))

            def piece(g):
                what, n, c, _ = pieces[g]
                if what == "max":
                    b, nk = n % 2, nkeys(items[n][0])
                    dve.wait_ge(ring_read, after["score", n, c])
                    aseq(dve.memset(probs[0:64, b, c, nk - 64:nk], -BIG))
                    aseq(dve.tensor_reduce(nmax[:, b, c:c + 1], probs[:, b, c, 0:nk], AX.X, ALU.max))
                    dve.tensor_scalar(bias[:, b, c:c + 1], nmax[:, b, c:c + 1], -DK ** -0.5, None, ALU.mult).then_inc(maxed, 1)
                elif what == "mix":
                    b, nk = n % 2, nkeys(items[n][0])
                    dve.wait_ge(exped, 2 * n + 2)
                    if n >= 2:
                        dve.wait_ge(ring_read, after["out", n - 2, 0])
                    aseq(dve.reciprocal(rinv[:, b, :], rsum[:, b, :]))
                    aseq(dve.tensor_scalar(coef[:, b:b + 1], rinv[:, b, 1:2], rsum[:, b, 0:1], lam[:, 5:6], ALU.mult, ALU.mult))
                    dve.scalar_tensor_tensor(probs[:, b, 0, 0:nk], probs[:, b, 1, 0:nk], coef[:, b:b + 1], probs[:, b, 0, 0:nk],
                                             ALU.mult, ALU.add).then_inc(mixed, 1)
                elif what == "scale":
                    if n == 0:
                        dve.wait_ge(a_root, 1)
                        aseq(dve.reciprocal(astat[:, 2, :], astat[:, 1, :]))
                        aseq(dve.tensor_scalar(astat[:, 2, :], astat[:, 2, :], 1.0 - LAM_INIT, None, ALU.mult))
                    o = mix[:, n, 0:512].rearrange("p (h d) -> p h d", d=VA)
                    r = astat[:, 2, HA * n:HA * n + HA].unsqueeze(2).to_broadcast([P, HA, VA])
                    aseq(dve.tensor_tensor(o, o, r, ALU.mult))
                    dve.tensor_tensor(o, o, again[:].unsqueeze(1).to_broadcast([P, HA, VA]), ALU.mult).then_inc(a_done, 1)

            attend = Share(piece, bounds)

            def prepare(j):
                r = rows(TILES[j])
                for b in range(2):
                    dve.wait_ge(gcb_full[b], j + 1)
                    if j >= 1:
                        dve.wait_ge(nt_done[b], j)
                    if j >= 2:
                        dve.wait_ge(aqk_raw[b], j - 1)
                    for hh in range(4):
                        ins = dve.tensor_scalar(dec[0:r, 2 * hh + b, 0:r], wide[b][0:r, hh * 128:hh * 128 + r], one(gc, j, 2 * hh + b, r),
                                                0.0, ALU.subtract, ALU.min)
                    ins.then_inc(d_done[b], 1)
                    if j >= 2:
                        dve.wait_ge(egs_done, 2 * (j - 1))
                    dve.tensor_copy(gl[:, j % 2, b, :], wide[b][:].rearrange("p (h c) -> p h c", h=4)[:, :, r - 1]).then_inc(gl_done, 1)
                    dve.wait_ge(gl_done, 2 * j + b + 1)
                    dst = glc[0:r, j % 2, :].rearrange("p (hh b) -> p b hh", b=2)[:, b, :]
                    seq(dve.tensor_tensor(dst, gl[0:r, j % 2, b, :], gate(gc, j, b, r), ALU.subtract))
                dve.sem_inc(glc_done, 1)
                attend()
                for b in range(2):
                    dve.wait_ge(kk_full[b], j + 1)
                    dve.wait_ge(dec_done[b], j + 1)
                    if j >= 1:
                        dve.wait_ge(bt_done[b], lev0(j))
                    for hh in range(4):
                        h = 2 * hh + b
                        ins = dve.scalar_tensor_tensor(ntm[0:r, h, 0:r], level_bank[b][0:r, hh * 128:hh * 128 + r], one(beta, j, h, r), dec[0:r, h, 0:r],
                                                       ALU.mult, ALU.mult)
                    ins.then_inc(nt_done[b], 1)
                if j >= 2:
                    dve.wait_ge(o_done, j - 1)
                for b in range(2):
                    dve.wait_ge(nt_done[b], j + 1)
                    m0 = cst[0:r, C_LEV:C_LEV + r].unsqueeze(1).to_broadcast([r, 4, r])
                    dst = batch(inv[:, j % 2], b, r)
                    seq(dve.tensor_tensor(dst, batch(ntm, b, r), m0, ALU.mult))
                    idb = ident[0:r, 0:r].unsqueeze(1).to_broadcast([r, 4, r])
                    dve.tensor_tensor(dst, idb, dst, ALU.subtract).then_inc(r1_done[b], 1)
                attend()
                attend()

            def decayed(j):
                for b in range(2):
                    dve.wait_ge(kq_full[b], j)
                    if j >= 2:
                        dve.wait_ge(o2_full, j - 1)
                    dve.tensor_tensor(batch(aqk[:], b, P), tmat(wide[b], P), batch(dec, b, P), ALU.mult).then_inc(aqk_raw[b], 1)

            def level(j, lv):
                r, n = rows(TILES[j]), lev0(j) + lv
                attend()
                for b in range(2):
                    dve.wait_ge(y_full[b], n)
                    if lv < nlev(j):
                        dve.tensor_tensor(batch(tri, b, r), batch(tri, b, r), tmat(level_bank[b], r), ALU.subtract).then_inc(t_new[b], 1)
                    else:
                        dst = batch(inv[:, j % 2], b, r)
                        dve.tensor_tensor(dst, dst, tmat(level_bank[b], r), ALU.subtract).then_inc(r_done[b], 1)
                attend()
                attend()

            def normalise(*tiles):
                part = slice(0, NT - 1) if tiles[0] < NT - 1 else slice(NT - 1, NT)
                if tiles[0] in (0, NT - 1):
                    dve.wait_ge(o_root, 1 if tiles[0] == 0 else 2)
                    seq(dve.reciprocal(stat[:, 2, HB * part.start:HB * part.stop], stat[:, 1, HB * part.start:HB * part.stop]))
                for t in tiles:
                    dve.wait_ge(zg_done, t + 1)
                    g = mix[:, t, 512:1024].rearrange("p (h d) -> p h d", d=DK)
                    z = zg[:, t, :].rearrange("p (h d) -> p h d", d=DK)
                    seq(dve.tensor_tensor(g, g, stat[:, 2, HB * t:HB * t + HB].unsqueeze(2).to_broadcast([P, HB, DK]), ALU.mult))
                    dve.tensor_tensor(g, g, z, ALU.mult).then_inc(normed, 1)

            v3 = lambda m, r: m[0:r, :].rearrange("p (h c) -> p h c", h=HB)

            def residual(j):
                r = rows(TILES[j])
                dve.wait_ge(vt_copied, j + 1)
                dve.wait_ge(ks_full, j)
                if j >= 2:
                    dve.wait_ge(v_full, j)
                for h in range(HB):
                    ins = dve.scalar_tensor_tensor(zz[0:r, h * DK:(h + 1) * DK], wide[h % 2][0:r, h // 2 * DK:h // 2 * DK + DK], one(neg, j, h, r),
                                                   vtok[0:r, h * DK:(h + 1) * DK], ALU.mult, ALU.add)
                ins.then_inc(z_done, 1)

            def new_values(j):
                r = rows(TILES[j])
                dve.wait_ge(v_full, j + 1)
                if j >= 1:
                    dve.wait_ge(v2_done, j)
                    if j >= 2:
                        dve.wait_ge(o2_full, j - 1)
                bb = beta.rearrange("p (t h) -> p t h", h=HB)[0:r, TILES[j], :].unsqueeze(2).to_broadcast([r, HB, DK])
                dve.tensor_tensor(v3(vn, r), v3(solo, r), bb, ALU.mult).then_inc(vn_done, 1)

            def update(j):
                r, t = rows(TILES[j]), TILES[j]
                if j < NJ - 1:
                    dve.wait_ge(s_full, j + 1)
                    if j == 0:
                        dve.tensor_copy(state[:].rearrange("p h c -> p (h c)"), solo[:, 0:256]).then_inc(s_done, 1)
                    else:
                        for hh in range(4):
                            ins = dve.scalar_tensor_tensor(state[:, hh, :], state[:, hh, :], egs[:, j % 2, hh:hh + 1], solo[:, hh * DK:(hh + 1) * DK],
                                                           ALU.mult, ALU.add)
                        ins.then_inc(s_done, 1)
                if j == 0:
                    dve.sem_inc(o_done, 1)
                    return
                dve.wait_ge(o2_full, j)
                for b in range(2):
                    ins = dve.tensor_copy(zz[0:r, :].rearrange("p (hh b c) -> p b hh c", b=2, c=DK)[:, b, :, :],
                                          wide[b][0:r, 0:256].rearrange("p (h c) -> p h c", c=DK))
                seq(ins)
                for h in range(HB):
                    ins = dve.scalar_tensor_tensor(mix[:, t, 512 + h * DK:512 + (h + 1) * DK],
                                                   wide[h % 2][0:r, 256 + h // 2 * DK:256 + h // 2 * DK + DK], one(eg, j, h, r),
                                                   zz[0:r, h * DK:(h + 1) * DK], ALU.mult, ALU.add)
                ins.then_inc(o_done, 1)
                dve.wait_ge(o_done, j + 1)
                seq(dve.tensor_tensor(zz[:], mix[:, t, 512:1024], mix[:, t, 512:1024], ALU.mult))
                dve.tensor_reduce(stat[:, 0, HB * t:HB * t + HB], zz[:].rearrange("p (h d) -> p h d", d=DK), AX.X, ALU.add).then_inc(o_sq, 1)
                dve.wait_ge(o_sq, j)

            for j in range(NJ + 1):
                if j >= 1:
                    attend()
                    attend()
                if j < NJ:
                    prepare(j)
                    level(j, 1)
                if j >= 2:
                    residual(j - 1)
                    attend()
                if j == NJ:
                    normalise(4)
                if j < NJ:
                    level(j, 2)
                if j >= 1:
                    new_values(j - 1)
                    attend()
                if j == NJ:
                    normalise(5, 6)
                if j < NJ:
                    level(j, 3)
                if j >= 1:
                    update(j - 1)
                    attend()
                if 1 <= j < NJ:
                    level(j, 4)
                    decayed(j)
                    attend()
                    level(j, 5)
                    if j == NJ - 1:
                        normalise(0, 1)
                    level(j, 6)
                    if j == NJ - 1:
                        normalise(2, 3)

            normalise(NT - 1)

        @block.tensor
        def _(pe):
            def piece(g):
                what, n, c, k0 = pieces[g]
                if g not in ring_pos:
                    return
                i, h = items[n]
                u = ring_pos[g]
                bank = ring[u % 3]
                if u >= 3:
                    pe.wait_ge(ring_read, u - 2)
                if what == "score":
                    k1 = min(nkeys(i), k0 + 512)
                    mm = pe.matmul(bank[:, 0:k1 - k0], s["aq"][64 * c:64 * c + 64, h, P * i:P * i + P],
                                   s["ak"][64 * c:64 * c + 64, h, k0:k1], start=True, stop=True)
                elif what == "turn":
                    if c == 0:
                        pe.wait_ge(mixed, n + 1)
                    for b in range(c, min(c + 4, i + 2)):
                        key, kn = (0, META) if b == 0 else (META + P * (b - 1), P)
                        mm = pe.transpose(bank[0:kn, (b - c) * 128:(b - c + 1) * 128], probs[:, n % 2, 0, key:key + kn], ident)
                else:
                    pe.wait_ge(ring_read, u)
                    for b in range(i + 2):
                        kn = META if b == 0 else P
                        mm = pe.matmul(bank[:, 0:VA], probsT[0:kn, b, :], s["av"][0:kn, NT if b == 0 else b - 1, h * VA:(h + 1) * VA],
                                       start=b == 0, stop=b == i + 1)
                mm.then_inc(ring_full, 1)

            attend = Share(piece, bounds)
            pe.wait_ge(g2, 2)
            pe.matmul(solo[:, 0:G8], upper, graw, start=True, stop=True).then_inc(gc_full, 1)

            def prepare(j):
                t = TILES[j]
                r, c = rows(t), col0(t)
                for b in range(2):
                    if j >= 2:
                        pe.wait_ge(aqk_raw[b], j - 1)
                    for hh in range(4):
                        g = graw[0:r, t * HB + 2 * hh + b:t * HB + 2 * hh + b + 1].to_broadcast([r, P])
                        mm = pe.matmul(wide[b][:, hh * 128:hh * 128 + r], g, upper[0:r, 0:r], start=True, stop=True)
                    mm.then_inc(gcb_full[b], 1)
                attend()
                for b in range(2):
                    if j >= 1:
                        pe.wait_ge(r_done[b], j)
                    for hh in range(4):
                        kt = gk[64 * b:64 * b + 64, hh, c:c + r]
                        mm = pe.matmul(level_bank[b][0:r, hh * 128:hh * 128 + r], kt, kt, start=True, stop=True)
                    mm.then_inc(kk_full[b], 1)
                attend()
                for b in range(2):
                    pe.wait_ge(r1_done[b], j + 1)
                    for hh in range(4):
                        mm = pe.transpose(level_bank[b][0:r, hh * 128:hh * 128 + r], inv[0:r, j % 2, 2 * hh + b, 0:r], ident[0:r, 0:r])
                    mm.then_inc(t1_turned[b], 1)
                attend()

            def tokens(j):
                t = TILES[j]
                r, c = rows(t), col0(t)
                if j == 0:
                    pe.wait_ge(gates, 1)
                else:
                    pe.wait_ge(s_done, j)
                for hh in range(4):
                    mm = pe.transpose(solo[0:r, hh * 128:(hh + 1) * 128], gk[:, hh, c:c + r], ident)
                mm.then_inc(kt_turned, 1)
                attend()
                pe.wait_ge(kt_copied, j + 1)
                for hh in range(4):
                    mm = pe.transpose(solo[0:r, hh * 128:(hh + 1) * 128], gv[:, hh, c:c + r], ident)
                mm.then_inc(vt_turned, 1)
                attend()

            def query_key(j):
                c = col0(TILES[j])
                if j >= 2:
                    pe.wait_ge(o_done, j)
                for b in range(2):
                    for hh in range(4):
                        mm = pe.matmul(wide[b][:, hh * 128:(hh + 1) * 128], gk[64 * b:64 * b + 64, hh, c:c + P],
                                       gq[64 * b:64 * b + 64, hh, c:c + P], start=True, stop=True)
                    mm.then_inc(kq_full[b], 1)

            def level(j, lv):
                r, n = rows(TILES[j]), lev0(j) + lv
                last = lv == nlev(j)
                for b in range(2):
                    pe.wait_ge(bt_done[b], n)
                    if lv == 1:
                        pe.wait_ge(t1_copied[b], j + 1)
                    else:
                        pe.wait_ge(r_copied[b], turns_before(j, lv - 1))
                    for hh in range(4):
                        h = 2 * hh + b
                        mm = pe.matmul(level_bank[b][0:r, hh * 128:hh * 128 + r], bt[0:r, h, 0:r], tri[0:r, h, 0:r], start=True, stop=True)
                    mm.then_inc(x_full[b], 1)
                attend()
                for b in range(2):
                    pe.wait_ge(x_copied[b], n)
                    for hh in range(4):
                        h = 2 * hh + b
                        m0, m1 = (xm[0:r, h, 0:r], inv[0:r, j % 2, h, 0:r]) if last else (inv[0:r, j % 2, h, 0:r], xm[0:r, h, 0:r])
                        mm = pe.matmul(level_bank[b][0:r, hh * 128:hh * 128 + r], m0, m1, start=True, stop=True)
                    mm.then_inc(y_full[b], 1)
                attend()
                if not last:
                    for b in range(2):
                        pe.wait_ge(t_new[b], turns_before(j, lv))
                        for hh in range(4):
                            mm = pe.transpose(level_bank[b][0:r, hh * 128:hh * 128 + r], tri[0:r, 2 * hh + b, 0:r], ident[0:r, 0:r])
                        mm.then_inc(r_turned[b], 1)
                attend()

            def from_state(j):
                t = TILES[j]
                r, c = rows(t), col0(t)
                pe.wait_ge(s_done, j)
                if j + 1 < NJ:
                    pe.wait_ge(glc_done, j + 2)
                for src, o in ((gk, 0), (gq, 256)):
                    for hh in range(4):
                        for b in range(2):
                            mm = pe.matmul(wide[b][0:r, o + hh * DK:o + (hh + 1) * DK], src[64 * b:64 * b + 64, hh, c:c + r],
                                           state[64 * b:64 * b + 64, hh, :], start=True, stop=True)
                mm.then_inc(ks_full, 1)

            def solve(j):
                r = rows(TILES[j])
                if j >= 1:
                    pe.wait_ge(z_done, j)
                for b in range(2):
                    pe.wait_ge(r_done[b], j + 1)
                pe.wait_ge(vt_copied, j + 1)
                for h in range(HB):
                    z = vtok[0:r, h * DK:(h + 1) * DK] if j == 0 else zz[0:r, h * DK:(h + 1) * DK]
                    mm = pe.matmul(solo[0:r, h * DK:(h + 1) * DK], inv[0:r, j % 2, h, 0:r], z, start=True, stop=True)
                mm.then_inc(v_full, 1)

            def carry(j):
                r = rows(TILES[j])
                pe.wait_ge(vn_done, j + 1)
                if j >= 1:
                    for b in range(2):
                        pe.wait_ge(aqk_done[b], j)
                    for h in range(HB):
                        mm = pe.matmul(wide[h % 2][0:r, h // 2 * DK:h // 2 * DK + DK], aqk[0:r, h, 0:r], vn[0:r, h * DK:(h + 1) * DK],
                                       start=True, stop=True)
                    mm.then_inc(o2_full, 1)
                if j < NJ - 1:
                    pe.wait_ge(v2_done, j + 1)
                    for hh in range(4):
                        for b in range(2):
                            h = 2 * hh + b
                            mm = pe.matmul(solo[64 * b:64 * b + 64, hh * DK:(hh + 1) * DK], ktok[0:r, h * DK:(h + 1) * DK],
                                           v2[0:r, h * DK:(h + 1) * DK], start=True, stop=True)
                    mm.then_inc(s_full, 1)

            for j in range(NJ + 1):
                if j >= 1:
                    tokens(j - 1)
                if j < NJ:
                    prepare(j)
                    level(j, 1)
                if j >= 2:
                    from_state(j - 1)
                    attend()
                if j < NJ:
                    level(j, 2)
                if j >= 1:
                    solve(j - 1)
                    attend()
                if j < NJ:
                    level(j, 3)
                if j >= 1:
                    carry(j - 1)
                    attend()
                if 1 <= j < NJ:
                    level(j, 4)
                    query_key(j)
                    attend()
                    level(j, 5)
                    level(j, 6)

        phase.close()
        clear(nc, sems)


def output_and_route(nc, a, s):
    with ExitStack() as ctx:
        sb = lambda n, sh, dt=F32: ctx.enter_context(nc.sbuf_tensor(n, sh, dt))
        ps = lambda n, sh, dt=F32: ctx.enter_context(nc.psum_tensor(n, sh, dt))
        sem = lambda n: s["semaphores"].enter_context(nc.semaphore(n))
        cst, mix, hres = s["cst"], s["mix"], s["hres"]
        ident = cst[:, C_ID:C_ID + 128]
        wout = s["wout"]
        mixT = sb("mixT", [P, 2, KD, P])
        uT = sb("u2T", [P, 2, KD, P])
        xr = sb("xr", [P, 2, D])
        u2 = sb("u2", [P, 2, D])
        scr = sb("scr", [P, D])
        gain = sb("ffn_gain", [P, D])
        wr = sb("wr", [P, KD, 36])
        rb = sb("rb", [P, 36])
        ss = sb("ss2", [P, NT, 3])
        lg = sb("lg", [P, NT, 36])
        big = lambda n: sb(n, [P, NT, NE])
        em, t1, t2, oh1, oh2, msum, mcum = (big(x) for x in ("em", "t1", "t2", "oh1", "oh2", "msum", "mcum"))
        sm = sb("sm", [P, 12, NT])
        g4, e4, goh = (sb(x, [P, NT, NG]) for x in ("g4", "e4", "goh"))
        tot = sb("tot", [P, NE])
        cmpn, ovc = sb("cmpn", [NE, 7]), sb("ovc", [NE, 1])
        base2, ovi = sb("base2", [P, NE]), sb("ovi", [P, NE])
        eob = sb("eob", [P, 16, NE])
        tabf = sb("tabf", [P, MAXBLK + 1])
        slf = sb("slf", [P, NT, 2])
        pmi, bmi = sb("pmi", [P, NT, 2], I32), sb("bmi", [P, NT, 2], I32)
        pmf, bmf = sb("pmf", [P, NT, 2]), sb("bmf", [P, NT, 2])
        ohp = s["region"][:, 0:2 * NT * P].rearrange("p (n s) -> p n s", s=P)
        ohb = s["region"][:, 2 * NT * P:2 * NT * (P + MAXBLK)].rearrange("p (n s) -> p n s", s=MAXBLK)
        gu, down = expert_slots(s)

        T, O, U = ([ps(f"{x}{i}", [P, 512]) for i in range(2)] for x in ("mT", "mO", "mU"))
        LGP = ps("LGP", [P, 512])
        w_first, x_in, gain_in, dve_seq = sem("w_first"), [sem(f"xr_in{i}") for i in range(2)], sem("gain_in"), sem("rdve_seq")
        m_turned, m_copied, o_full, h_done, sq_done, root, u_done, u_out = (
            sem(x) for x in ("m_turned", "m_copied", "o_full", "h_done", "sq2", "root2", "u_done", "u_out"))
        u_turned, uT_copied, lg_full, lg_done = (sem(x) for x in ("u_turned", "uT_copied", "lg_full", "lg_done"))
        ex_in, ex_done, p2_in, p2_done, m_done, rank_full, ovc_done, ov_full, oh_done, idx_full = (
            sem(x) for x in ("ex_in", "ex_done", "p2_in", "p2_done", "m_done", "rank_full", "ovc_done", "ov_full", "oh_done", "idx_full"))
        u_outs = [u_out, sem("u_out1")]

        block = ctx.enter_context(nc.Block())

        @block.sync
        def _(sp):
            for t in range(NT):
                if t >= 2:
                    sp.wait_ge(h_done, 2 * (t - 1))
                sp.dma_start(xr[:, t % 2, :], a["x"][0, t * P:(t + 1) * P, :]).then_inc(x_in[t % 2], 16)
                if t == 1:
                    sp.dma_start(gain[:], a["norm_ffn"].to_broadcast([P, D])).then_inc(gain_in, 16)
                    with nc.allow_non_contiguous_dma(reason="router columns, 16 and 128 bytes a row"):
                        sp.dma_start(wr[:, :, 0:4], a["w_group"].rearrange("o (k p) c -> (o p) k c", p=P)).then_inc(gain_in, 16)
                        sp.dma_start(wr[:, :, 4:36], a["w_router"].rearrange("o (k p) c -> (o p) k c", p=P)).then_inc(gain_in, 16)
                    sp.dma_start(rb[:, 0:4], a["b_group"].to_broadcast([P, 4])).then_inc(gain_in, 16)
                    sp.dma_start(rb[:, 4:36], a["b_router"].to_broadcast([P, 32])).then_inc(gain_in, 16)
                if t >= 1:
                    sp.wait_ge(u_done, t)
                    sp.dma_start(a["u2"][(t - 1) * P:t * P, :], u2[:, (t - 1) % 2, :]).then_inc(u_outs[(t - 1) % 2], 16)
                if t in (2, 3):
                    load_gate_up(sp, a, gu[t - 2], t - 2, w_first)
                elif t in (4, 5):
                    load_down(sp, a, down[t - 4], t - 4, w_first)
            sp.wait_ge(u_done, NT)
            sp.dma_start(a["u2"][(NT - 1) * P:NT * P, :], u2[:, (NT - 1) % 2, :]).then_inc(u_outs[(NT - 1) % 2], 16)
            for b in range(2):
                sp.wait_ge(u_outs[b], 16 * NT // 2)
            sp.wait_ge(w_first, 96)

        @block.scalar
        def _(act):
            def turned_mix(t):
                for half in range(2):
                    act.wait_ge(m_turned, 2 * t + half + 1)
                    if t >= 2:
                        act.wait_ge(o_full, 2 * (t - 1))
                    act.activation(mixT[:, t % 2, 4 * half:4 * half + 4, :], T[half][:], ACT.Copy).then_inc(m_copied, 1)

            def statistics(t):
                act.wait_ge(h_done, 2 * t + 2)
                if t >= 1:
                    act.wait_ge(sq_done, t)
                act.activation(scr[:], hres[:, t, :], ACT.Square, accum_out=ss[:, t, 0:1]).then_inc(sq_done, 1)
                act.wait_ge(sq_done, t + 1)
                act.activation(ss[:, t, 1:2], ss[:, t, 0:1], ACT.Sqrt, bias=cst[:, C_EPS:C_EPS + 1], scale=1.0 / D).then_inc(root, 1)

            def turned_u(t):
                for half in range(2):
                    act.wait_ge(u_turned, 2 * t + half + 1)
                    if t >= 2:
                        act.wait_ge(lg_full, t - 1)
                    act.activation(uT[:, t % 2, 4 * half:4 * half + 4, :], U[half][:], ACT.Copy).then_inc(uT_copied, 1)

            act.wait_ge(gain_in, 80)
            for t in range(NT + 1):
                if t < NT:
                    turned_mix(t)
                if t >= 1:
                    turned_u(t - 1)
                if t < NT:
                    statistics(t)
            act.wait_ge(ex_in, 1)
            act.activation(e4[:], e4[:], ACT.Exp).then_inc(ex_done, 1)
            act.wait_ge(p2_in, 1)
            act.activation(sm[:, 8, :], sm[:, 8, :], ACT.Exp).then_inc(p2_done, 1)

        @block.vector
        def _(dve):
            seq = Seq(dve, dve_seq)

            def logits(t):
                dve.wait_ge(lg_full, t + 1)
                dve.tensor_tensor(lg[:, t, :], LGP[:, 0:36], rb[:], ALU.add).then_inc(lg_done, 1)

            seq(dve.memset(s["idx"][:], -1))
            dve.wait_ge(gain_in, 80)
            for t in range(NT):
                dve.wait_ge(x_in[t % 2], 16 * (t // 2 + 1))
                for half in range(2):
                    dve.wait_ge(o_full, 2 * t + half + 1)
                    c = slice(512 * half, 512 * half + 512)
                    dve.tensor_tensor(hres[:, t, c], O[half][:], xr[:, t % 2, c], ALU.add).then_inc(h_done, 1)
                dve.wait_ge(root, t + 1)
                seq(dve.reciprocal(ss[:, t, 2:3], ss[:, t, 1:2]))
                if t >= 2:
                    dve.wait_ge(u_outs[t % 2], 16 * (t // 2))
                    dve.wait_ge(u_turned, 2 * (t - 1))
                dve.scalar_tensor_tensor(u2[:, t % 2, :], hres[:, t, :], ss[:, t, 2:3], gain[:], ALU.mult, ALU.mult).then_inc(u_done, 1)
                if t >= 1:
                    logits(t - 1)
            logits(NT - 1)
            dve.wait_ge(lg_done, NT)

            bc = lambda v, n: v.unsqueeze(2).to_broadcast([P, NT, n])
            row = lambda c, n: cst[:, c:c + n].unsqueeze(1).to_broadcast([P, NT, n])
            m = lambda i: sm[:, i, :]

            def first_max(values, n, top, onehot, work):
                seq(dve.tensor_reduce(top, values, AX.X, ALU.max))
                seq(dve.tensor_tensor(work, values, bc(top, n), ALU.is_equal))
                seq(dve.tensor_tensor(work, work, row(C_IG, n), ALU.mult))
                seq(dve.tensor_reduce(m(11), work, AX.X, ALU.min))
                seq(dve.tensor_tensor(onehot, row(C_IG, n), bc(m(11), n), ALU.is_equal))

            first_max(lg[:, :, 0:NG], NG, m(0), goh[:], g4[:])
            dve.tensor_tensor(e4[:], lg[:, :, 0:NG], bc(m(0), NG), ALU.subtract).then_inc(ex_in, 1)
            seq(dve.tensor_scalar(g4[:], goh[:], BIG, -BIG, ALU.mult, ALU.add))
            groups = lambda v: v.rearrange("p t (g e) -> p (t g) e", g=NG)
            wide = lambda v: v[:].rearrange("p t g -> p (t g)").unsqueeze(2).to_broadcast([P, NT * NG, EPG])
            seq(dve.tensor_copy(em[:], lg[:, :, NG:NG + NE]))
            seq(dve.tensor_tensor(groups(em[:]), groups(em[:]), wide(goh), ALU.mult))
            seq(dve.tensor_tensor(groups(em[:]), groups(em[:]), wide(g4), ALU.add))
            first_max(em[:], NE, m(1), oh1[:], t1[:])
            seq(dve.scalar_tensor_tensor(em[:], oh1[:], -2.0 * BIG, em[:], ALU.mult, ALU.add))
            first_max(em[:], NE, m(2), oh2[:], t1[:])
            dve.tensor_tensor(m(8), m(2), m(1), ALU.subtract).then_inc(p2_in, 1)
            dve.wait_ge(ex_done, 1)
            seq(dve.tensor_reduce(m(3), e4[:], AX.X, ALU.add))
            seq(dve.reciprocal(m(4), m(3)))
            dve.wait_ge(p2_done, 1)
            seq(dve.tensor_scalar(m(5), m(8), 1.0, None, ALU.add))
            seq(dve.reciprocal(m(6), m(5)))
            seq(dve.tensor_tensor(s["wts"][:, 0, :], m(4), m(6), ALU.mult))
            seq(dve.tensor_tensor(s["wts"][:, 1, :], s["wts"][:, 0, :], m(8), ALU.mult))
            seq(dve.tensor_tensor(msum[:], oh1[:], oh2[:], ALU.add))
            seq(dve.memset(mcum[:, 0, :], 0.0))
            for t in range(1, NT):
                seq(dve.tensor_tensor(mcum[:, t, :], mcum[:, t - 1, :], msum[:, t - 1, :], ALU.add))
            dve.tensor_tensor(tot[:], mcum[:, NT - 1, :], msum[:, NT - 1, :], ALU.add).then_inc(m_done, 1)
            dve.wait_ge(rank_full, 1)
            seq(dve.tensor_tensor(cmpn[:], T[1][0:NE, 0:1].to_broadcast([NE, 7]), cst[0:NE, C_E128 + 1:C_E128 + 8], ALU.is_gt))
            dve.tensor_reduce(ovc[:], cmpn[:], AX.X, ALU.add).then_inc(ovc_done, 1)
            rank = t1[:]
            seq(dve.tensor_copy(rank, T[0][:, 0:NT * NE].rearrange("p (t e) -> p t e", t=NT)))
            dve.wait_ge(ov_full, 1)
            seq(dve.tensor_scalar(base2[:], O[0][:, 0:NE], 128.0, 31.0 * 128.0, ALU.mult, ALU.add))
            seq(dve.tensor_tensor(base2[:], base2[:], cst[:, C_E128:C_E128 + NE], ALU.subtract))
            seq(dve.tensor_copy(ovi[:], O[0][:, NE:2 * NE]))
            seq(dve.tensor_scalar(t2[:], rank, 128.0, None, ALU.is_ge))
            seq(dve.tensor_tensor(t2[:], t2[:], base2[:].unsqueeze(1).to_broadcast([P, NT, NE]), ALU.mult))
            seq(dve.tensor_tensor(t2[:], t2[:], rank, ALU.add))
            seq(dve.tensor_tensor(t2[:], t2[:], row(C_E128, NE), ALU.add))
            for c, oh in enumerate((oh1, oh2)):
                seq(dve.tensor_tensor(em[:], t2[:], oh[:], ALU.mult))
                seq(dve.tensor_reduce(slf[:, :, c], em[:], AX.X, ALU.add))
            seq(dve.tensor_copy(s["slot"][:], slf[:]))
            seq(dve.tensor_scalar(pmi[:], s["slot"][:], 127, None, ALU.bitwise_and))
            seq(dve.tensor_scalar(bmi[:], s["slot"][:], 7, None, ALU.arith_shift_right))
            seq(dve.tensor_copy(pmf[:], pmi[:]))
            seq(dve.tensor_copy(bmf[:], bmi[:]))
            grid = lambda v, n: v.rearrange("p t c -> p (t c)").unsqueeze(2).to_broadcast([P, 2 * NT, n])
            step = lambda c, n: cst[:, c:c + n].unsqueeze(1).to_broadcast([P, 2 * NT, n])
            seq(dve.tensor_tensor(ohb, step(C_IOTA, MAXBLK), grid(bmf[:], MAXBLK), ALU.is_equal))
            seq(dve.tensor_tensor(ohb, ohb, cst[:, C_TOK:C_TOK + 2 * NT].unsqueeze(2).to_broadcast([P, 2 * NT, MAXBLK]), ALU.mult))
            seq(dve.tensor_tensor(ohp, step(C_IOTA, P), grid(pmf[:], P), ALU.is_equal))
            dve.sem_inc(oh_done, 1)
            io = cst[:, C_IOTA:C_IOTA + 16].unsqueeze(2).to_broadcast([P, 16, NE])
            seq(dve.tensor_tensor(eob[:], ovi[:].unsqueeze(1).to_broadcast([P, 16, NE]), io, ALU.is_le))
            seq(dve.tensor_copy(tabf[:, 0:32], cst[:, C_IOTA:C_IOTA + 32]))
            seq(dve.tensor_reduce(tabf[:, 32:48], eob[:], AX.X, ALU.add))
            seq(dve.tensor_scalar(tabf[:, 32:48], tabf[:, 32:48], 31.0, None, ALU.min))
            seq(dve.tensor_scalar(tabf[:, 48:49], ovi[:, NE - 1:NE], 33.0, None, ALU.add))
            seq(dve.tensor_copy(s["table"][:], tabf[:]))
            seq(dve.tensor_scalar(s["table"][:, 48:49], s["table"][:, 48:49], 1, None, ALU.arith_shift_right))
            dve.wait_ge(idx_full, 1)
            seq(dve.tensor_scalar(tabf[:, 0:MAXBLK], U[0][:, 0:MAXBLK], -1.0, None, ALU.add))
            seq(dve.tensor_copy(s["idx"][:, 0, 0:MAXBLK], tabf[:, 0:MAXBLK]))
            seq(dve.tensor_scalar(s["idx"][:, 1, :], s["idx"][:, 0, :], 1, None, ALU.arith_shift_right))

        @block.tensor
        def _(pe):
            def turn_mix(t):
                for half in range(2):
                    if t >= 1:
                        pe.wait_ge(m_copied, 2 * t - 1 + half)
                    for kk in range(4):
                        kx = 4 * half + kk
                        mm = pe.transpose(T[half][:, kk * P:(kk + 1) * P], mix[:, t, kx * P:(kx + 1) * P], ident)
                    mm.then_inc(m_turned, 1)

            def out_proj(t):
                pe.wait_ge(m_copied, 2 * t + 2)
                for half in range(2):
                    if t >= 1:
                        pe.wait_ge(h_done, 2 * t - 1 + half)
                    for kx in range(KD):
                        mm = pe.matmul(O[half][:], mixT[:, t % 2, kx, :], wout[:, kx, 512 * half:512 * half + 512], start=kx == 0, stop=kx == KD - 1)
                    mm.then_inc(o_full, 1)

            def turn_u(t):
                pe.wait_ge(u_done, t + 1)
                for half in range(2):
                    if t >= 1:
                        pe.wait_ge(uT_copied, 2 * t - 1 + half)
                    for kk in range(4):
                        kx = 4 * half + kk
                        mm = pe.transpose(U[half][:, kk * P:(kk + 1) * P], u2[:, t % 2, kx * P:(kx + 1) * P], ident)
                    mm.then_inc(u_turned, 1)

            def router(t):
                pe.wait_ge(uT_copied, 2 * t + 2)
                if t >= 1:
                    pe.wait_ge(lg_done, t)
                for kx in range(KD):
                    mm = pe.matmul(LGP[:, 0:36], uT[:, t % 2, kx, :], wr[:, kx, :], start=kx == 0, stop=kx == KD - 1)
                mm.then_inc(lg_full, 1)

            turn_mix(0)
            pe.wait_ge(gain_in, 80)
            for t in range(NT + 1):
                if t + 1 < NT:
                    turn_mix(t + 1)
                if t < NT:
                    out_proj(t)
                if t >= 1:
                    turn_u(t - 1)
                    router(t - 1)
            pe.wait_ge(m_done, 1)
            pe.wait_ge(m_copied, 2 * NT)
            ones = cst[:, C_ONE:C_ONE + P]
            pe.matmul(T[0][:, 0:NT * NE], cst[:, C_SUP:C_SUP + P], msum[:].rearrange("p t e -> p (t e)"), start=True, stop=False)
            pe.matmul(T[0][:, 0:NT * NE], ones, mcum[:].rearrange("p t e -> p (t e)"), start=False, stop=True)
            pe.matmul(T[1][0:NE, 0:1], tot[:], cst[:, C_ONE:C_ONE + 1], start=True, stop=True).then_inc(rank_full, 1)
            pe.wait_ge(ovc_done, 1)
            lhs = ovc[:].to_broadcast([NE, P])
            pe.matmul(O[0][:, 0:NE], lhs, cst[0:NE, C_SUP:C_SUP + NE], start=True, stop=True)
            pe.matmul(O[0][:, NE:2 * NE], lhs, cst[0:NE, C_UP:C_UP + NE], start=True, stop=True).then_inc(ov_full, 1)
            pe.wait_ge(oh_done, 1)
            for n in range(2 * NT):
                mm = pe.matmul(U[0][:, 0:MAXBLK], ohp[:, n, :], ohb[:, n, :], start=n == 0, stop=n == 2 * NT - 1)
            mm.then_inc(idx_full, 1)



def expert_slots(s):
    flat, n = s["gqkv"][:].rearrange("p m l -> p (m l)"), KD * 2 * FE + 2 * D
    store = [flat[:, n * u:n * u + n] for u in range(2)]
    return ([w[:, 0:KD * 2 * FE].rearrange("p (k g f) -> p k g f", k=KD, g=2) for w in store],
            [w[:, KD * 2 * FE:].rearrange("p (k c) -> p k c", k=2) for w in store])


def load_gate_up(sp, a, dst, e, signal):
    for g, w in enumerate(("w_gate", "w_up")):
        v = a[w].rearrange("o e (p k) f -> (o e) p k f", k=KD)
        sp.dma_start(dst[:, :, g, :], v[bass.ds(e, 1)].rearrange("o p k f -> (o p) k f")).then_inc(signal, 16)


def load_down(sp, a, dst, e, signal):
    v = a["w_down"].rearrange("o e (p k) c -> (o e) p k c", k=2)
    sp.dma_start(dst, v[bass.ds(e, 1)].rearrange("o p k c -> (o p) k c")).then_inc(signal, 16)


def experts(nc, a, s):
    with ExitStack() as ctx:
        sb = lambda n, sh, dt=F32: ctx.enter_context(nc.sbuf_tensor(n, sh, dt))
        ps = lambda n, sh, dt=F32: ctx.enter_context(nc.psum_tensor(n, sh, dt))
        sem = lambda n: s["semaphores"].enter_context(nc.semaphore(n))
        sem2 = lambda n: [sem(f"{n}{b}") for b in range(2)]
        ident = s["cst"][:, C_ID:C_ID + 128]
        gu, down = expert_slots(s)
        xg, xT, yb = sb("xg", [P, 2, D]), sb("xT", [P, 2, KD, P]), sb("yb", [P, 2, D])
        sg, hb, hT = sb("sg", [P, 2, FE]), sb("hb", [P, 2, FE]), sb("hT", [P, 2, 2, P])
        cur = sb("cur", [P, 2, 2], I32)
        XY = [[ps(f"XY{u}{half}", [P, 512]) for half in range(2)] for u in range(2)]
        GU = [ps(f"GU{u}", [P, 512]) for u in range(2)]
        HT = [ps(f"HT{u}", [P, 512]) for u in range(2)]
        w_in, d_in, cur_done, x_in, x_turned, xT_act, xT_dve, gu_full, silu_done, h_done, h_turned, hT_done, y_full, y_act, y_dve, y_out = (
            sem2(x) for x in ("ew_in", "ed_in", "cur_done", "ex_in_", "ex_turned", "xT_act", "xT_dve", "gu_full", "esilu", "eh_done",
                              "eh_turned", "ehT_done", "ey_full", "ey_act", "ey_dve", "ey_out"))
        wait = lambda eng, x, v: None if isinstance(v, int) and v == 0 else eng.wait_ge(x, v)
        go_pool, x_clear, cur2_done = sem("go_pool"), sem("x_clear"), sem2("cur2_done")
        pairs = lambda eng: eng.value_load(s["table"][0:1, 48:49], min_val=16, max_val=24)

        block = ctx.enter_context(nc.Block())

        @block.sync
        def _(sp):
            with sp.Fori(1, pairs(sp)) as i:
                experts_of = [sp.value_load(s["table"][0:1, bass.ds(2 * i + u, 1)], min_val=0, max_val=NE - 1) for u in range(2)]
                for u, e in enumerate(experts_of):
                    sp.wait_ge(gu_full[u], i)
                    load_gate_up(sp, a, gu[u], e, w_in[u])
                for u, e in enumerate(experts_of):
                    sp.wait_ge(y_full[u], 2 * i)
                    load_down(sp, a, down[u], e, d_in[u])

        @block.gpsimd
        def _(pool):
            rows_of = lambda u, c: bass.IndirectOffsetOnAxis(ap=cur[:, u, c:c + 1].bitcast(U32), axis=0)

            def gather(i, j):
                for u in range(2):
                    wait(pool, x_in[u], 16 * i)
                    pool.tensor_copy(cur[:, u, 0:1], s["idx"][:, 1, bass.ds(2 * j + u, 1)]).then_inc(cur_done[u], 1)
                    pool.wait_ge(cur_done[u], j + 1)
                    wait(pool, x_turned[u], 2 * i)
                    pool.sem_inc(go_pool, 1)
                    pool.indirect_dma_start(out=xg[:, u, :], out_offset=None, in_=a["u2"], in_offset=rows_of(u, 0),
                                            bounds_check=SEQ - 1, oob_is_err=False).then_inc(x_in[u], 16)

            def scatter(i):
                for u in range(2):
                    wait(pool, y_out[u], 16 * i)
                    pool.tensor_copy(cur[:, u, 1:2], s["idx"][:, 0, bass.ds(2 * i + u, 1)]).then_inc(cur2_done[u], 1)
                    pool.wait_ge(cur2_done[u], i + 1)
                    pool.wait_ge(y_act[u], i + 1)
                    pool.wait_ge(y_dve[u], i + 1)
                    pool.sem_inc(go_pool, 1)
                    pool.indirect_dma_start(out=a["ys"], out_offset=rows_of(u, 1), in_=yb[:, u, :], in_offset=None,
                                            bounds_check=2 * SEQ - 1, oob_is_err=False).then_inc(y_out[u], 16)

            pool.wait_ge(x_clear, 1)
            gather(0, 0)
            gather(1, 1)
            scatter(0)
            n = pairs(pool)
            with pool.Fori(1, n) as i:
                gather(i + 1, i + 1)
                scatter(i)
            for u in range(2):
                pool.wait_ge(y_out[u], 16 * n)
                pool.wait_ge(x_in[u], 16 * n + 16)
            pool.sem_inc(go_pool, 1)

        @block.scalar
        def _(act):
            def turn(i):
                for u in range(2):
                    act.wait_ge(x_turned[u], 2 * i + 1)
                    act.activation(xT[:, u, 0:4, :], XY[u][0][:], ACT.Copy).then_inc(xT_act[u], 1)
                for u in range(2):
                    act.wait_ge(gu_full[u], i + 1)
                    act.activation(sg[:, u, :], GU[u][:, 0:FE], ACT.Silu).then_inc(silu_done[u], 1)
                for u in range(2):
                    act.wait_ge(h_turned[u], i + 1)
                    act.activation(hT[:, u], HT[u][:, 0:2 * P], ACT.Copy).then_inc(hT_done[u], 1)
                for u in range(2):
                    act.wait_ge(y_full[u], 2 * i + 1)
                    wait(act, y_out[u], 16 * i)
                    act.activation(yb[:, u, 0:512], XY[u][0][:], ACT.Copy).then_inc(y_act[u], 1)

            turn(0)
            with act.Fori(1, pairs(act)) as i:
                turn(i)

        @block.vector
        def _(dve):
            dve.memset(xg[:], 0.0).then_inc(x_clear, 1)
            def turn(i):
                for u in range(2):
                    dve.wait_ge(x_turned[u], 2 * i + 2)
                    dve.tensor_copy(xT[:, u, 4:8, :], XY[u][1][:].rearrange("p (k t) -> p k t", k=4)).then_inc(xT_dve[u], 1)
                for u in range(2):
                    dve.wait_ge(silu_done[u], i + 1)
                    dve.tensor_tensor(hb[:, u, :], GU[u][:, FE:2 * FE], sg[:, u, :], ALU.mult).then_inc(h_done[u], 1)
                for u in range(2):
                    dve.wait_ge(y_full[u], 2 * i + 2)
                    wait(dve, y_out[u], 16 * i)
                    dve.tensor_copy(yb[:, u, 512:1024], XY[u][1][:]).then_inc(y_dve[u], 1)

            turn(0)
            with dve.Fori(1, pairs(dve)) as i:
                turn(i)

        @block.tensor
        def _(pe):
            def turn(i):
                for u in range(2):
                    pe.wait_ge(x_in[u], 16 * i + 16)
                    for half in range(2):
                        wait(pe, (y_act if half == 0 else y_dve)[u], i)
                        for kk in range(4):
                            kx = 4 * half + kk
                            mm = pe.transpose(XY[u][half][:, kk * P:(kk + 1) * P], xg[:, u, kx:D:KD], ident)
                        mm.then_inc(x_turned[u], 1)
                for u in range(2):
                    wait(pe, w_in[u], 32 * i)
                    pe.wait_ge(xT_act[u], i + 1)
                    pe.wait_ge(xT_dve[u], i + 1)
                    wait(pe, h_done[u], i)
                    for kx in range(KD):
                        mm = pe.matmul(GU[u][:], xT[:, u, kx, :], gu[u][:, kx, :, :], start=kx == 0, stop=kx == KD - 1)
                    mm.then_inc(gu_full[u], 1)
                for u in range(2):
                    pe.wait_ge(h_done[u], i + 1)
                    wait(pe, hT_done[u], i)
                    for kx in range(2):
                        mm = pe.transpose(HT[u][:, kx * P:(kx + 1) * P], hb[:, u, kx:FE:2], ident)
                    mm.then_inc(h_turned[u], 1)
                for u in range(2):
                    pe.wait_ge(hT_done[u], i + 1)
                    wait(pe, d_in[u], 16 * i)
                    for half in range(2):
                        for kx in range(2):
                            mm = pe.matmul(XY[u][half][:], hT[:, u, kx, :], down[u][:, kx, 512 * half:512 * half + 512], start=kx == 0, stop=kx == 1)
                        mm.then_inc(y_full[u], 1)

            turn(0)
            with pe.Fori(1, pairs(pe)) as i:
                turn(i)



def combine(nc, a, s):
    with ExitStack() as ctx:
        sb = lambda n, sh, dt=F32: ctx.enter_context(nc.sbuf_tensor(n, sh, dt))
        sem = lambda n: ctx.enter_context(nc.semaphore(n))
        RB = 3
        cst, hres = s["cst"], s["hres"]
        y = sb("yc", [P, RB, 2, D])
        ob = sb("ob", [P, 2, D])
        scr, gain, ss = sb("cscr", [P, D]), sb("fgain", [P, D]), sb("ss3", [P, NT, 3])
        gain_in, seq_s, sq, root = sem("fgain_in"), sem("cseq"), sem("csq"), sem("croot")
        y_in, added, o_done, o_out = [sem(f"y_in{b}") for b in range(RB)], sem("cadded"), sem("co_done"), [sem(f"co_out{b}") for b in range(2)]

        block = ctx.enter_context(nc.Block())

        @block.sync
        def _(sp):
            sp.dma_start(gain[:], a["norm_final"].rearrange("(o d) -> o d", o=1).to_broadcast([P, D])).then_inc(gain_in, 16)
            def put(t):
                sp.wait_ge(o_done, t + 1)
                sp.dma_start(a["out"][0, t * P:(t + 1) * P, :], ob[:, t % 2, :]).then_inc(o_out[t % 2], 16)

            for t in range(NT):
                if t >= RB:
                    sp.wait_ge(added, t - RB + 1)
                sp.dma_start(y[:, t % RB, :, :], a["ys"].rearrange("(t p c) d -> t p c d", c=2, p=P)[t]).then_inc(y_in[t % RB], 16)
                if t < RB - 1:
                    continue
                put(t - RB + 1)
            for t in range(NT - RB + 1, NT):
                put(t)
            for b in range(2):
                sp.wait_ge(o_out[b], 16 * NT // 2)

        @block.scalar
        def _(act):
            for t in range(NT):
                act.wait_ge(added, t + 1)
                if t >= 1:
                    act.wait_ge(sq, t)
                act.activation(scr[:], hres[:, t, :], ACT.Square, accum_out=ss[:, t, 0:1]).then_inc(sq, 1)
                act.wait_ge(sq, t + 1)
                act.activation(ss[:, t, 1:2], ss[:, t, 0:1], ACT.Sqrt, bias=cst[:, C_EPS:C_EPS + 1], scale=1.0 / D).then_inc(root, 1)

        @block.vector
        def _(dve):
            seq = Seq(dve, seq_s)

            def finish(t):
                dve.wait_ge(root, t + 1)
                seq(dve.reciprocal(ss[:, t, 2:3], ss[:, t, 1:2]))
                if t >= 2:
                    dve.wait_ge(o_out[t % 2], 16 * (t // 2))
                dve.scalar_tensor_tensor(ob[:, t % 2, :], hres[:, t, :], ss[:, t, 2:3], gain[:], ALU.mult, ALU.mult).then_inc(o_done, 1)

            dve.wait_ge(gain_in, 16)
            for t in range(NT):
                dve.wait_ge(y_in[t % RB], 16 * (t // RB + 1))
                h = hres[:, t, :]
                seq(dve.scalar_tensor_tensor(h, y[:, t % RB, 0, :], s["wts"][:, 0, t:t + 1], h, ALU.mult, ALU.add))
                dve.scalar_tensor_tensor(h, y[:, t % RB, 1, :], s["wts"][:, 1, t:t + 1], h, ALU.mult, ALU.add).then_inc(added, 1)
                if t >= 1:
                    finish(t - 1)
            finish(NT - 1)


def build(nc, a):
    with ExitStack() as ctx:
        sb = lambda n, sh, dt=F32: ctx.enter_context(nc.sbuf_tensor(n, sh, dt))
        a["z"] = nc.dram_tensor("z_dram", (NT, P, 512), F32, kind="Internal").ap()
        a["u2"] = nc.dram_tensor("u2_dram", (SEQ, D), F32, kind="Internal").ap()
        a["ys"] = nc.dram_tensor("ys_dram", (SEQ * 2, D), F32, kind="Internal").ap()
        s = {
            "cst": sb("cst", [P, C_N]), "cols": sb("cols", [P, 64]), "gqkv": sb("gqkv", [P, 12, L]),
            "ab": sb("ab", [P, NT + 1, 16]),
            "wts": sb("wts", [P, 2, NT]), "slot": sb("slot", [P, NT, 2], I32), "idx": sb("idx", [P, 2, MAXBLK + 2], I32),
            "table": sb("table", [P, MAXBLK + 1], I32),
        }
        with ExitStack() as shared:
            s["split_in_region"] = [split_place(nc, shared, n) for n in ("first", "second")]
        s["region"] = sb("region", [P, HA * SEQ + HA * L + (NT + 1) * HA * VA])
        s["gq"], s["gk"], s["gv"] = (s["gqkv"][:, 4 * i:4 * i + 4, :] for i in range(3))
        reg, e1, e2 = s["region"], HA * SEQ, HA * (SEQ + L)
        s["aq"] = reg[:, 0:e1].rearrange("p (h t) -> p h t", h=HA)
        s["ak"] = reg[:, e1:e2].rearrange("p (h t) -> p h t", h=HA)
        s["av"] = reg[:, e2:].rearrange("p (t c) -> p t c", t=NT + 1)
        project(nc, a, s)
        s["mix"] = sb("mix", [P, NT, D])
        s["wout"] = reg[:, NT * 512:NT * 512 + KD * D].rearrange("p (k c) -> p k c", k=KD)
        mixers(nc, a, s)
        s["hres"] = s["mix"][:]
        s["semaphores"] = ctx
        output_and_route(nc, a, s)
        experts(nc, a, s)
        combine(nc, a, s)


_INS = ["x", "meta", "norm_mix", "w_in", "lambda_q1", "lambda_k1", "lambda_q2", "lambda_k2", "diff_norm", "conv_w",
        "a_log", "dt_bias", "gdn_norm", "w_out", "norm_ffn", "w_group", "b_group", "w_router", "b_router",
        "w_gate", "w_up", "w_down", "norm_final"]


def kernel(**inputs):
    import concourse.bacc as _bacc
    from concourse.bass_utils import run_bass_kernel_spmd as _run

    nc = _bacc.Bacc("TRN2", target_bir_lowering=False, num_devices=1)
    arrays = {"in_consts": constants()}
    arrays.update({f"in_{n}": np.ascontiguousarray(inputs[n]) for n in _INS})
    a = {n[3:]: nc.dram_tensor(n, v.shape, F32, kind="ExternalInput").ap() for n, v in arrays.items()}
    a["out"] = nc.dram_tensor("out_0", (1, SEQ, D), F32, kind="ExternalOutput").ap()
    build(nc, a)
    r = _run(nc, [arrays], core_ids=[0])
    return r.results[0]["out_0"]
```
